# Optimizing a Trainium2 kernel written in Bass

```python
import jax, jax.numpy as jnp
from jax import lax
import numpy as np

D_MODEL = 1024
BATCH = 1
SEQ = 512
DEPTH = 1
DEC_BATCH = 8
DEC_SEQ = 8
PAST_LEN = 4096
PAGE_SIZE = 128

N_BRANCH = 4
BR_WIDTH = D_MODEL // 2
SGU_GROUPS = 4
SGU_CHUNK = 128
SGU_GDIM = BR_WIDTH // SGU_GROUPS
LRU_HEADS = 4
LRU_HDIM = BR_WIDTH // LRU_HEADS
CONV_W = 4
LRU_C = 8.0
POOL_WINDOWS = (2, 4, 8, 16)
POOL_GROUPS = len(POOL_WINDOWS)
POOL_GDIM = BR_WIDTH // POOL_GROUPS
POOL_BUF = max(POOL_WINDOWS) - 1
HG_HEADS = 4
HG_DK = BR_WIDTH // HG_HEADS
HG_DV = BR_WIDTH // HG_HEADS
HG_CHUNK = 64
N_MEM = 256
X_HEADS = 4
X_HDIM = D_MODEL // X_HEADS
N_EXPERTS = 16
N_GROUPS = 4
EXPERTS_PER_GROUP = N_EXPERTS // N_GROUPS
TOP_K = 2
D_EXPERT = D_MODEL // 2
DN_ALPHA = (2 * DEPTH) ** 0.25
DN_BETA = (8 * DEPTH) ** -0.25
LN_EPS = 1e-5
RMS_EPS = 1e-6
SPLIT_POINTS = tuple(BR_WIDTH * k for k in range(1, 10))
IN_WIDTH = 9 * BR_WIDTH + N_BRANCH * D_MODEL

kernel_name = 'hybrid_gated_sgu_rglru_pool_hgrn2_moe_step'

def layer_norm(x, g, b):
    xf = x.astype(jnp.float32)
    mu = jnp.mean(xf, axis=-1, keepdims=True)
    var = jnp.mean(jnp.square(xf - mu), axis=-1, keepdims=True)
    return ((xf - mu) * lax.rsqrt(var + LN_EPS) * g + b).astype(x.dtype)

def chunk_sgu(u, v, ln_g, ln_b, w_s, b_s):
    B, T, _ = u.shape
    v = layer_norm(v, ln_g, ln_b)
    L = SGU_CHUNK if T % SGU_CHUNK == 0 else T
    n = T // L
    mask = jnp.tril(jnp.ones((L, L), dtype=bool))
    w = jnp.where(mask, w_s[:, :L, :L], 0.0)
    vg = v.reshape(B, n, L, SGU_GROUPS, SGU_GDIM)
    mixed = jnp.einsum('gts,bnsgc->bntgc', w, vg) + b_s[:, :L].T[None, None, :, :, None]
    return u * mixed.reshape(B, T, BR_WIDTH).astype(u.dtype), v

def causal_conv(x, buf, w, b):
    T = x.shape[1]
    xp = jnp.concatenate([buf.astype(x.dtype), x], axis=1)
    y = b + xp[:, 0:T] * w[0]
    for j in range(1, CONV_W):
        y = y + xp[:, j:j + T] * w[j]
    return y, xp[:, -(CONV_W - 1):]

def rg_lru(x, h0, w_r, b_r, w_i, b_i, lam):
    B, T, _ = x.shape
    xf = x.astype(jnp.float32)
    xh = xf.reshape(B, T, LRU_HEADS, LRU_HDIM)
    r = jax.nn.sigmoid(jnp.einsum('bthc,hcd->bthd', xh, w_r).reshape(B, T, BR_WIDTH) + b_r)
    i = jax.nn.sigmoid(jnp.einsum('bthc,hcd->bthd', xh, w_i).reshape(B, T, BR_WIDTH) + b_i)
    log_a = -LRU_C * r * jax.nn.softplus(-lam.astype(jnp.float32))
    a = jnp.exp(log_a)
    bx = jnp.sqrt(-jnp.expm1(2.0 * log_a)) * (i * xf)
    bx = bx.at[:, 0].add(a[:, 0] * h0.astype(jnp.float32))

    def combine(lhs, rhs):
        return (lhs[0] * rhs[0], rhs[0] * lhs[1] + rhs[1])

    _, h = lax.associative_scan(combine, (a, bx), axis=1)
    return h.astype(x.dtype), h[:, -1].astype(h0.dtype)

def pool_mixer(c, buf, pos0, w_p, b_p, scale):
    B, T, _ = c.shape
    cat = jnp.concatenate([buf.astype(c.dtype), c], axis=1)
    catf = cat.astype(jnp.float32)
    cs = jnp.concatenate([jnp.zeros_like(catf[:, :1]), jnp.cumsum(catf, axis=1)], axis=1)
    end = cs[:, POOL_BUF + 1:]
    pooled = []
    for g, w in enumerate(POOL_WINDOWS):
        sl = slice(g * POOL_GDIM, (g + 1) * POOL_GDIM)
        s = end[..., sl] - cs[:, POOL_BUF + 1 - w:POOL_BUF + 1 - w + T, sl]
        cnt = jnp.minimum(w, pos0 + 1 + jnp.arange(T)).astype(jnp.float32)
        pooled.append(s / cnt[None, :, None])
    d = (jnp.concatenate(pooled, axis=-1) - c.astype(jnp.float32)).reshape(B, T, POOL_GROUPS, POOL_GDIM)
    y = (jnp.einsum('btgc,gcd->btgd', d, w_p).reshape(B, T, BR_WIDTH) + b_p) * scale
    return y.astype(c.dtype), cat[:, -POOL_BUF:]

def hgrn2(q, f, i, g_out, s0, lb, norm_g):
    B, T, _ = q.shape
    f32 = jnp.float32
    ff = f.astype(f32)
    log_f = jnp.logaddexp(jnp.log(lb), jnp.log1p(-lb) + jax.nn.log_sigmoid(ff))
    k = (1.0 - lb) * jax.nn.sigmoid(-ff)
    qf = jax.nn.silu(q.astype(f32))
    vf = i.astype(f32)
    L = HG_CHUNK if T % HG_CHUNK == 0 else T
    n = T // L

    def to_chunks(a, d):
        return a.reshape(B, n, L, HG_HEADS, d).swapaxes(0, 1)

    mask = jnp.tril(jnp.ones((L, L), dtype=bool))[None, :, :, None, None]

    def step(S, inp):
        qc, kc, vc, lfc = inp
        bcum = jnp.cumsum(lfc, axis=1)
        o_inter = jnp.einsum('bthk,bhkv->bthv', qc * jnp.exp(bcum), S)
        diff = bcum[:, :, None] - bcum[:, None, :]
        decay = jnp.exp(jnp.where(mask, diff, -jnp.inf))
        att = jnp.einsum('bthk,bshk,btshk->bhts', qc, kc, decay)
        o_intra = jnp.einsum('bhts,bshv->bthv', att, vc)
        b_last = bcum[:, -1]
        kd = kc * jnp.exp(b_last[:, None] - bcum)
        S_new = jnp.exp(b_last)[..., None] * S + jnp.einsum('bshk,bshv->bhkv', kd, vc)
        return S_new, o_inter + o_intra

    s_t, o = lax.scan(step, s0.astype(f32),
                      (to_chunks(qf, HG_DK), to_chunks(k, HG_DK), to_chunks(vf, HG_DV), to_chunks(log_f, HG_DK)))
    o = o.swapaxes(0, 1).reshape(B, T, HG_HEADS, HG_DV)
    o = o * lax.rsqrt(jnp.mean(o * o, axis=-1, keepdims=True) + RMS_EPS) * norm_g
    o = o.reshape(B, T, BR_WIDTH) * jax.nn.silu(g_out.astype(f32))
    return o.astype(q.dtype), s_t.astype(s0.dtype)

def memory_kv(mem, wk, wv):
    B, M, _ = mem.shape
    k = jnp.einsum('bmd,de->bme', mem, wk).reshape(B, M, X_HEADS, X_HDIM)
    v = jnp.einsum('bmd,de->bme', mem, wv).reshape(B, M, X_HEADS, X_HDIM)
    return k, v

def cross_attend(x, mem_k, mem_v, wq, wo):
    B, T, _ = x.shape
    q = jnp.einsum('btd,de->bte', x, wq).reshape(B, T, X_HEADS, X_HDIM)
    s = jnp.einsum('bthd,bmhd->bhtm', q.astype(jnp.float32), mem_k.astype(jnp.float32)) * (X_HDIM ** -0.5)
    p = jax.nn.softmax(s, axis=-1)
    o = jnp.einsum('bhtm,bmhd->bthd', p, mem_v.astype(jnp.float32)).reshape(B, T, D_MODEL).astype(x.dtype)
    return jnp.einsum('btd,de->bte', o, wo)

def moe(x, router_w, router_b, e_wg, e_wu, e_wd):
    B, T, D = x.shape
    xt = x.reshape(B * T, D)
    f32 = jnp.float32
    s = jax.nn.sigmoid(jnp.einsum('nd,de->ne', xt.astype(f32), router_w.astype(f32)))
    sel = (s + router_b.astype(f32)).reshape(-1, N_GROUPS, EXPERTS_PER_GROUP)
    group_score = lax.top_k(sel, TOP_K)[0].sum(axis=-1)
    g_idx = jnp.argmax(group_score, axis=-1)
    g_take = jnp.broadcast_to(g_idx[:, None, None], (g_idx.shape[0], 1, EXPERTS_PER_GROUP))
    in_group = jnp.take_along_axis(sel, g_take, axis=1)[:, 0]
    _, loc = lax.top_k(in_group, TOP_K)
    e_idx = g_idx[:, None] * EXPERTS_PER_GROUP + loc
    w = jnp.take_along_axis(s, e_idx, axis=-1)
    w = w / jnp.sum(w, axis=-1, keepdims=True)
    combine = jnp.einsum('nk,nke->ne', w, jax.nn.one_hot(e_idx, N_EXPERTS, dtype=f32))
    y = jnp.zeros((B * T, D), f32)
    for e in range(N_EXPERTS):
        h = jax.nn.silu(xt @ e_wg[e]) * (xt @ e_wu[e])
        y = y + combine[:, e:e + 1] * (h @ e_wd[e])
    return y.reshape(B, T, D).astype(x.dtype)

def mixer_block(x, conv_buf, h0, pool_buf, s0, pos0, lb, p):
    B, T, _ = x.shape
    z = jnp.einsum('btd,de->bte', x, p['w_in']) + p['b_in']
    u, v, yg, xb, c, q, f, i, go, gz = jnp.split(z, SPLIT_POINTS, axis=-1)
    o_a, v_rows = chunk_sgu(u, v, p['sgu_ln_g'], p['sgu_ln_b'], p['sgu_w'], p['sgu_b'])
    xc, conv_new = causal_conv(xb, conv_buf, p['conv_w'], p['conv_b'])
    h, h_new = rg_lru(xc, h0, p['lru_wr'], p['lru_br'], p['lru_wi'], p['lru_bi'], p['lru_lambda'])
    o_b = jax.nn.gelu(yg) * h
    o_c, pool_new = pool_mixer(c, pool_buf, pos0, p['pool_w'], p['pool_b'], p['pool_scale'])
    o_d, s_new = hgrn2(q, f, i, go, s0, lb, p['hgrn_norm_g'])
    branches = jnp.stack([o_a, o_b, o_c, o_d], axis=2)
    proj = jnp.einsum('btgc,gcd->btgd', branches, p['w_branch'])
    gates = jax.nn.sigmoid(gz.reshape(B, T, N_BRANCH, D_MODEL))
    y = jnp.einsum('btd,de->bte', jnp.sum(gates * proj, axis=2), p['w_out'])
    return y, (conv_new, h_new, pool_new, s_new, v_rows)

def trunk_layer(x, conv_buf, h0, pool_buf, s0, mem_k, mem_v, pos0, lb, p):
    mix, states = mixer_block(x, conv_buf, h0, pool_buf, s0, pos0, lb, p)
    x = layer_norm(DN_ALPHA * x + mix, p['ln_g'][0], p['ln_b'][0])
    x = layer_norm(DN_ALPHA * x + cross_attend(x, mem_k, mem_v, p['x_wq'], p['x_wo']), p['ln_g'][1], p['ln_b'][1])
    x = layer_norm(DN_ALPHA * x + moe(x, p['router_w'], p['router_b'], p['e_wg'], p['e_wu'], p['e_wd']),
                   p['ln_g'][2], p['ln_b'][2])
    return x, states

def setup_inputs(seed: int = 0) -> dict:
    key = jax.random.key(seed)
    keys = iter(jax.random.split(key, 64))
    f32 = jnp.float32

    def nrm(shape, scale):
        return jax.random.normal(next(keys), shape, f32) * scale

    d_s = D_MODEL ** -0.5
    u = jax.random.uniform(next(keys), (DEPTH, BR_WIDTH), f32, 0.9, 0.999)
    a = u ** (1.0 / LRU_C)
    inp = {}
    inp['x_prompt'] = nrm((BATCH, SEQ, D_MODEL), 1.0)
    inp['x_sample'] = nrm((DEC_BATCH, DEC_SEQ, D_MODEL), 1.0)
    inp['mem_prompt'] = nrm((BATCH, N_MEM, D_MODEL), 1.0)
    inp['cache_mem_k'] = nrm((DEPTH, DEC_BATCH, N_MEM, X_HEADS, X_HDIM), 1.0)
    inp['cache_mem_v'] = nrm((DEPTH, DEC_BATCH, N_MEM, X_HEADS, X_HDIM), DN_BETA)
    inp['state_conv'] = nrm((DEPTH, DEC_BATCH, CONV_W - 1, BR_WIDTH), 1.0)
    inp['state_rglru'] = nrm((DEPTH, DEC_BATCH, BR_WIDTH), 0.5)
    inp['state_pool'] = nrm((DEPTH, DEC_BATCH, POOL_BUF, BR_WIDTH), 1.0)
    inp['state_hgrn'] = nrm((DEPTH, DEC_BATCH, HG_HEADS, HG_DK, HG_DV), 1.0)
    inp['ln_in_g'] = 1.0 + nrm((D_MODEL,), 0.1)
    inp['ln_in_b'] = nrm((D_MODEL,), 0.02)
    inp['w_in'] = nrm((DEPTH, D_MODEL, IN_WIDTH), d_s)
    inp['b_in'] = nrm((DEPTH, IN_WIDTH), 0.02)
    inp['sgu_ln_g'] = 1.0 + nrm((DEPTH, BR_WIDTH), 0.1)
    inp['sgu_ln_b'] = nrm((DEPTH, BR_WIDTH), 0.02)
    inp['sgu_w'] = nrm((DEPTH, SGU_GROUPS, SGU_CHUNK, SGU_CHUNK), SGU_CHUNK ** -0.5)
    inp['sgu_b'] = 1.0 + nrm((DEPTH, SGU_GROUPS, SGU_CHUNK), 0.1)
    inp['conv_w'] = nrm((DEPTH, CONV_W, BR_WIDTH), CONV_W ** -0.5)
    inp['conv_b'] = nrm((DEPTH, BR_WIDTH), 0.02)
    inp['lru_wr'] = nrm((DEPTH, LRU_HEADS, LRU_HDIM, LRU_HDIM), LRU_HDIM ** -0.5)
    inp['lru_br'] = nrm((DEPTH, BR_WIDTH), 0.02)
    inp['lru_wi'] = nrm((DEPTH, LRU_HEADS, LRU_HDIM, LRU_HDIM), LRU_HDIM ** -0.5)
    inp['lru_bi'] = nrm((DEPTH, BR_WIDTH), 0.02)
    inp['lru_lambda'] = jnp.log(a) - jnp.log1p(-a)
    inp['pool_w'] = nrm((DEPTH, POOL_GROUPS, POOL_GDIM, POOL_GDIM), POOL_GDIM ** -0.5)
    inp['pool_b'] = nrm((DEPTH, BR_WIDTH), 0.02)
    inp['pool_scale'] = 1.0 + nrm((DEPTH, BR_WIDTH), 0.1)
    inp['hgrn_lb'] = nrm((DEPTH, BR_WIDTH), 1.0)
    inp['hgrn_norm_g'] = 1.0 + nrm((DEPTH, HG_DV), 0.1)
    inp['w_branch'] = nrm((DEPTH, N_BRANCH, BR_WIDTH, D_MODEL), BR_WIDTH ** -0.5)
    inp['w_out'] = nrm((DEPTH, D_MODEL, D_MODEL), d_s * DN_BETA)
    inp['x_wq'] = nrm((DEPTH, D_MODEL, D_MODEL), d_s)
    inp['x_wk'] = nrm((DEPTH, D_MODEL, D_MODEL), d_s)
    inp['x_wv'] = nrm((DEPTH, D_MODEL, D_MODEL), d_s * DN_BETA)
    inp['x_wo'] = nrm((DEPTH, D_MODEL, D_MODEL), d_s * DN_BETA)
    inp['ln_g'] = 1.0 + nrm((DEPTH, 3, D_MODEL), 0.1)
    inp['ln_b'] = nrm((DEPTH, 3, D_MODEL), 0.02)
    inp['router_w'] = nrm((D_MODEL, N_EXPERTS), d_s)
    inp['router_b'] = nrm((N_EXPERTS,), 0.01)
    inp['e_wg'] = nrm((DEPTH, N_EXPERTS, D_MODEL, D_EXPERT), d_s)
    inp['e_wu'] = nrm((DEPTH, N_EXPERTS, D_MODEL, D_EXPERT), d_s)
    inp['e_wd'] = nrm((DEPTH, N_EXPERTS, D_EXPERT, D_MODEL), D_EXPERT ** -0.5 * DN_BETA)
    return inp

def reference(x_prompt, x_sample, mem_prompt, cache_mem_k, cache_mem_v, state_conv, state_rglru, state_pool,
              state_hgrn, ln_in_g, ln_in_b, w_in, b_in, sgu_ln_g, sgu_ln_b, sgu_w, sgu_b, conv_w, conv_b,
              lru_wr, lru_br, lru_wi, lru_bi, lru_lambda, pool_w, pool_b, pool_scale, hgrn_lb, hgrn_norm_g,
              w_branch, w_out, x_wq, x_wk, x_wv, x_wo, ln_g, ln_b, router_w, router_b, e_wg, e_wu, e_wd):
    f32 = jnp.float32
    lb_cum = jnp.cumsum(jax.nn.softmax(hgrn_lb.astype(f32), axis=0), axis=0)
    lbs = lb_cum - lb_cum[0]
    xp = layer_norm(x_prompt, ln_in_g, ln_in_b)
    xs = layer_norm(x_sample, ln_in_g, ln_in_b)
    dt = x_prompt.dtype
    zero_conv = jnp.zeros((BATCH, CONV_W - 1, BR_WIDTH), dt)
    zero_h = jnp.zeros((BATCH, BR_WIDTH), dt)
    zero_pool = jnp.zeros((BATCH, POOL_BUF, BR_WIDTH), dt)
    zero_s = jnp.zeros((BATCH, HG_HEADS, HG_DK, HG_DV), dt)
    mk_pl, mv_pl, cp_l, hp_l, pp_l, sp_l = [], [], [], [], [], []
    cs_l, hs_l, ps_l, ss_l, vs_l = [], [], [], [], []
    for l in range(DEPTH):
        p = dict(w_in=w_in[l], b_in=b_in[l], sgu_ln_g=sgu_ln_g[l], sgu_ln_b=sgu_ln_b[l], sgu_w=sgu_w[l],
                 sgu_b=sgu_b[l], conv_w=conv_w[l], conv_b=conv_b[l], lru_wr=lru_wr[l], lru_br=lru_br[l],
                 lru_wi=lru_wi[l], lru_bi=lru_bi[l], lru_lambda=lru_lambda[l], pool_w=pool_w[l],
                 pool_b=pool_b[l], pool_scale=pool_scale[l], hgrn_norm_g=hgrn_norm_g[l],
                 w_branch=w_branch[l], w_out=w_out[l], x_wq=x_wq[l], x_wo=x_wo[l], ln_g=ln_g[l], ln_b=ln_b[l],
                 router_w=router_w, router_b=router_b, e_wg=e_wg[l], e_wu=e_wu[l], e_wd=e_wd[l])
        mk_p, mv_p = memory_kv(mem_prompt, x_wk[l], x_wv[l])
        xp, (cp, hp, pp, sp, _) = trunk_layer(xp, zero_conv, zero_h, zero_pool, zero_s, mk_p, mv_p, 0, lbs[l], p)
        xs, (cs_, hs, ps, ss, vs) = trunk_layer(xs, state_conv[l], state_rglru[l], state_pool[l], state_hgrn[l],
                                                cache_mem_k[l], cache_mem_v[l], PAST_LEN, lbs[l], p)
        mk_pl.append(mk_p); mv_pl.append(mv_p); cp_l.append(cp); hp_l.append(hp); pp_l.append(pp); sp_l.append(sp)
        cs_l.append(cs_); hs_l.append(hs); ps_l.append(ps); ss_l.append(ss); vs_l.append(vs)
    return (xp, xs, jnp.stack(mk_pl), jnp.stack(mv_pl), jnp.stack(cp_l), jnp.stack(hp_l), jnp.stack(pp_l),
            jnp.stack(sp_l), jnp.stack(cs_l), jnp.stack(hs_l), jnp.stack(ps_l), jnp.stack(ss_l), jnp.stack(vs_l))


_drawn_inputs = setup_inputs


def setup_inputs(seed=0):
    import zlib

    import numpy as np

    out = dict(_drawn_inputs(seed))
    spreads = {}
    factors = {'sgu_ln_b': 2.872, 'lru_br': 8.0, 'lru_bi': 8.0, 'pool_b': 3.005}
    for name, (base, spread) in spreads.items():
        noise = np.random.default_rng([zlib.crc32(name.encode()), seed]).standard_normal(out[name].shape)
        drawn = base * np.exp(spread * noise) if base else spread * noise
        out[name] = __import__('jax').numpy.asarray(drawn.astype(out[name].dtype))
    for name, factor in factors.items():
        out[name] = (out[name] * factor).astype(out[name].dtype)
    return out
```

```python
from contextlib import ExitStack

import numpy as np

import concourse.bass as bass
from concourse import mybir

F32 = mybir.dt.float32
I32 = mybir.dt.int32
ALU = mybir.AluOpType
ACT = mybir.ActivationFunctionType
AX = mybir.AxisListType.X

D = 1024
W = 512
TP = 512
NSEQ, LSEQ = 8, 8
TS = NSEQ * LSEQ
T = TP + TS
P = 128
KD = D // P
KW = W // P
TILES = [P] * (TP // P) + [TS]
NT = len(TILES)
HALF = T // 2
PP = HALF * 2 - TP
PH = HALF - PP
NMEM, XH, XD = 256, 4, 256
NE, NG, EPG, DE = 16, 4, 4, 512
ALPHA = 2.0 ** 0.25
LN_EPS, RMS_EPS = 1e-5, 1e-6
CONV_W, POOL_BUF = 4, 15
WINDOWS = (2, 4, 8, 16)
LRU_C = 8.0
LEVELS = (64, 32, 16, 8, 4, 2, 1)
SLOT = 2048
ITEMS = TP // P + NSEQ
PEEL = 2
MOE_MIN = 2 * T // 128
MOE_T = 24
GU, GV, GY, GX, GC, GQ, GF, GI, GO, GZ = range(10)

PAR_BIN = 0
PAR_CW = 68
PAR_CB = PAR_CW + CONV_W * KW
PAR_BR, PAR_BI, PAR_LAM, PAR_PB, PAR_PS = (PAR_CB + 4 * k for k in range(1, 6))
PAR_NG = PAR_PS + 4
PAR_N = PAR_NG + 1

C_ID, C_ONE, C_TRI, C_STRI, C_MASK = 0, 128, 256, 384, 512
C_RH = C_MASK + 7 * 128
C_RL = C_RH + T
C_BLK = C_RL + T
C_RC = C_BLK + NSEQ
C_N = C_RC + 4 * 16
C2_TILE, C2_TOK = 0, MOE_T * NE
C2_N = C2_TOK + NT


def shape_constants():
    c = np.zeros((P, C_N), np.float32)
    i = np.arange(P)
    s, t = i[:, None], i[None, :]
    c[:, C_ID:C_ID + P] = s == t
    c[:, C_ONE:C_ONE + P] = 1.0
    c[:, C_TRI:C_TRI + P] = s <= t
    c[:, C_STRI:C_STRI + P] = s < t
    for n, h in enumerate(LEVELS):
        c[:, C_MASK + n * P:C_MASK + (n + 1) * P] = (s // (2 * h) == t // (2 * h)) & (s // h % 2 == 0) & (t // h % 2 == 1)
    tok = np.arange(T)
    starts = (tok >= TP) & ((tok - TP) % LSEQ == 0)
    c[:, C_RH:C_RH + T] = ~(starts | ((tok < TP) & (tok % P == 0)))
    c[:, C_RL:C_RL + T] = ~(starts | (tok == 0))
    c[:, C_BLK:C_BLK + NSEQ] = (s // LSEQ == np.arange(NSEQ)[None, :])
    for g, w in enumerate(WINDOWS):
        c[:, C_RC + 16 * g:C_RC + 16 * g + 16] = 1.0 / np.minimum(w, np.arange(16) + 1)
    c2 = np.zeros((P, C2_N), np.float32)
    c2[:, C2_TILE:C2_TILE + MOE_T * NE] = np.repeat(np.arange(MOE_T), NE)[None, :]
    c2[:, C2_TOK:C2_TOK + NT] = s + P * np.arange(NT)[None, :]
    return c, c2


def psum_schedule():
    uses, count = {}, [0] * 8

    def add(name, bank):
        uses[name] = (bank, count[bank])
        count[bank] += 1

    turn = {"low": 0, "high": 0}

    def low(name):
        add(name, turn["low"] % 4)
        turn["low"] += 1

    def high(name):
        add(name, 4 + turn["high"] % 4)
        turn["high"] += 1

    for name in ["par", "pst", "cst", "sgw", "wbd"] + [f"memT{k}" for k in range(4)]:
        high(name)
    for k in range(8):
        low(f"kv{k}")
    for t in range(NT):
        high(f"xT{t}a")
        high(f"xT{t}b")
    merge_base = None
    for step in mixer_steps():
        if step[0] == "merge":
            merge_base = merge_base or list(count)
            add(f"mg{step[1]}_{step[2]}", step[2] % 2)
            add(f"mp{step[1]}_{step[2]}", 2 + step[2] % 2)
        for name in step_units(step):
            (low if step[0] == "z" else high)(name)
    for b in range(4):
        count[b] += (4 - PEEL) * 8
    turn["low"] = 0
    for t in range(NT):
        low(f"mix{t}a")
        low(f"mix{t}b")
        high(f"yT{t}a")
        high(f"yT{t}b")
    for c in range(4):
        for n in range(4):
            low(f"q{c}{n}")
    for n in range(4):
        high(f"KT0_{n}")
    for item in range(ITEMS + 1):
        if item < ITEMS:
            low(f"S{item}a")
            low(f"S{item}b")
            if 3 <= item < ITEMS - 1:
                for n in range(4):
                    high(f"KT{item + 1}_{n}")
        if item:
            high(f"PT{item - 1}a")
            high(f"PT{item - 1}b")
            low(f"O{item - 1}a")
            low(f"O{item - 1}b")
    for t in range(NT):
        low(f"att{t}a")
        low(f"att{t}b")
        high(f"zT{t}a")
        high(f"zT{t}b")
    for t in range(NT):
        high(f"rt{t}")
    high("pos")
    high("cnt")
    high("tab")
    moe_base = list(count)
    return uses, merge_base, moe_base


def z_units():
    out = [("go", h) for h in range(KW)] + [(g, j) for j in range(KW) for g in ("xb", "c")]
    out += [(g, j) for j in range(KW) for g in ("yg", "u")] + [("v", t) for t in range(NT)]
    return out


def mixer_steps():
    steps = [("z", "i", t, 0) for t in range(NT)]
    steps += [("z", g, h, n) for h in range(KW) for g in ("q", "f") for n in range(2)]
    rest = [("z", g, j, n) for g, j in z_units() for n in range(1 if g == "v" else 2)]
    own = [("hgrn", what, h) for h in range(KW) for what in ["prep", "keys", "state", "diag"]
           + [f"lev{n}" for n in range(len(LEVELS) + 2)] + ["out", "norm"]]
    weight = {"prep": 5, "keys": 2, "out": 2, "norm": 3}
    total = sum(weight.get(step[1], 1) for step in own)
    count, done = len(rest), 0
    for step in own:
        steps.append(step)
        done += weight.get(step[1], 1)
        while rest and (count - len(rest)) * total < count * done:
            steps.append(rest.pop(0))
    units = [("merge", i, u) for i in range(PEEL) for u in range(16)]

    def merge(count):
        for _ in range(count):
            if units:
                steps.append(units.pop(0))

    for j in range(KW):
        steps.append(("pool", "window", j))
        merge(1)
        steps.append(("pool", "product", j))
        merge(1)
        steps.append(("pool", "out", j))
    steps.append(("lru", "conv", 0))
    merge(1)
    steps += [("lru", "product", 0), ("lru", "sigmoids", 0)]
    for j in range(KW):
        merge(1)
        steps.append(("lru", "gate", j))
        merge(1)
        if j < KW - 1:
            steps.append(("lru", "conv", j + 1))
            merge(1)
            steps.append(("lru", "product", j + 1))
            merge(1)
        steps.append(("lru", "scan", j))
        if j < KW - 1:
            steps.append(("lru", "sigmoids", j + 1))
        merge(1)
    steps.append(("sgu", "norm", 0))
    merge(2)
    for j in range(KW):
        steps.append(("sgu", "product", j))
        merge(1)
        steps.append(("sgu", "out", j))
    merge(len(units))
    steps.append(("states",))
    return steps


def step_units(step):
    if step[0] == "z":
        return [f"{step[1]}{step[2]}_{step[3]}"]
    if step[0] == "hgrn":
        what, h = step[1], step[2]
        if what == "keys":
            return [f"kdT{h}", f"kdS{h}"]
        if what == "state":
            return [f"U{h}", f"US{h}a", f"US{h}b"]
        if what == "diag":
            return [f"L{h}d", f"M{h}d"]
        if what.startswith("lev"):
            n = int(what[3:]) - 1
            if 0 <= n < len(LEVELS):
                return [f"L{h}{n}"] + ([f"M{h}{n}"] if LEVELS[n] <= 4 else [])
            return []
        if what == "out":
            return [f"OP{h}", f"OS{h}"]
        if what == "norm":
            return [f"SP{h}", f"SS{h}"]
        return []
    if step[0] == "states":
        return ["oc", "op", "oq"]
    if step[1] != "product":
        return []
    return [f"{name}{step[2]}" for name in {"pool": ("pp", "ps"), "lru": ("rp", "ip", "rs"), "sgu": ("gp", "gs")}[step[0]]]


def weight_plan():
    plan = [(f"wk{c}", 1, f"kv{c}") for c in range(4)] + [(f"wv{c}", 1, f"kv{4 + c}") for c in range(4)]
    plan += [(f"i{c}", 1, f"i{NT - 1}_0") for c in range(2)]
    plan += [(f"qf{h}", 2, f"f{h}_1") for h in range(KW)]
    plan += [(f"go{c}", 1, f"go{2 * c + 1}_1") for c in range(2)]
    plan += [(f"xc{j}", 2, f"c{j}_1") for j in range(KW)]
    plan += [(f"yu{j}", 2, f"u{j}_1") for j in range(KW)]
    plan += [(f"v{c}", 1, f"v{NT - 1}_0") for c in range(2)]
    before = len(plan)
    plan += [(f"merge{i}_{k}", 1, f"mp{i}_{MERGE_LAST[k]}" if i < PEEL else None) for i in range(4) for k in range(6)]
    plan += [(f"wo{c}", 1, f"mix{NT - 1}{'ab'[c // 2]}") for c in range(4)]
    plan += [(f"wq{c}", 1, f"q{c}3") for c in range(4)]
    plan += [(f"wx{c}", 1, f"att{NT - 1}{'ab'[c // 2]}") for c in range(4)]
    landed, out = [0] * RING, []
    for n, (name, dmas, last) in enumerate(plan):
        landed[n % RING] += 16 * dmas
        out.append((name, n % RING, landed[n % RING], last))
    return out, before, landed


RING = 6
MERGE_LAST = (7, 3, 7, 15, 11, 15)


def trunk(nc, x_p, x_s, mem, ck, cv, st_conv, st_h, st_pool, st_hg, ln_in_g, ln_in_b, w_in, b_in, sgu_g, sgu_b_ln,
          sgu_w, sgu_b, conv_w, conv_b, lru_wr, lru_br, lru_wi, lru_bi, lru_lam, pool_w, pool_b, pool_s, norm_g,
          w_branch, w_out, x_wq, x_wk, x_wv, x_wo, ln_g, ln_b, rt_w, rt_b, e_wg, e_wu, e_wd, cst_in, cst2_in,
          y_p, y_s, o_mk, o_mv, o_conv_p, o_h_p, o_pool_p, o_hg_p, o_conv_s, o_h_s, o_pool_s, o_hg_s, o_sgu):
    uses, merge_base, moe_base = psum_schedule()
    steps = mixer_steps()
    chunks, first_merge, landed_all = weight_plan()
    moe_landed = landed_all + [0] * RING
    chunk = {name: (slot, value) for name, slot, value, _ in chunks}

    x0_d = nc.dram_tensor("x0_scratch", (T, D), F32, kind="Internal").ap()
    x2_d = nc.dram_tensor("x2_scratch", (T, D), F32, kind="Internal").ap()
    ys_d = nc.dram_tensor("expert_rows", (MOE_T * P, D), F32, kind="Internal").ap()

    with ExitStack() as ctx:
        base = 16512

        def place(name, at, shape, dtype=F32):
            size = int(np.prod(shape[1:]))
            assert base + 4 * (at + size) <= 229344, name
            return nc.alloc_sbuf_tensor_at(name, shape, dtype, offset=base + 4 * at, align_bytes=4)

        def sem(name):
            return ctx.enter_context(nc.semaphore(name))

        ring = place("ring", 0, [P, RING, SLOT])
        xT = place("xT", 12288, [P, KD, T])
        ob = place("ob", 16896, [P, 4, KW, T])
        mer = place("mer", 26112, [P, KD, T])
        q_all = place("q_all", 26112, [P, KW, T])
        f_all = place("f_all", 28416, [P, KW, T])
        v_tok = place("v_tok", 30720, [P, NT, W])
        i_tok = place("i_tok", 33280, [P, NT, W])
        lng = place("lng", 35840, [P, D])
        lnb = place("lnb", 36864, [P, D])
        s_old = place("s_old", 35840, [P, NSEQ, P])
        s_new = place("s_new", 36864, [P, NSEQ, P])
        cst = place("cst", 37888, [P, C_N])
        pc = place("pc", 40520, [P, 120])
        wr = place("wr", 40640, [P, KW, P])
        wi = place("wi", 41152, [P, KW, P])
        wp = place("wp", 41664, [P, KW, P])
        swT = place("swT", 42176, [P, KW, P])
        sbT = place("sbT", 42688, [P, KW, TS])
        x_tok = place("x_tok", 42944, [P, NT, D])
        tmp = place("tmp", 42944, [P, 6, T])
        att = place("att", 46400, [P, T])
        att_m = place("att_m", 46976, [P, T])
        kdT = place("kdT", 47552, [P, 5, P])
        conv_out = [tmp[:, 0], place("conv_odd", 47552, [P, T])[:]]
        s_pr = place("s_pr", 48192, [P, 4, P])
        xpad = place("xpad", 48704, [P, KW, 3 + TP + NSEQ * (3 + LSEQ)])
        bias_i = place("bias_i", 51116, [P, W])
        bias_v = place("bias_v", 51628, [P, W])
        vm = place("vm", 52140, [P, 4, P])
        pst = place("pst", 52652, [P, KW, NSEQ * POOL_BUF])
        h0 = place("h0", 53132, [P, KW, NSEQ])
        mem_tok = place("mem_tok", 16896, [P, 2, D])
        memT = place("memT", 18944, [P, KD, NMEM])
        par = place("par", 20992, [P, P])
        raw_pool = place("raw_pool", 21120, [P, W])
        raw_conv = place("raw_conv", 21632, [P, W])
        raw_h = place("raw_h", 22144, [P, W])
        raw_sw = place("raw_sw", 22656, [P, KW, P])
        raw_sb = place("raw_sb", 23168, [P, KW, TS])
        k_stage = place("k_stage", 30720, [P, 2, D])
        v_stage = place("v_stage", 32768, [P, 2, D])
        small = place("small", 53164, [P, 44])
        st_out = place("st_out", 30720, [P, 3, W])
        cpad = place("cpad", 42944, [P, 2, POOL_BUF + TP + NSEQ * (POOL_BUF + LSEQ)])
        csum = place("csum", 42944 + 1422, [P, 2, POOL_BUF + TP + NSEQ * (POOL_BUF + LSEQ)])
        sgu_rows = place("sgu_rows", 51116, [P, W])
        sg_g = place("sg_g", 35840, [P, W])
        sg_b = place("sg_b", 36352, [P, W])
        gate = place("gate", 33280, [P, 2, HALF])
        prod = place("prod", 33856, [P, 2, HALF])
        qT = place("qT", 26112, [P, KD, T])
        oT = place("oT", 48064, [P, KD, T])
        kv_k = [place("kv_k0", 16896, [P, 2, D]), place("kv_k1", 23040, [P, 2, D])]
        kv_t = [place("kv_t0", 18944, [P, KD, NMEM]), place("kv_t1", 30720, [P, KD, NMEM])]
        kv_v = [place("kv_v0", 20992, [P, 2, D]), place("kv_v1", 32768, [P, 2, D])]
        prob = [place("prob0", 40640, [P, XH, NMEM]), place("prob1", 41664, [P, XH, NMEM])]
        pT = [place("pT0", 34816, [P, KD, P]), place("pT1", 25088, [P, KD, P])]
        smx = place("smx", 42688, [P, 2, 12])
        rw = place("rw", 52672, [P, KD, NE])
        NRING = 12
        mring = place("mring", 0, [P, NRING, SLOT])
        xg = place("xg", 24576, [P, 2, D])
        xgT = place("xgT", 26624, [P, 2, KD, P])
        hs = place("hs", 28672, [P, 2, DE])
        hT = place("hT", 29696, [P, 2, 4, P])
        y_out = place("y_out", 30720, [P, 2, D])
        ya = place("ya", 48064, [P, 2, D])
        yb = place("yb", 50112, [P, 2, D])
        rsc = place("rsc", 40640, [P, 17, NT * NE])
        c2 = place("c2", 42000, [P, C2_N])
        rbias = place("rbias", 42400, [P, NE])
        cols = place("cols", 42424, [P, 12, 20])
        ints = place("ints", 42664, [P, 5, 8], I32)
        eid = place("eid", 42704, [P, MOE_T], I32)
        eidf = place("eidf", 42728, [P, MOE_T])
        used_tiles = place("used_tiles", 42816, [P, 1], I32)
        table = place("table", 42752, [P, MOE_T + 2], I32)
        hot_row = place("hot_row", 30720, [P, 2 * NT, P])
        hot_col = place("hot_col", 32000, [P, 2 * NT, MOE_T])
        places = place("places", 32240, [P, P])
        tile_starts = place("tile_starts", 32368, [P, MOE_T])
        tile_numbers = place("tile_numbers", 32392, [P, MOE_T])
        slots = place("slots", 32416, [P, 2 * NT])
        slot_tiles = place("slot_tiles", 32432, [P, 2 * NT])
        tokens = place("tokens", 32448, [P, 2 * NT])

        bank = [ctx.enter_context(nc.psum_tensor(f"bank{b}", [P, 512], F32)) for b in range(8)]
        full = [sem(f"bank{b}_full") for b in range(8)]
        free = [sem(f"bank{b}_free") for b in range(8)]
        passed = sem("loop_wait_passed")
        landed = [sem(f"ring{k}_landed") for k in range(RING)]

        def acquire(eng, name):
            b, n = uses[name]
            if n:
                eng.wait_ge(free[b], n)
            return bank[b], full[b]

        def loop_wait(eng, semaphore, value):
            eng.wait_ge(semaphore, value)
            eng.sem_inc(passed, 1)

        def plain_wait(eng, semaphore, value):
            eng.wait_ge(semaphore, value)

        def tiles_used(eng):
            eng.wait_ge(rt_eid, 1)
            return eng.value_load(used_tiles[0:1, 0:1], min_val=0, max_val=MOE_T)

        def attention_item(item):
            if item < TP // P:
                return P, P * item, 0, item == 0
            b = item - TP // P
            return LSEQ, TP + LSEQ * b, (1 + b) % 2, True

        def arrived(eng, name):
            b, n = uses[name]
            eng.wait_ge(full[b], n + 1)
            return bank[b], free[b]

        ld_x, ld_rows, ld_cst, ld_par, ld_raw, ld_small, ld_bias = (
            sem("x_landed"), sem("norm_rows_landed"), sem("constants_landed"), sem("params_landed"),
            sem("raw_states_landed"), sem("mixer_weights_landed"), sem("bias_rows_landed"))
        zeroed, mem_landed, s0_landed = sem("zeroed"), sem("memory_landed"), sem("hgrn_state_landed")
        dve_step, act_step, pool_step = sem("vector_step"), sem("scalar_step"), sem("gpsimd_step")
        ln_var, ln_std, ln_out = sem("norm_variance"), sem("norm_deviation"), sem("norm_written")
        x0_stored, kv_stored, out_stored = sem("x0_stored"), sem("memory_kv_stored"), sem("outputs_stored")
        biased = sem("token_major_biased")
        hg_ln, hg_b, hg_e, hg_d, hg_k, hg_kd = (sem("hgrn_log"), sem("hgrn_cumulated"), sem("hgrn_decay"),
                                                sem("hgrn_tail_log"), sem("hgrn_tail"), sem("hgrn_keys"))
        hg_vm, hg_sub, hg_exp, hg_x, hg_att, hg_rs, hg_done = (
            sem("hgrn_values_masked"), sem("hgrn_level_log"), sem("hgrn_level_decay"), sem("hgrn_level_scaled"),
            sem("hgrn_scores"), sem("hgrn_rms"), sem("hgrn_head_done"))
        hg_snew, hg_stored = sem("hgrn_states_new"), sem("hgrn_states_stored")
        pl_pad, pl_d = sem("pool_padded"), sem("pool_differences")
        lr_c0, lr_y, lr_u, lr_l = sem("lru_abs"), sem("lru_exp"), sem("lru_one_plus"), sem("lru_ln")
        lr_xc, lr_a, lr_m, lr_s, lr_done = (sem("lru_conv"), sem("lru_decay"), sem("lru_square"), sem("lru_root"),
                                            sem("lru_head_done"))
        v_normed, st_cols, sgu_done = sem("spatial_values_normed"), sem("state_columns"), sem("sgu_done")
        mer_add = sem("merge_added")

        b_in_rows = b_in.rearrange("a (c p) -> (a c) p", p=P)
        win = w_in.rearrange("a (k p) n -> p (a k) n", p=P)

        def w1024(w, c):
            return w[0].rearrange("(k p) n -> p k n", p=P)[:, :, 256 * c:256 * c + 256]

        def slot_k8(k):
            return ring[:, k, :].rearrange("p (k n) -> p k n", k=KD)

        def slot_k4(k):
            return ring[:, k, :].rearrange("p (k n) -> p k n", k=KW)

        def xp_prompt(t, j, at):
            return t[:, j, at:at + TP]

        table_rest = sem("table_past_tiles_zeroed")
        k_landed, v_landed = ([sem(f"memory_{x}{n}_landed") for n in range(2)] for x in ("keys", "values"))
        att_max, att_prob = sem("scores_max"), sem("probabilities")
        x2_stored, rt_landed, rt_logit, rt_chosen, rt_slots, rt_eid = (
            sem("x2_stored"), sem("router_inputs_landed"), sem("router_scores"), sem("experts_chosen"),
            sem("slots_written"), sem("tile_experts"))
        hot_ready, xg_idx, xg_landed = sem("slot_table_one_hots"), sem("gather_index"), [sem("rows0_gathered"), sem("rows1_gathered")]
        ys_stored, yab_landed = [sem("expert_rows0_stored"), sem("expert_rows1_stored")], [sem("pair0_gathered"), sem("pair1_gathered")]
        landed_hi = [sem(f"ring{k}_landed") for k in range(RING, 2 * RING)]
        mlanded = landed + landed_hi
        combined = sem("expert_rows_combined")
        rows_filled = sem("unused_tiles_filled")

        PAR_LOADS, RAW_LOADS, SMALL_LOADS = 9, 4 + NSEQ, 3
        block = ctx.enter_context(nc.Block())

        @block.sync
        def _(sp):
            sp.dma_start(mem_tok[:], mem[0].rearrange("(m p) n -> p m n", p=P)).then_inc(mem_landed, 16)

            def slot_free(n):
                if n >= RING:
                    last = chunks[n - RING][3]
                    if last is None:
                        i, k = divmod(n - RING - first_merge, 6)
                        u = MERGE_LAST[k]
                        b = 2 + u % 2
                        sp.wait_ge(full[b], merge_base[b] + 8 * i + u // 2 + 1)
                    else:
                        b, use = uses[last]
                        sp.wait_ge(full[b], use + 1)

            def load(n, parts):
                slot_free(n)
                for dst, src in parts:
                    sp.dma_start(dst, src).then_inc(landed[chunks[n][1]], 16)

            n = 0
            for w in (x_wk, x_wv):
                for c in range(4):
                    load(n, [(slot_k8(chunks[n][1]), w1024(w, c))])
                    n += 1

            def columns(g, at, size):
                return win[:, :, g * W + at:g * W + at + size]

            def pair(n, ga, gb, j):
                s = slot_k8(chunks[n][1])
                load(n, [(s[:, :, 0:P], columns(ga, j * P, P)), (s[:, :, P:2 * P], columns(gb, j * P, P))])

            for c in range(2):
                load(n, [(slot_k8(chunks[n][1]), columns(GI, 256 * c, 256))])
                n += 1
            for h in range(KW):
                pair(n, GQ, GF, h)
                n += 1
            for c in range(2):
                load(n, [(slot_k8(chunks[n][1]), columns(GO, 256 * c, 256))])
                n += 1
            for j in range(KW):
                pair(n, GX, GC, j)
                n += 1
            for j in range(KW):
                pair(n, GY, GU, j)
                n += 1
            for c in range(2):
                load(n, [(slot_k8(chunks[n][1]), columns(GV, 256 * c, 256))])
                n += 1
            assert n == first_merge

            def merge_parts(br, k):
                s = (first_merge + k) % RING
                if k % 3 == 0:
                    src = w_branch[0, bass.ds(br, 1), :, (k // 3) * 512:(k // 3) * 512 + 512]
                    return slot_k4(s), src.rearrange("a (k p) n -> p (a k) n", p=P)
                c = (k // 3) * 2 + k % 3 - 1
                return slot_k8(s), win[:, :, bass.ds(GZ * W + br * D + 256 * c, 256)]

            for i in range(PEEL + 1):
                for k in range(6):
                    load(n, [merge_parts(3 - i, k)])
                    n += 1
            with sp.Fori(PEEL + 1, 4) as i:
                for k in range(6):
                    u = MERGE_LAST[k]
                    b = 2 + u % 2
                    loop_wait(sp, full[b], i * 8 + (merge_base[b] - 8 + u // 2 + 1))
                    dst, src = merge_parts(3 - i, k)
                    sp.dma_start(dst, src).then_inc(landed[(first_merge + k) % RING], 16)
            n += 6 * (3 - PEEL)
            for w in (w_out, x_wq, x_wo):
                for c in range(4):
                    load(n, [(slot_k8(chunks[n][1]), w1024(w, c))])
                    n += 1
            assert n == len(chunks)

            def expert_parts(e, u, k):
                s = mring[:, 6 * u + k, :]
                if k < 4:
                    w = (e_wg, e_wu)[k // 2][0, bass.ds(e, 1), :, 256 * (k % 2):256 * (k % 2) + 256]
                    return s.rearrange("p (k n) -> p k n", k=KD), w.rearrange("a (k p) n -> p (a k) n", p=P)
                w = e_wd[0, bass.ds(e, 1), :, 512 * (k - 4):512 * (k - 4) + 512]
                return s.rearrange("p (k n) -> p k n", k=KW), w.rearrange("a (k p) n -> p (a k) n", p=P)

            chunk_bank = (0, 0, 1, 1, 5, 6)
            sp.wait_ge(rt_eid, 1)
            for u in range(2):
                e = sp.value_load(eid[0:1, u:u + 1], min_val=0, max_val=NE - 1)
                if u:
                    sp.wait_ge(xg_landed[0], 16)
                for k in range(6):
                    if u == 0:
                        b, use = uses[chunks[len(chunks) - RING + (k - len(chunks)) % RING][3]]
                        sp.wait_ge(full[b], use + 1)
                    dst, src = expert_parts(e, u, k)
                    sp.dma_start(dst, src).then_inc(mlanded[6 * u + k], 16)
            used = tiles_used(sp)
            with sp.Fori(1, MOE_T // 2) as i:
                for u in range(2):
                    with sp.If(i * 2 + u < used):
                        e = sp.value_load(eid[0:1, bass.ds(i * 2 + u, 1)], min_val=0, max_val=NE - 1)
                        for k in range(6):
                            b = chunk_bank[k]
                            loop_wait(sp, full[b], i * 2 + (moe_base[b] + u - 1))
                            dst, src = expert_parts(e, u, k)
                            sp.dma_start(dst, src).then_inc(mlanded[6 * u + k], 16)

        @block.scalar
        def _(act):
            seen = [0]

            def link(ins):
                seen[0] += 1
                ins.then_inc(act_step, 1)
                act.wait_ge(act_step, seen[0])

            def copy_out(name, dst, cols, rows=P):
                ps, fr = arrived(act, name)
                act.activation(dst, ps[0:rows, cols[0]:cols[1]] if len(dst.shape) == 2 else
                               ps[0:rows, cols[0]:cols[1]].rearrange("p (a b) -> p a b", a=dst.shape[1]),
                               ACT.Copy).then_inc(fr, 1)

            act.dma_start(cst[:], cst_in).then_inc(ld_cst, 16)
            copy_out("par", pc[:, 0:PAR_N], (0, PAR_N))
            copy_out("pst", pst[:], (0, 480))
            ps, fr = arrived(act, "cst")
            for j in range(KW):
                dst = xpad[:, j, 3 + TP:].rearrange("p (b t) -> p b t", b=NSEQ)[:, :, 0:3]
                act.activation(dst, ps[:, 24 * j:24 * j + 24].rearrange("p (b t) -> p b t", b=NSEQ), ACT.Copy)
            act.activation(h0[:], ps[:, 96:128].rearrange("p (a b) -> p a b", a=KW), ACT.Copy).then_inc(fr, 1)
            copy_out("sgw", swT[:], (0, 512))
            copy_out("wbd", sbT[0:TS], (0, 256), TS)
            for k in range(4):
                copy_out(f"memT{k}", memT[:, 2 * k:2 * k + 2, :], (0, 512))
            def deviation(n, rows):
                act.wait_ge(ln_var, n + 1)
                o = 16 * (n % 2)
                act.activation(small[0:rows, o + 15:o + 16], small[0:rows, o + 14:o + 15], ACT.Sqrt).then_inc(ln_std, 1)

            for t in range(NT):
                deviation(t, TILES[t])
            n_ln = NT
            for k in range(8):
                st = k_stage if k < 4 else v_stage
                copy_out(f"kv{k}", st[:, :, 256 * (k % 4):256 * (k % 4) + 256], (0, 512))
            for t in range(NT):
                for s in range(2):
                    copy_out(f"xT{t}{'ab'[s]}", xT[:, 4 * s:4 * s + 4, t * P:t * P + TILES[t]], (0, 4 * TILES[t]))

            def z_out(step):
                _, g, j, half = step
                name = step_units(step)[0]
                ps, fr = arrived(act, name)
                if g in ("i", "v"):
                    rows = TILES[j]
                    if g == "i" and j == 0:
                        act.wait_ge(kv_stored, 32)
                    act.activation((i_tok if g == "i" else v_tok)[0:rows, j, :], ps[0:rows, :], ACT.Copy).then_inc(fr, 1)
                    return
                col = {"u": GU, "yg": GY, "xb": GX, "c": GC, "q": GQ, "f": GF, "go": GO}[g] * KW + j
                b = pc[:, col:col + 1]
                fn = {"yg": ACT.Gelu_apprx_tanh, "q": ACT.Silu, "go": ACT.Silu}.get(g, ACT.Identity)
                at = half * HALF
                if g == "xb":
                    if half == 0:
                        act.activation(xpad[:, j, 3:3 + HALF], ps[:, 0:HALF], fn, bias=b).then_inc(fr, 1)
                    else:
                        act.activation(xpad[:, j, 3 + HALF:3 + TP], ps[:, 0:PH], fn, bias=b)
                        dst = xpad[:, j, 3 + TP:].rearrange("p (b t) -> p b t", b=NSEQ)[:, :, 3:]
                        act.activation(dst, ps[:, PH:HALF].rearrange("p (b t) -> p b t", b=NSEQ), fn, bias=b).then_inc(fr, 1)
                    return
                dst = {"u": ob[:, 0, j], "yg": ob[:, 1, j], "c": ob[:, 2, j], "go": ob[:, 3, j],
                       "q": q_all[:, j], "f": f_all[:, j]}[g]
                act.activation(dst[:, at:at + HALF], ps[:, 0:HALF], fn, bias=b).then_inc(fr, 1)

            def hgrn(what, h):
                if what == "prep":
                    if h:
                        act.wait_ge(hg_done, h)
                    else:
                        act.wait_ge(x0_stored, 16 * NT)
                    f = f_all[:, h]
                    for half in range(2):
                        released(act, f"f{h}_{half}")
                    act.activation(tmp[:, 3], f, ACT.Sigmoid, scale=-1.0)
                    link(act.activation(tmp[:, 1], f, ACT.Abs))
                    link(act.activation(tmp[:, 1], tmp[:, 1], ACT.Exp, scale=-1.0))
                    act.activation(tmp[:, 4], tmp[:, 1], ACT.Ln, bias=small[:, 33:34]).then_inc(hg_ln, 1)
                elif what == "keys":
                    act.wait_ge(hg_b, h + 1)
                    act.activation(tmp[:, 1], tmp[:, 0], ACT.Exp).then_inc(hg_e, 1)
                    act.wait_ge(hg_d, h + 1)
                    act.activation(tmp[:, 4], tmp[:, 4], ACT.Exp).then_inc(hg_k, 1)
                    copy_out(f"kdT{h}", kdT[:, 0:4, :], (0, 512))
                    copy_out(f"kdS{h}", kdT[0:TS, 4, :], (0, P), TS)
                elif what.startswith("lev") and int(what[3:]) < len(LEVELS):
                    n = len(LEVELS) * h + int(what[3:])
                    act.wait_ge(hg_sub, n + 1)
                    size = T if LEVELS[int(what[3:])] <= 4 else TP
                    e = tmp[:, 1 if int(what[3:]) % 2 == 0 else 4, 0:size]
                    act.activation(e, e, ACT.Exp).then_inc(hg_exp, 1)
                elif what == "out":
                    for name, a, b in ((f"OP{h}", 0, TP), (f"OS{h}", TP, T)):
                        ps, fr = arrived(act, name)
                        act.activation(tmp[:, 1, a:b], ps[:, 0:b - a], ACT.Copy)
                        act.activation(tmp[:, 4, a:b], ps[:, 0:b - a], ACT.Square).then_inc(fr, 1)
                elif what == "norm":
                    for name, a, b in ((f"SP{h}", 0, TP), (f"SS{h}", TP, T)):
                        ps, fr = arrived(act, name)
                        act.activation(tmp[:, 4, a:b], ps[:, 0:b - a], ACT.Ln, bias=small[:, 32:33],
                                       scale=1.0 / P).then_inc(fr, 1)
                    released(act, f"SP{h}")
                    released(act, f"SS{h}")
                    act.activation(tmp[:, 4], tmp[:, 4], ACT.Exp, scale=-0.5).then_inc(hg_rs, 1)

            def released(eng, name):
                b, n = uses[name]
                eng.wait_ge(free[b], n + 1)

            def lru(what, j):
                if what == "scan":
                    act.wait_ge(lr_m, j + 1)
                    act.activation(tmp[:, 1], tmp[:, 1], ACT.Sqrt).then_inc(lr_s, 1)
                if what != "sigmoids":
                    return
                if j:
                    act.wait_ge(st_cols, KW + j)
                if j == 0:
                    act.wait_ge(lr_c0, 1)
                    act.activation(small[:, 4:8], small[:, 0:4], ACT.Exp, scale=-1.0).then_inc(lr_y, 1)
                    act.wait_ge(lr_u, 1)
                    act.activation(small[:, 20:24], small[:, 8:12], ACT.Ln).then_inc(lr_l, 1)
                for name, row, dst in ((f"rp{j}", PAR_BR, 1), (f"ip{j}", PAR_BI, 2)):
                    ps, fr = arrived(act, name)
                    act.activation(tmp[:, dst, 0:TP], ps[:, :], ACT.Sigmoid, bias=pc[:, row + j:row + j + 1]).then_inc(fr, 1)
                ps, fr = arrived(act, f"rs{j}")
                act.activation(tmp[:, 1, TP:T], ps[:, 0:TS], ACT.Sigmoid, bias=pc[:, PAR_BR + j:PAR_BR + j + 1])
                act.activation(tmp[:, 2, TP:T], ps[:, TS:2 * TS], ACT.Sigmoid,
                               bias=pc[:, PAR_BI + j:PAR_BI + j + 1]).then_inc(fr, 1)
                for name in (f"rp{j}", f"ip{j}", f"rs{j}"):
                    released(act, name)
                act.wait_ge(lr_c0, 2)
                link(act.activation(tmp[:, 3], tmp[:, 1], ACT.Exp, scale=pc[:, 109 + j:110 + j]))
                act.activation(tmp[:, 1], tmp[:, 1], ACT.Tanh, scale=pc[:, 113 + j:114 + j]).then_inc(lr_a, 1)

            def merge_unit(wait, i, u):
                d = (u // 4) * 2 + (u % 4) // 2
                b = u % 2
                wait(act, full[b], i * 8 + (merge_base[b] + u // 2 + 1))
                wait(act, free[2 + b], i * 8 + (merge_base[2 + b] + u // 2))
                col = i * (-8) + (PAR_BIN + GZ * KW + 8 * 3 + d)
                act.activation(gate[:, b, :], bank[b][:, 0:HALF], ACT.Sigmoid,
                               bias=pc[:, bass.ds(col, 1)]).then_inc(free[b], 1)

            for step in steps:
                if step[0] == "z":
                    z_out(step)
                elif step[0] == "hgrn":
                    hgrn(step[1], step[2])
                elif step[0] == "lru":
                    lru(step[1], step[2])
                elif step[0] == "merge":
                    if step == ("merge", 0, 0):
                        act.wait_ge(hg_done, KW)
                    merge_unit(plain_wait, step[1], step[2])
                elif step == ("sgu", "norm", 0):
                    for t in range(NT):
                        deviation(n_ln, TILES[t])
                        n_ln += 1
                elif step[0] == "states":
                    for k, (name, rows) in enumerate((("oc", 36), ("op", 120), ("oq", 15))):
                        copy_out(name, st_out[0:rows, k, :], (0, 512), rows)
            with act.Fori(PEEL, 4) as i:
                for u in range(16):
                    merge_unit(loop_wait, i, u)

            def layer_out(n_ln, names, dst):
                for t in range(NT):
                    deviation(n_ln + t, TILES[t])
                for t in range(NT):
                    for s in range(2):
                        copy_out(f"{names}{t}{'ab'[s]}", dst[:, 4 * s:4 * s + 4, t * P:t * P + TILES[t]], (0, 4 * TILES[t]))

            layer_out(n_ln, "yT", xT)
            for c in range(4):
                for n in range(4):
                    copy_out(f"q{c}{n}", qT[:, 2 * c + n // 2, (n % 2) * HALF:(n % 2) * HALF + HALF], (0, HALF))

            def keys_turned(item):
                if item < ITEMS and attention_item(item)[3]:
                    for n in range(4):
                        copy_out(f"KT{item}_{n}", kv_t[attention_item(item)[2]][:, 2 * n:2 * n + 2, :], (0, 512))

            keys_turned(0)
            for item in range(ITEMS + 1):
                keys_turned(item + 1)
                if item:
                    rows = attention_item(item - 1)[0]
                    for s in range(2):
                        copy_out(f"PT{item - 1}{'ab'[s]}", pT[(item - 1) % 2][:, 4 * s:4 * s + 4, 0:rows], (0, 4 * rows))
                if item < ITEMS:
                    rows, _, kset, _ = attention_item(item)
                    p, m = prob[item % 2], smx[:, item % 2, :]
                    act.wait_ge(att_max, item + 1)
                    for s in range(2):
                        ps, fr = arrived(act, f"S{item}{'ab'[s]}")
                        for e in range(2):
                            h = 2 * s + e
                            ins = act.activation(p[0:rows, h, :], ps[0:rows, 256 * e:256 * e + 256], ACT.Exp,
                                                 bias=m[0:rows, h:h + 1], scale=XD ** -0.5, accum_out=m[0:rows, 4 + h:5 + h])
                        ins.then_inc(fr, 1)
            layer_out(n_ln + NT, "zT", xT)
            for t in range(NT):
                ps, fr = arrived(act, f"rt{t}")
                if t == 0:
                    act.wait_ge(rt_logit, 1)
                act.activation(rsc[0:TILES[t], 0, NE * t:NE * t + NE], ps[0:TILES[t], 0:NE], ACT.Sigmoid).then_inc(fr, 1)

            def turn_rows(n_expr, u):
                loop_wait(act, full[2], n_expr + (moe_base[2] + 1))
                act.activation(xgT[:, u, 0:4, :], bank[2][:, :].rearrange("p (a b) -> p a b", a=4), ACT.Copy).then_inc(free[2], 1)

            act.wait_ge(full[2], moe_base[2] + 1)
            act.activation(xgT[:, 0, 0:4, :], bank[2][:, :].rearrange("p (a b) -> p a b", a=4), ACT.Copy).then_inc(free[2], 1)
            act.sem_inc(ys_stored[0], 16)
            act.sem_inc(ys_stored[1], 16)
            used = tiles_used(act)
            with act.Fori(0, MOE_T // 2) as i:
                for u in range(2):
                    with act.If(i * 2 + u < used):
                        n = i * 2 + u
                        loop_wait(act, full[0], i * 2 + (moe_base[0] + u + 1))
                        act.activation(hs[:, u, :], bank[0][:, :], ACT.Silu).then_inc(free[0], 1)
                        turn_rows(i * 2 + (u + 1), 1 - u)
                        loop_wait(act, full[4], i * 2 + (moe_base[4] + u + 1))
                        act.activation(hT[:, u], bank[4][:, :].rearrange("p (a b) -> p a b", a=4), ACT.Copy).then_inc(free[4], 1)
                        loop_wait(act, full[5], i * 2 + (moe_base[5] + u + 1))
                        loop_wait(act, ys_stored[u], i * 16 + 16)
                        act.activation(y_out[:, u, 0:512], bank[5][:, :], ACT.Copy).then_inc(free[5], 1)
                        loop_wait(act, free[5], i * 2 + (moe_base[5] + u + 1))
                        loop_wait(act, free[6], i * 2 + (moe_base[6] + u + 1))
                        act.dma_start(ys_d[bass.ds(i * (2 * P) + u * P, P), :], y_out[:, u, :]).then_inc(ys_stored[u], 16)
                    with act.If(i * 2 + u >= used):
                        act.sem_inc(ys_stored[u], 16)
            for t in range(NT):
                deviation(n_ln + 2 * NT + t, TILES[t])

        @block.tensor
        def _(pe):
            ident = cst[:, C_ID:C_ID + P]

            def mm(out, lhsT, rhs, start, stop):
                return pe.matmul(out, lhsT, rhs, start=start, stop=stop)

            def released(name):
                b, n = uses[name]
                pe.wait_ge(free[b], n + 1)

            def arrived_chunk(name):
                slot, value = chunk[name]
                pe.wait_ge(landed[slot], value)
                return slot

            pe.wait_ge(ld_cst, 16)
            pe.wait_ge(zeroed, 3)
            pe.wait_ge(ld_par, PAR_LOADS * 16)
            ps, fu = acquire(pe, "par")
            pe.transpose(ps[:, 0:PAR_N], par[0:PAR_N, :], ident[0:PAR_N, 0:PAR_N]).then_inc(fu, 1)
            pe.wait_ge(ld_raw, 16 * RAW_LOADS)
            ps, fu = acquire(pe, "pst")
            for j in range(KW):
                m = pe.transpose(ps[:, 120 * j:120 * j + 120], raw_pool[0:120, P * j:P * j + P], ident[0:120, 0:120])
            m.then_inc(fu, 1)
            ps, fu = acquire(pe, "cst")
            for j in range(KW):
                pe.transpose(ps[:, 24 * j:24 * j + 24], raw_conv[0:24, P * j:P * j + P], ident[0:24, 0:24])
            for j in range(KW):
                m = pe.transpose(ps[:, 96 + 8 * j:104 + 8 * j], raw_h[0:8, P * j:P * j + P], ident[0:8, 0:8])
            m.then_inc(fu, 1)
            ps, fu = acquire(pe, "sgw")
            for j in range(KW):
                m = pe.transpose(ps[:, P * j:P * j + P], raw_sw[:, j, :], ident)
            m.then_inc(fu, 1)
            ps, fu = acquire(pe, "wbd")
            for j in range(KW):
                m = pe.transpose(ps[0:TS, TS * j:TS * j + TS], raw_sb[0:TS, j, :], ident[0:TS, 0:TS])
            m.then_inc(fu, 1)
            pe.wait_ge(mem_landed, 16)
            for k in range(4):
                ps, fu = acquire(pe, f"memT{k}")
                for e in range(2):
                    for m2 in range(2):
                        c = 2 * k + e
                        m = pe.transpose(ps[:, 256 * e + P * m2:256 * e + P * m2 + P], mem_tok[:, m2, P * c:P * c + P], ident)
                m.then_inc(fu, 1)
            for k in range(4):
                released(f"memT{k}")
            for c in range(8):
                slot = arrived_chunk(f"w{'kv'[c // 4]}{c % 4}")
                ps, fu = acquire(pe, f"kv{c}")
                for m2 in range(2):
                    for k in range(KD):
                        m = mm(ps[:, 256 * m2:256 * m2 + 256], memT[:, k, P * m2:P * m2 + P], slot_k8(slot)[:, k, :],
                               k == 0, k == KD - 1)
                m.then_inc(fu, 1)

            def turn_tokens(name, source, t, ready, value):
                pe.wait_ge(ready, value)
                rows = TILES[t]
                for s in range(2):
                    ps, fu = acquire(pe, f"{name}{t}{'ab'[s]}")
                    for e in range(4):
                        c = 4 * s + e
                        m = pe.transpose(ps[:, rows * e:rows * e + rows], source[0:rows, t, P * c:P * c + P],
                                         ident[0:rows, 0:rows])
                    m.then_inc(fu, 1)

            for t in range(NT):
                turn_tokens("xT", x_tok, t, ln_out, t + 1)
            for t in range(NT):
                released(f"xT{t}a")
                released(f"xT{t}b")

            place_of = {"q": ("qf", 0), "f": ("qf", 1), "xb": ("xc", 0), "c": ("xc", 1), "yg": ("yu", 0), "u": ("yu", 1)}

            def z_mm(step):
                _, g, j, half = step
                ps, fu = acquire(pe, step_units(step)[0])
                if g in ("i", "v"):
                    rows = TILES[j]
                    for c in range(2):
                        slot = arrived_chunk(f"{g}{c}")
                        for k in range(KD):
                            m = mm(ps[0:rows, 256 * c:256 * c + 256], xT[:, k, P * j:P * j + rows],
                                   slot_k8(slot)[:, k, :], k == 0, k == KD - 1)
                    m.then_inc(fu, 1)
                    return
                if g == "go":
                    slot, at = arrived_chunk(f"go{j // 2}"), P * (j % 2)
                else:
                    slot, at = arrived_chunk(f"{place_of[g][0]}{j}"), P * place_of[g][1]
                for k in range(KD):
                    m = mm(ps[:, 0:HALF], slot_k8(slot)[:, k, at:at + P], xT[:, k, half * HALF:half * HALF + HALF],
                           k == 0, k == KD - 1)
                m.then_inc(fu, 1)

            def hgrn(what, h):
                hc = slice(P * h, P * h + P)
                if what == "keys":
                    pe.wait_ge(hg_kd, h + 1)
                    ps, fu = acquire(pe, f"kdT{h}")
                    for c in range(4):
                        m = pe.transpose(ps[:, P * c:P * c + P], tmp[:, 4, P * c:P * c + P], ident)
                    m.then_inc(fu, 1)
                    ps, fu = acquire(pe, f"kdS{h}")
                    pe.transpose(ps[0:TS, 0:P], tmp[:, 4, TP:T], ident).then_inc(fu, 1)
                elif what == "state":
                    released(f"kdT{h}")
                    released(f"kdS{h}")
                    if h == 0:
                        pe.wait_ge(biased, NT)
                    ps, fu = acquire(pe, f"U{h}")
                    for c in range(4):
                        m = mm(ps[:, P * c:P * c + P], kdT[:, c, :], i_tok[:, c, hc], True, True)
                    m.then_inc(fu, 1)
                    for s in range(2):
                        pe.wait_ge(hg_vm, 2 * h + s + 1)
                        ps, fu = acquire(pe, f"US{h}{'ab'[s]}")
                        rhs = vm[0:TS].rearrange("p a b -> p (a b)") if s == 0 else att_m[0:TS, 0:512]
                        mm(ps[:, :], kdT[0:TS, 4, :], rhs, True, True).then_inc(fu, 1)
                elif what == "diag":
                    pe.wait_ge(hg_ln, h + 1)
                    for half in range(2):
                        released(f"q{h}_{half}")
                    level(f"L{h}d", f"M{h}d", tmp[:, 3], q_all[:, h])
                elif what.startswith("lev"):
                    n = int(what[3:]) - 1
                    if 0 <= n < len(LEVELS):
                        pe.wait_ge(hg_x, len(LEVELS) * h + n + 1)
                        x = tmp[:, 2 if n % 2 == 0 else 5]
                        level(f"L{h}{n}", f"M{h}{n}" if LEVELS[n] <= 4 else None, x, x)
                elif what == "out":
                    pe.wait_ge(hg_att, h + 1)
                    released(f"U{h}")
                    qe = f_all[:, h]
                    ps, fu = acquire(pe, f"OP{h}")
                    for c in range(4):
                        o = ps[:, P * c:P * c + P]
                        m = mm(o, i_tok[:, c, hc], att[:, P * c:P * c + P], True, c == 0)
                        if c:
                            m = mm(o, s_pr[:, c - 1, :], qe[:, P * c:P * c + P], False, True)
                    m.then_inc(fu, 1)
                    pe.wait_ge(s0_landed, 16 * (h + 1))
                    ps, fu = acquire(pe, f"OS{h}")
                    mm(ps[:, 0:TS], i_tok[0:TS, 4, hc], att[0:TS, TP:T], True, False)
                    for b in range(NSEQ):
                        m = mm(ps[:, LSEQ * b:LSEQ * b + LSEQ], s_old[:, b, :], qe[:, TP + LSEQ * b:TP + LSEQ * b + LSEQ],
                               False, b == NSEQ - 1)
                    m.then_inc(fu, 1)
                elif what == "norm":
                    released(f"OP{h}")
                    released(f"OS{h}")
                    ones = cst[:, C_ONE:C_ONE + P]
                    ps, fu = acquire(pe, f"SP{h}")
                    mm(ps[:, :], ones, tmp[:, 4, 0:TP], True, True).then_inc(fu, 1)
                    ps, fu = acquire(pe, f"SS{h}")
                    mm(ps[:, 0:TS], ones, tmp[:, 4, TP:T], True, True).then_inc(fu, 1)

            def level(name, sname, left, right):
                ps, fu = acquire(pe, name)
                for c in range(4):
                    m = mm(ps[:, P * c:P * c + P], left[:, P * c:P * c + P], right[:, P * c:P * c + P], True, True)
                m.then_inc(fu, 1)
                if sname:
                    ps, fu = acquire(pe, sname)
                    mm(ps[0:TS, 0:TS], left[:, TP:T], right[:, TP:T], True, True).then_inc(fu, 1)

            def both(weights, x, names):
                ps, fu = acquire(pe, names[0])
                mm(ps[:, :], weights, x[:, 0:TP], True, True).then_inc(fu, 1)
                ps, fu = acquire(pe, names[1])
                mm(ps[:, 0:TS], weights, x[:, TP:T], True, True).then_inc(fu, 1)

            def merge_unit(wait, i, u):
                d, half, gk, pk = (u // 4) * 2 + (u % 4) // 2, u % 2, (1, 2, 4, 5)[u // 4], (0, 3)[u // 8]
                for k in (gk, pk):
                    s = (first_merge + k) % RING
                    wait(pe, landed[s], i * 16 + (chunk[f"merge0_{k}"][1]))
                wait(pe, free[half], i * 8 + (merge_base[half] + u // 2))
                g_w = slot_k8((first_merge + gk) % RING)
                for k in range(KD):
                    m = mm(bank[half][:, 0:HALF], g_w[:, k, P * (d % 2):P * (d % 2) + P],
                           xT[:, k, half * HALF:half * HALF + HALF], k == 0, k == KD - 1)
                m.then_inc(full[half], 1)
                wait(pe, free[2 + half], i * 8 + (merge_base[2 + half] + u // 2))
                p_w = slot_k4((first_merge + pk) % RING)
                for k in range(KW):
                    rhs = ob[:, bass.ds(3 - i, 1), k, half * HALF:half * HALF + HALF].rearrange("p a n -> p (a n)")
                    m = mm(bank[2 + half][:, 0:HALF], p_w[:, k, P * (d % 4):P * (d % 4) + P], rhs, k == 0, k == KW - 1)
                m.then_inc(full[2 + half], 1)

            for step in steps:
                if step[0] == "z":
                    z_mm(step)
                elif step[0] == "hgrn":
                    hgrn(step[1], step[2])
                elif step[0] == "merge":
                    if step[2] == 0:
                        if step[1] == 0:
                            pe.wait_ge(hg_done, KW)
                        else:
                            for j in range(KW):
                                released(f"pp{j}")
                                released(f"ps{j}")
                    merge_unit(plain_wait, step[1], step[2])
                elif step[0] != "states" and step[1] != "product":
                    pass
                elif step[0] == "pool":
                    j = step[2]
                    pe.wait_ge(ld_small, 16 * SMALL_LOADS)
                    pe.wait_ge(pl_d, j + 1)
                    both(wp[:, j, :], ob[:, 2, j], (f"pp{j}", f"ps{j}"))
                elif step[0] == "lru":
                    j = step[2]
                    pe.wait_ge(lr_xc, j + 1)
                    x = conv_out[j % 2]
                    ps, fu = acquire(pe, f"rp{j}")
                    mm(ps[:, :], wr[:, j, :], x[:, 0:TP], True, True).then_inc(fu, 1)
                    ps, fu = acquire(pe, f"ip{j}")
                    mm(ps[:, :], wi[:, j, :], x[:, 0:TP], True, True).then_inc(fu, 1)
                    ps, fu = acquire(pe, f"rs{j}")
                    mm(ps[:, 0:TS], wr[:, j, :], x[:, TP:T], True, True)
                    mm(ps[:, TS:2 * TS], wi[:, j, :], x[:, TP:T], True, True).then_inc(fu, 1)
                elif step[0] == "sgu":
                    j = step[2]
                    pe.wait_ge(v_normed, NT + 2)
                    ps, fu = acquire(pe, f"gp{j}")
                    for c in range(4):
                        m = mm(ps[:, P * c:P * c + P], v_tok[:, c, P * j:P * j + P], swT[:, j, :], True, True)
                    m.then_inc(fu, 1)
                    ps, fu = acquire(pe, f"gs{j}")
                    mm(ps[:, 0:TS], v_tok[0:TS, 4, P * j:P * j + P], sbT[0:TS, j, :], True, True).then_inc(fu, 1)
                elif step[0] == "states":
                    pe.wait_ge(st_cols, KW * 2)
                    for name, src, rows in (("oc", lambda j: att_m[:, 36 * j:36 * j + 36], 36),
                                            ("op", lambda j: att[:, 135 * j + 15:135 * j + 135], 120),
                                            ("oq", lambda j: att[:, 135 * j:135 * j + 15], 15)):
                        ps, fu = acquire(pe, name)
                        for j in range(KW):
                            m = pe.transpose(ps[0:rows, P * j:P * j + P], src(j), ident)
                        m.then_inc(fu, 1)
            pe.wait_ge(sgu_done, KW)
            with pe.Fori(PEEL, 4) as i:
                for u in range(16):
                    merge_unit(loop_wait, i, u)

            def token_major(name, x, w, t):
                rows = TILES[t]
                for s in range(2):
                    ps, fu = acquire(pe, f"{name}{t}{'ab'[s]}")
                    for c in range(2):
                        slot = arrived_chunk(f"{w}{2 * s + c}")
                        for k in range(KD):
                            m = mm(ps[0:rows, 256 * c:256 * c + 256], x[:, k, P * t:P * t + rows], slot_k8(slot)[:, k, :],
                                   k == 0, k == KD - 1)
                    m.then_inc(fu, 1)

            pe.wait_ge(mer_add, 3 * 16)
            for t in range(NT):
                token_major("mix", mer, "wo", t)
            for t in range(NT):
                turn_tokens("yT", x_tok, t, ln_out, NT + t + 1)
            for t in range(NT):
                released(f"yT{t}a")
                released(f"yT{t}b")
            for c in range(4):
                slot = arrived_chunk(f"wq{c}")
                for n in range(4):
                    ps, fu = acquire(pe, f"q{c}{n}")
                    for k in range(KD):
                        m = mm(ps[:, 0:HALF], slot_k8(slot)[:, k, P * (n // 2):P * (n // 2) + P],
                               xT[:, k, (n % 2) * HALF:(n % 2) * HALF + HALF], k == 0, k == KD - 1)
                    m.then_inc(fu, 1)
            k_use, v_use = [0, 0], [0, 0]

            def turn_keys(item):
                if item == ITEMS or not attention_item(item)[3]:
                    return
                kset = attention_item(item)[2]
                k_use[kset] += 1
                pe.wait_ge(k_landed[kset], 16 * k_use[kset])
                for n in range(4):
                    ps, fu = acquire(pe, f"KT{item}_{n}")
                    for e in range(2):
                        for m2 in range(2):
                            c = 2 * n + e
                            m = pe.transpose(ps[:, 256 * e + P * m2:256 * e + P * m2 + P],
                                             kv_k[kset][:, m2, P * c:P * c + P], ident)
                    m.then_inc(fu, 1)

            turn_keys(0)
            for item in range(ITEMS + 1):
                if item < ITEMS:
                    rows, at, kset, fresh = attention_item(item)
                    if fresh:
                        for n in range(4):
                            released(f"KT{item}_{n}")
                    if item == 0:
                        for c in range(4):
                            for n in range(4):
                                released(f"q{c}{n}")
                    for s in range(2):
                        ps, fu = acquire(pe, f"S{item}{'ab'[s]}")
                        for e in range(2):
                            for k in range(2):
                                c = 2 * (2 * s + e) + k
                                m = mm(ps[0:rows, 256 * e:256 * e + 256], qT[:, c, at:at + rows], kv_t[kset][:, c, :],
                                       k == 0, k == 1)
                        m.then_inc(fu, 1)
                    turn_keys(item + 1)
                if item:
                    it = item - 1
                    rows, at, kset, fresh = attention_item(it)
                    if fresh:
                        v_use[kset] += 1
                        pe.wait_ge(v_landed[kset], 16 * v_use[kset])
                    pe.wait_ge(att_prob, it + 1)
                    for s in range(2):
                        ps, fu = acquire(pe, f"PT{it}{'ab'[s]}")
                        for e in range(4):
                            h, m2 = 2 * s + e // 2, e % 2
                            m = pe.transpose(ps[:, rows * e:rows * e + rows], prob[it % 2][0:rows, h, P * m2:P * m2 + P],
                                             ident[0:rows, 0:rows])
                        m.then_inc(fu, 1)
                    released(f"PT{it}a")
                    released(f"PT{it}b")
                    for s in range(2):
                        ps, fu = acquire(pe, f"O{it}{'ab'[s]}")
                        for e in range(4):
                            c = 4 * s + e
                            for m2 in range(2):
                                m = mm(ps[:, rows * e:rows * e + rows], kv_v[kset][:, m2, P * c:P * c + P],
                                       pT[it % 2][:, 2 * (c // 2) + m2, 0:rows], m2 == 0, m2 == 1)
                        m.then_inc(fu, 1)
            for item in range(ITEMS):
                released(f"O{item}a")
                released(f"O{item}b")
            for t in range(NT):
                token_major("att", oT, "wx", t)
            for t in range(NT):
                turn_tokens("zT", x_tok, t, ln_out, 2 * NT + t + 1)
            pe.wait_ge(rt_landed, 16 * 3)
            for t in range(NT):
                released(f"zT{t}a")
                released(f"zT{t}b")
                ps, fu = acquire(pe, f"rt{t}")
                for k in range(KD):
                    m = mm(ps[0:TILES[t], 0:NE], xT[:, k, P * t:P * t + TILES[t]], rw[:, k, :], k == 0, k == KD - 1)
                m.then_inc(fu, 1)
            pe.wait_ge(rt_chosen, 1)
            chosen = rsc[:, 5, :]
            ps, fu = acquire(pe, "pos")
            for t in range(NT):
                for j in range(t + 1):
                    rows = TILES[j]
                    lhs = cst[0:rows, (C_STRI if j == t else C_ONE):(C_STRI if j == t else C_ONE) + TILES[t]]
                    m = mm(ps[0:TILES[t], NE * t:NE * t + NE], lhs, chosen[0:rows, NE * j:NE * j + NE], j == 0, j == t)
            m.then_inc(fu, 1)
            ps, fu = acquire(pe, "cnt")
            for j in range(NT):
                m = mm(ps[:, 0:NE], cst[0:TILES[j], C_ONE:C_ONE + P], chosen[0:TILES[j], NE * j:NE * j + NE],
                       j == 0, j == NT - 1)
            m.then_inc(fu, 1)
            pe.wait_ge(hot_ready, 1)
            ps, fu = acquire(pe, "tab")
            for j in range(2 * NT):
                rows = TILES[j % NT]
                m = mm(ps[:, 0:MOE_T], hot_row[0:rows, j, :], hot_col[0:rows, j, :], j == 0, j == 2 * NT - 1)
            m.then_inc(fu, 1)

            def turn_gathered(u):
                for s in range(2):
                    for e in range(4):
                        c = 4 * s + e
                        m = pe.transpose(bank[2 + s][:, P * e:P * e + P], xg[:, u, P * c:P * c + P], ident)
                    m.then_inc(full[2 + s], 1)

            pe.wait_ge(xg_landed[0], 16)
            pe.wait_ge(free[2], moe_base[2])
            pe.wait_ge(free[3], moe_base[3])
            turn_gathered(0)
            used = tiles_used(pe)
            with pe.Fori(0, MOE_T // 2) as i:
                for u in range(2):
                    with pe.If(i * 2 + u < used):
                        loop_wait(pe, free[2], i * 2 + (moe_base[2] + u + 1))
                        loop_wait(pe, free[3], i * 2 + (moe_base[3] + u + 1))
                        for g in range(2):
                            loop_wait(pe, free[g], i * 2 + (moe_base[g] + u))
                            for c in range(2):
                                k6 = 6 * u + 2 * g + c
                                loop_wait(pe, mlanded[k6], i * 16 + (moe_landed[k6] + 16))
                                w = mring[:, k6, :].rearrange("p (k n) -> p k n", k=KD)
                                for k in range(KD):
                                    m = mm(bank[g][:, 256 * c:256 * c + 256], xgT[:, u, k, :], w[:, k, :], k == 0, k == KD - 1)
                            m.then_inc(full[g], 1)
                        loop_wait(pe, xg_landed[1 - u], i * 16 + (16 + 16 * u))
                        turn_gathered(1 - u)
                        loop_wait(pe, free[1], i * 2 + (moe_base[1] + u + 1))
                        loop_wait(pe, free[4], i * 2 + (moe_base[4] + u))
                        for e in range(4):
                            m = pe.transpose(bank[4][:, P * e:P * e + P], hs[:, u, P * e:P * e + P], ident)
                        m.then_inc(full[4], 1)
                        loop_wait(pe, free[4], i * 2 + (moe_base[4] + u + 1))
                        for s in range(2):
                            k6 = 6 * u + 4 + s
                            loop_wait(pe, free[5 + s], i * 2 + (moe_base[5 + s] + u))
                            loop_wait(pe, mlanded[k6], i * 16 + (moe_landed[k6] + 16))
                            w = mring[:, k6, :].rearrange("p (k n) -> p k n", k=KW)
                            for k in range(KW):
                                m = mm(bank[5 + s][:, :], hT[:, u, k, :], w[:, k, :], k == 0, k == KW - 1)
                            m.then_inc(full[5 + s], 1)

        @block.vector
        def _(dve):
            seen = [0]

            def link(ins):
                seen[0] += 1
                ins.then_inc(dve_step, 1)
                dve.wait_ge(dve_step, seen[0])

            def released(name):
                b, n = uses[name]
                dve.wait_ge(free[b], n + 1)

            n_ln = [0]

            def norm_stats(x, rows):
                o = 16 * (n_ln[0] % 2)
                size = x.shape[-1]
                pieces = size // 512
                for k in range(pieces):
                    ins = dve.bn_stats(small[0:rows, o + 6 * k:o + 6 * k + 6], x[:, 512 * k:512 * k + 512])
                    link(ins)
                link(dve.bn_aggr(small[0:rows, o + 12:o + 14], small[0:rows, o:o + 6 * pieces]))
                dve.tensor_scalar(small[0:rows, o + 14:o + 15], small[0:rows, o + 13:o + 14], LN_EPS, None,
                                  ALU.add).then_inc(ln_var, 1)
                n_ln[0] += 1

            def norm_apply(n, x, g, b, rows, done):
                o = 16 * (n % 2)
                dve.wait_ge(ln_std, n + 1)
                link(dve.reciprocal(small[0:rows, o + 14:o + 15], small[0:rows, o + 15:o + 16]))
                link(dve.tensor_scalar(x, x, small[0:rows, o + 12:o + 13], small[0:rows, o + 14:o + 15],
                                       ALU.subtract, ALU.mult))
                link(dve.tensor_tensor(x, x, g[0:rows], ALU.mult))
                dve.tensor_tensor(x, x, b[0:rows], ALU.add).then_inc(done, 1)

            def norm_tiles(get, g, b, done, before=None):
                first = n_ln[0]
                for t in range(NT + 1):
                    if t < NT:
                        if before:
                            before(t)
                        norm_stats(get(t), TILES[t])
                    if t:
                        norm_apply(first + t - 1, get(t - 1), g, b, TILES[t - 1], done)

            dve.wait_ge(ld_x, 16 * NT)
            dve.wait_ge(ld_rows, 32)
            norm_tiles(lambda t: x_tok[0:TILES[t], t, :], lng, lnb, ln_out)

            def cview(col, rows, shape):
                return cst[0:rows, col:col + shape[1]].unsqueeze(1).to_broadcast([rows, shape[0], shape[1]])

            def hgrn(what, h):
                b, e1, x2, kk, e4, x5 = (tmp[:, n] for n in range(6))
                q, qe, f = q_all[:, h], f_all[:, h], f_all[:, h]
                bs = b[:, TP:T].rearrange("p (a c) -> p a c", c=LSEQ)
                bp = b[:, 0:TP].rearrange("p (a c) -> p a c", c=P)
                if what == "prep":
                    dve.wait_ge(hg_ln, h + 1)
                    link(dve.scalar_tensor_tensor(x2, f, 0.0, e4, ALU.min, ALU.subtract))
                    dve.tensor_tensor_scan(b, cst[:, C_RH:C_RH + T], x2, 0.0, ALU.mult, ALU.add).then_inc(hg_b, 1)
                    dve.wait_ge(hg_b, h + 1)
                elif what == "keys":
                    dve.tensor_tensor(e4[:, 0:TP].rearrange("p (a c) -> p a c", c=P),
                                      bp[:, :, P - 1:P].to_broadcast([P, 4, P]), bp, ALU.subtract)
                    dve.tensor_tensor(e4[:, TP:T].rearrange("p (a c) -> p a c", c=LSEQ),
                                      bs[:, :, LSEQ - 1:LSEQ].to_broadcast([P, NSEQ, LSEQ]), bs,
                                      ALU.subtract).then_inc(hg_d, 1)
                    dve.wait_ge(hg_e, h + 1)
                    for half in range(2):
                        released(f"q{h}_{half}")
                    dve.tensor_tensor(qe, q, e1, ALU.mult)
                    dve.tensor_copy(small[:, 16:20], e1[:, P - 1:TP:P])
                    link(dve.tensor_copy(small[:, 20:28], e1[:, TP + LSEQ - 1:T:LSEQ]))
                    dve.wait_ge(hg_k, h + 1)
                    dve.tensor_tensor(e4, kk, e4, ALU.mult).then_inc(hg_kd, 1)
                elif what == "state":
                    if h == 0:
                        dve.wait_ge(biased, NT)
                    vals = i_tok[0:TS, 4, P * h:P * h + P].unsqueeze(1).to_broadcast([TS, 4, P])
                    for s in range(2):
                        out = vm[0:TS] if s == 0 else att_m[0:TS, 0:512].rearrange("p (a c) -> p a c", c=P)
                        if s == 0 and h:
                            b0, n0 = uses[f"US{h - 1}b"]
                            dve.wait_ge(full[b0], n0 + 1)
                        mask = cst[0:TS, C_BLK + 4 * s:C_BLK + 4 * s + 4].unsqueeze(2).to_broadcast([TS, 4, P])
                        dve.tensor_tensor(out, vals, mask, ALU.mult).then_inc(hg_vm, 1)
                    ps, fr = arrived(dve, f"U{h}")
                    if h:
                        dve.wait_ge(hg_stored, 32 * h)
                    link(dve.tensor_copy(s_pr[:, 0, :], ps[:, 0:P]))
                    for c in range(1, 4):
                        ins = dve.scalar_tensor_tensor(s_pr[:, c, :], s_pr[:, c - 1, :], small[:, 16 + c:17 + c],
                                                       ps[:, P * c:P * c + P], ALU.mult, ALU.add)
                        if c < 3:
                            link(ins)
                    ins.then_inc(fr, 1)
                    dve.wait_ge(s0_landed, 16 * (h + 1))
                    link(dve.tensor_tensor(s_new[:], s_old[:], small[:, 20:28].unsqueeze(2).to_broadcast([P, NSEQ, P]),
                                           ALU.mult))
                    for s in range(2):
                        ps, fr = arrived(dve, f"US{h}{'ab'[s]}")
                        v = s_new[:, 4 * s:4 * s + 4, :]
                        dve.tensor_tensor(v, v, ps[:, :].rearrange("p (a c) -> p a c", c=P), ALU.add).then_inc(fr, 1)
                elif what == "diag":
                    for name, out, shape, rows in ((f"L{h}d", att[:, 0:TP], (4, P), P), (f"M{h}d", att[0:TS, TP:T], (1, TS), TS)):
                        ps, fr = arrived(dve, name)
                        o = out.rearrange("p (a c) -> p a c", c=shape[1])
                        dve.tensor_tensor(o, ps[0:rows, 0:shape[0] * shape[1]].rearrange("p (a c) -> p a c", c=shape[1]),
                                          cview(C_ID, rows, shape), ALU.mult).then_inc(fr, 1)
                        released(name)
                elif what.startswith("lev"):
                    n = int(what[3:])
                    if n < len(LEVELS):
                        step, size = LEVELS[n], (T if LEVELS[n] <= 4 else TP)
                        src = b[:, 0:size].rearrange("p (a u c) -> p a u c", u=2, c=step)
                        dst = (e1 if n % 2 == 0 else e4)[:, 0:size].rearrange("p (a u c) -> p a u c", u=2, c=step)
                        ref = src[:, :, 0, step - 1:step].to_broadcast([P, size // step // 2, step])
                        if n == 1:
                            for k in ("kdT", "kdS"):
                                b1, n1 = uses[f"{k}{h}"]
                                dve.wait_ge(full[b1], n1 + 1)
                        if n >= 2:
                            dve.wait_ge(hg_x, len(LEVELS) * h + n - 1)
                        dve.tensor_tensor(dst[:, :, 1, :], src[:, :, 1, :], ref, ALU.subtract)
                        dve.tensor_tensor(dst[:, :, 0, :], ref, src[:, :, 0, :], ALU.subtract).then_inc(hg_sub, 1)
                    if 1 <= n <= len(LEVELS):
                        l = n - 1
                        step, size = LEVELS[l], (T if LEVELS[l] <= 4 else TP)
                        dve.wait_ge(hg_exp, len(LEVELS) * h + l + 1)
                        if l >= 2:
                            b1, n1 = uses[f"M{h}{l - 2}" if LEVELS[l - 2] <= 4 else f"L{h}{l - 2}"]
                            dve.wait_ge(full[b1], n1 + 1)

                        def cut(t, side):
                            return t[:, 0:size].rearrange("p (a u c) -> p a u c", u=2, c=step)[:, :, side, :]

                        e, x = (e1, e4)[l % 2], (x2, x5)[l % 2]
                        dve.tensor_tensor(cut(x, 1), cut(q, 1), cut(e, 1), ALU.mult)
                        dve.tensor_tensor(cut(x, 0), cut(kk, 0), cut(e, 0), ALU.mult).then_inc(hg_x, 1)
                    if n >= 2:
                        l = n - 2
                        parts = [(f"L{h}{l}", 0, TP, (4, P), P)]
                        if LEVELS[l] <= 4:
                            parts.append((f"M{h}{l}", TP, T, (1, TS), TS))
                        for name, a, z, shape, rows in parts:
                            ps, fr = arrived(dve, name)
                            o = att_m[0:rows, a:z]
                            dve.tensor_tensor(o.rearrange("p (a c) -> p a c", c=shape[1]),
                                              ps[0:rows, 0:z - a].rearrange("p (a c) -> p a c", c=shape[1]),
                                              cview(C_MASK + P * l, rows, shape), ALU.mult).then_inc(fr, 1)
                            released(name)
                            s = att[0:rows, a:z]
                            ins = dve.tensor_tensor(s, s, o, ALU.add)
                            if l == len(LEVELS) - 1 and a:
                                ins.then_inc(hg_att, 1)
                            else:
                                link(ins)
                elif what == "norm":
                    dve.wait_ge(hg_rs, h + 1)
                    for half in range(2):
                        released(f"go{h}_{half}")
                    link(dve.scalar_tensor_tensor(e1, e1, pc[:, PAR_NG:PAR_NG + 1], e4, ALU.mult, ALU.mult))
                    o = ob[:, 3, h, :]
                    dve.tensor_tensor(o, o, e1, ALU.mult).then_inc(hg_done, 1)

            LP, LS = POOL_BUF + TP, POOL_BUF + LSEQ

            def pool(what, j):
                c = cpad[:, j % 2, :]
                o = ob[:, 2, j]
                if what == "out":
                    for name, a, z in ((f"pp{j}", 0, TP), (f"ps{j}", TP, T)):
                        ps, fr = arrived(dve, name)
                        dve.tensor_scalar(o[:, a:z], ps[:, 0:z - a], pc[:, PAR_PB + j:PAR_PB + j + 1],
                                          pc[:, PAR_PS + j:PAR_PS + j + 1], ALU.add, ALU.mult).then_inc(fr, 1)
                if what != "window":
                    return
                dve.wait_ge(pl_pad, j + 1)
                src = c
                for n in range(j + 1):
                    h = 1 << n
                    lo = 2 * h - 1
                    dst = csum[:, n % 2, :]
                    link(dve.tensor_tensor(dst[:, lo:], src[:, lo:], src[:, lo - h:LP + NSEQ * LS - h], ALU.add))
                    src = dst

                def prompt(t):
                    return t[:, POOL_BUF:LP]

                def samples(t):
                    return t[:, LP:].rearrange("p (b t) -> p b t", b=NSEQ)[:, :, POOL_BUF:]

                w = 1.0 / WINDOWS[j]
                link(dve.scalar_tensor_tensor(o[:, 0:TP], prompt(src), w, prompt(c), ALU.mult, ALU.subtract))
                dve.scalar_tensor_tensor(o[:, TP:T].rearrange("p (b t) -> p b t", b=NSEQ), samples(src), w, samples(c),
                                         ALU.mult, ALU.subtract)
                link(dve.tensor_tensor(small[:, 0:16], src[:, POOL_BUF:POOL_BUF + 16],
                                       cst[:, C_RC + 16 * j:C_RC + 16 * j + 16], ALU.mult))
                link(dve.tensor_tensor(o[:, 0:16], small[:, 0:16], c[:, POOL_BUF:POOL_BUF + 16], ALU.subtract))
                dve.tensor_copy(att[:, 135 * j:135 * j + 15], c[:, LP - 15:LP]).then_inc(st_cols, 1)
                dve.tensor_copy(att[:, 135 * j + 15:135 * j + 135].rearrange("p (b t) -> p b t", b=NSEQ),
                                c[:, LP:].rearrange("p (b t) -> p b t", b=NSEQ)[:, :, LSEQ:]).then_inc(pl_d, 1)

            def lru_conv(j):
                x = conv_out[j % 2]
                if j == 0:
                    lam = pc[:, PAR_LAM:PAR_LAM + 4]
                    link(dve.tensor_scalar(small[:, 28:32], lam, -1.0, None, ALU.mult))
                    dve.tensor_tensor(small[:, 0:4], small[:, 28:32], lam, ALU.max).then_inc(lr_c0, 1)
                    dve.wait_ge(lr_y, 1)
                    dve.tensor_scalar(small[:, 8:12], small[:, 4:8], 1.0, None, ALU.add).then_inc(lr_u, 1)
                    dve.wait_ge(lr_u, 1)
                    link(dve.tensor_scalar(small[:, 12:16], small[:, 8:12], -1.0, None, ALU.add))
                    link(dve.tensor_scalar(small[:, 16:20], small[:, 12:16], 0.0, None, ALU.is_equal))
                    link(dve.tensor_tensor(small[:, 12:16], small[:, 12:16], small[:, 16:20], ALU.add))
                    link(dve.reciprocal(small[:, 12:16], small[:, 12:16]))
                    dve.wait_ge(lr_l, 1)
                    link(dve.tensor_tensor(small[:, 20:24], small[:, 20:24], small[:, 16:20], ALU.add))
                    link(dve.tensor_tensor(small[:, 20:24], small[:, 20:24], small[:, 4:8], ALU.mult))
                    link(dve.tensor_tensor(small[:, 20:24], small[:, 20:24], small[:, 12:16], ALU.mult))
                    link(dve.scalar_tensor_tensor(small[:, 20:24], small[:, 28:32], 0.0, small[:, 20:24], ALU.max, ALU.add))
                    dve.tensor_scalar(pc[:, 109:113], small[:, 20:24], -LRU_C, None, ALU.mult)
                    dve.tensor_scalar(pc[:, 113:117], small[:, 20:24], LRU_C, None, ALU.mult).then_inc(lr_c0, 1)
                xs = xpad[:, j, 3 + TP:].rearrange("p (b t) -> p b t", b=NSEQ)
                for half in range(2):
                    released(f"xb{j}_{half}")
                released("cst")
                dve.wait_ge(zeroed, 4)
                dve.wait_ge(pl_d, KW)
                xo = x[:, TP:T].rearrange("p (b t) -> p b t", b=NSEQ)

                def cw(k):
                    return pc[:, PAR_CW + KW * k + j:PAR_CW + KW * k + j + 1]

                cb = pc[:, PAR_CB + j:PAR_CB + j + 1]
                dve.tensor_scalar(x[:, 0:TP], xpad[:, j, 0:TP], cw(0), cb, ALU.mult, ALU.add)
                link(dve.tensor_scalar(xo, xs[:, :, 0:LSEQ], cw(0), cb, ALU.mult, ALU.add))
                for k in range(1, CONV_W):
                    dve.scalar_tensor_tensor(x[:, 0:TP], xpad[:, j, k:k + TP], cw(k), x[:, 0:TP], ALU.mult, ALU.add)
                    ins = dve.scalar_tensor_tensor(xo, xs[:, :, k:k + LSEQ], cw(k), xo, ALU.mult, ALU.add)
                    if k < CONV_W - 1:
                        link(ins)
                ins.then_inc(lr_xc, 1)
                dve.tensor_copy(att_m[:, 36 * j:36 * j + 3], xpad[:, j, TP:TP + 3])
                dve.tensor_copy(att_m[:, 36 * j + 3:36 * j + 27].rearrange("p (b t) -> p b t", b=NSEQ),
                                xs[:, :, LSEQ:LSEQ + 3])

            def lru_gate(j):
                r, g, a, u, hh = (tmp[:, n] for n in range(1, 6))
                dve.wait_ge(lr_xc, j + 1)
                dve.wait_ge(lr_a, j + 1)
                link(dve.tensor_tensor(g, g, conv_out[j % 2], ALU.mult))
                link(dve.tensor_scalar(u, r, 1.0, None, ALU.add))
                link(dve.reciprocal(u, u))
                dve.scalar_tensor_tensor(r, r, 2.0, u, ALU.mult, ALU.mult).then_inc(lr_m, 1)

            def lru_scan(j):
                r, g, a, u, hh = (tmp[:, n] for n in range(1, 6))
                dve.wait_ge(lr_s, j + 1)
                link(dve.tensor_tensor(g, g, r, ALU.mult))
                link(dve.tensor_tensor(small[:, 0:8], a[:, TP:T:LSEQ], h0[:, j, :], ALU.mult))
                dve.tensor_tensor(g[:, TP:T:LSEQ], g[:, TP:T:LSEQ], small[:, 0:8], ALU.add)
                link(dve.tensor_tensor(a, a, cst[:, C_RL:C_RL + T], ALU.mult))
                link(dve.tensor_tensor_scan(hh, a, g, 0.0, ALU.mult, ALU.add))
                dve.tensor_copy(att_m[:, 36 * j + 27:36 * j + 28], hh[:, TP - 1:TP])
                dve.tensor_copy(att_m[:, 36 * j + 28:36 * j + 36], hh[:, TP + LSEQ - 1:T:LSEQ]).then_inc(st_cols, 1)
                for half in range(2):
                    released(f"yg{j}_{half}")
                o = ob[:, 1, j]
                link(dve.tensor_tensor(o, o, hh, ALU.mult))

            def sgu(what, j):
                if what == "norm":
                    dve.wait_ge(biased, 2 * NT)
                    dve.wait_ge(ld_rows, 32 + 48)
                    norm_tiles(lambda t: v_tok[0:TILES[t], t, :], sg_g, sg_b, v_normed)
                    released("sgw")
                    released("wbd")
                    dve.tensor_tensor(swT[:], swT[:], cview(C_TRI, P, (KW, P)), ALU.mult).then_inc(v_normed, 1)
                    dve.tensor_tensor(sbT[0:TS], sbT[0:TS], cview(C_TRI, TS, (KW, TS)), ALU.mult).then_inc(v_normed, 1)
                if what != "out":
                    return
                t0 = tmp[:, 0]
                row = sgu_rows[:, P * j:P * j + P]
                ps, fr = arrived(dve, f"gp{j}")
                dve.tensor_tensor(t0[:, 0:TP].rearrange("p (a c) -> p a c", c=P),
                                  ps[:, :].rearrange("p (a c) -> p a c", c=P),
                                  row.unsqueeze(1).to_broadcast([P, 4, P]), ALU.add).then_inc(fr, 1)
                ps, fr = arrived(dve, f"gs{j}")
                dve.tensor_tensor(t0[:, TP:T].rearrange("p (a c) -> p a c", c=LSEQ),
                                  ps[:, 0:TS].rearrange("p (a c) -> p a c", c=LSEQ),
                                  row[:, 0:LSEQ].unsqueeze(1).to_broadcast([P, NSEQ, LSEQ]), ALU.add).then_inc(fr, 1)
                released(f"gp{j}")
                released(f"gs{j}")
                for half in range(2):
                    released(f"u{j}_{half}")
                dve.tensor_tensor(ob[:, 0, j], ob[:, 0, j], t0, ALU.mult).then_inc(sgu_done, 1)
                dve.wait_ge(sgu_done, j + 1)

            def merge_unit(wait, i, u, first=False, second=False):
                d, half = (u // 4) * 2 + (u % 4) // 2, u % 2
                nb = 2 + half
                wait(dve, full[nb], i * 8 + (merge_base[nb] + u // 2 + 1))
                wait(dve, free[half], i * 8 + (merge_base[half] + u // 2 + 1))
                o = mer[:, d, half * HALF:half * HALF + HALF]
                if first:
                    dve.tensor_tensor(o, gate[:, half, :], bank[nb][:, 0:HALF], ALU.mult).then_inc(free[nb], 1)
                    wait(dve, free[nb], i * 8 + (merge_base[nb] + u // 2 + 1))
                    return
                if not (second and u == 0):
                    wait(dve, mer_add, (i - 1) * 16 + u)
                dve.tensor_tensor(prod[:, half, :], gate[:, half, :], bank[nb][:, 0:HALF], ALU.mult).then_inc(free[nb], 1)
                wait(dve, free[nb], i * 8 + (merge_base[nb] + u // 2 + 1))
                dve.tensor_tensor(o, o, prod[:, half, :], ALU.add).then_inc(mer_add, 1)

            for step in steps:
                if step[0] == "hgrn":
                    hgrn(step[1], step[2])
                elif step[0] == "pool":
                    pool(step[1], step[2])
                elif step[0] == "merge":
                    if step == ("merge", 0, 0):
                        dve.wait_ge(hg_done, KW)
                    merge_unit(plain_wait, step[1], step[2], step[1] == 0, step[1] == 1)
                elif step[0] == "lru" and step[1] in ("conv", "gate", "scan"):
                    {"conv": lru_conv, "gate": lru_gate, "scan": lru_scan}[step[1]](step[2])
                elif step[0] == "sgu":
                    sgu(step[1], step[2])
            with dve.Fori(PEEL, 4) as i:
                for u in range(16):
                    merge_unit(loop_wait, i, u)

            def freed(name, ins):
                b, n = uses[name]
                ins.then_inc(free[b], 1)
                dve.wait_ge(free[b], n + 1)

            def residual(name, t):
                rows = TILES[t]
                for s in range(2):
                    ps, _ = arrived(dve, f"{name}{t}{'ab'[s]}")
                    x = x_tok[0:rows, t, 512 * s:512 * s + 512]
                    freed(f"{name}{t}{'ab'[s]}", dve.scalar_tensor_tensor(x, x, ALPHA, ps[0:rows, :], ALU.mult, ALU.add))

            def tile_of(t):
                return x_tok[0:TILES[t], t, :]

            dve.wait_ge(ld_x, 32 * NT)
            dve.wait_ge(ld_rows, 112)
            dve.wait_ge(rows_filled, 16)
            norm_tiles(tile_of, lng, lnb, ln_out, lambda t: residual("mix", t))
            for item in range(ITEMS + 1):
                if item < ITEMS:
                    rows = attention_item(item)[0]
                    m, p = smx[0:rows, item % 2, :], prob[item % 2][0:rows]
                    for s in range(2):
                        ps, _ = arrived(dve, f"S{item}{'ab'[s]}")
                        link(dve.tensor_reduce(m[:, 2 * s:2 * s + 2], ps[0:rows, :].rearrange("p (a c) -> p a c", a=2), AX, ALU.max))
                    dve.tensor_scalar(m[:, 0:4], m[:, 0:4], -XD ** -0.5, None, ALU.mult).then_inc(att_max, 1)
                if item:
                    r, at, _, _ = attention_item(item - 1)
                    for s in range(2):
                        name = f"O{item - 1}{'ab'[s]}"
                        ps, fr = arrived(dve, name)
                        dve.tensor_copy(oT[:, 4 * s:4 * s + 4, at:at + r],
                                        ps[:, 0:4 * r].rearrange("p (a c) -> p a c", a=4)).then_inc(fr, 1)
                if item < ITEMS:
                    released(f"S{item}a")
                    released(f"S{item}b")
                    link(dve.reciprocal(m[:, 8:12], m[:, 4:8]))
                    dve.tensor_tensor(p, p, m[:, 8:12].unsqueeze(2).to_broadcast([rows, XH, NMEM]), ALU.mult).then_inc(att_prob, 1)
            released(f"PT{ITEMS - 1}a")
            released(f"PT{ITEMS - 1}b")
            dve.wait_ge(att_prob, ITEMS)
            dve.memset(rsc[:], 0.0).then_inc(rt_logit, 1)
            dve.wait_ge(ld_rows, 144)
            norm_tiles(tile_of, lng, lnb, ln_out, lambda t: residual("att", t))

            dve.wait_ge(rt_landed, 16 * 3)
            link(dve.tensor_tensor_scan(places[:], cst[:, C_ONE:C_ONE + P], cst[:, C_ONE:C_ONE + P], -float(P), ALU.mult, ALU.add))
            tile_row = c2[:, C2_TILE:C2_TILE + MOE_T * NE:NE]
            dve.tensor_scalar(tile_starts[:], tile_row, float(P), None, ALU.mult)
            dve.tensor_scalar(tile_numbers[:], tile_row, 1.0, None, ALU.add)
            dve.tensor_copy(tokens[:, 0:NT], c2[:, C2_TOK:C2_TOK + NT])
            link(dve.tensor_copy(tokens[:, NT:], c2[:, C2_TOK:C2_TOK + NT]))
            for t in range(NT):
                released(f"rt{t}")
            names = ("score", "select", "first", "second", "scratch", "chosen", "weight", "combine", "slot", "equal")
            arr = {n: rsc[:, k, :] for k, n in enumerate(names)}
            col = {n: cols[:, k, :] for k, n in enumerate(("m1", "m2", "group", "rest", "gmax", "gbest", "den", "mx", "sum", "wa", "wb"))}

            def by(a, size):
                return a.rearrange("p (a c) -> p a c", c=size)

            def first_max(v, mx, out, rest, n):
                link(dve.tensor_tensor(arr["equal"][:, 0:4 * n].rearrange("p (a c) -> p a c", c=4), v,
                                       mx.unsqueeze(2).to_broadcast([P, n, 4]), ALU.is_equal))
                eq = arr["equal"][:, 0:4 * n].rearrange("p (a c) -> p a c", c=4)
                dve.tensor_copy(out[:, :, 0], eq[:, :, 0])
                link(dve.tensor_scalar(rest, eq[:, :, 0], -1.0, 1.0, ALU.mult, ALU.add))
                for k in range(1, 4):
                    link(dve.tensor_tensor(out[:, :, k], eq[:, :, k], rest, ALU.mult))
                    if k < 3:
                        link(dve.tensor_tensor(rest, rest, out[:, :, k], ALU.subtract))

            sel, fst, snd = by(arr["select"], 4), by(arr["first"], 4), by(arr["second"], 4)
            link(dve.tensor_tensor(by(arr["select"], NE), by(arr["score"], NE), rbias[:].unsqueeze(1).to_broadcast([P, NT, NE]), ALU.add))
            link(dve.tensor_reduce(col["m1"], sel, AX, ALU.max))
            first_max(sel, col["m1"], fst, col["rest"], NT * NG)
            link(dve.scalar_tensor_tensor(arr["scratch"], arr["first"], -1e30, arr["select"], ALU.mult, ALU.add))
            link(dve.tensor_reduce(col["m2"], by(arr["scratch"], 4), AX, ALU.max))
            first_max(by(arr["scratch"], 4), col["m2"], snd, col["rest"], NT * NG)
            link(dve.tensor_tensor(col["group"], col["m1"], col["m2"], ALU.add))
            link(dve.tensor_reduce(col["gmax"][:, 0:NT], by(col["group"], NG), AX, ALU.max))
            first_max(by(col["group"], NG), col["gmax"][:, 0:NT], by(col["gbest"], NG), col["rest"][:, 0:NT], NT)
            link(dve.tensor_tensor(arr["chosen"], arr["first"], arr["second"], ALU.add))
            dve.tensor_tensor(by(arr["chosen"], EPG), by(arr["chosen"], EPG),
                              col["gbest"].unsqueeze(2).to_broadcast([P, NT * NG, EPG]), ALU.mult).then_inc(rt_chosen, 1)
            dve.wait_ge(rt_chosen, 1)
            ps, fr = arrived(dve, "cnt")
            cnt, tiles, ends, starts = (rsc[:, 10, NE * k:NE * k + NE] for k in range(4))
            link(dve.tensor_scalar(tiles, ps[:, 0:NE], 0.0, None, ALU.is_gt))
            for k in range(1, NT):
                ins = dve.scalar_tensor_tensor(tiles, ps[:, 0:NE], float(P * k), tiles, ALU.is_gt, ALU.add)
                if k < NT - 1:
                    link(ins)
            ins.then_inc(fr, 1)
            released("cnt")
            ones = cst[:, C_ONE:C_ONE + NE]
            link(dve.tensor_tensor_scan(ends, ones, tiles, 0.0, ALU.mult, ALU.add))
            link(dve.tensor_tensor(starts, ends, tiles, ALU.subtract))
            link(dve.tensor_scalar(starts, starts, float(P), 1.0, ALU.mult, ALU.add))
            grid = rsc[0:1, 11:17, :].rearrange("p a b -> p (a b)")[:, 0:MOE_T * NE].rearrange("p (a c) -> p a c", c=NE)
            link(dve.tensor_tensor(grid, c2[0:1, C2_TILE:C2_TILE + MOE_T * NE].rearrange("p (a c) -> p a c", c=NE),
                                   ends[0:1].unsqueeze(1).to_broadcast([1, MOE_T, NE]), ALU.is_ge))
            link(dve.tensor_reduce(eidf[0:1, :], grid, AX, ALU.add))
            link(dve.tensor_scalar(eidf[0:1, :], eidf[0:1, :], float(NE - 1), None, ALU.min))
            dve.tensor_copy(used_tiles[0:1, :], ends[0:1, NE - 1:NE])
            dve.tensor_copy(eid[0:1, :], eidf[0:1, :]).then_inc(rt_eid, 1)
            ps, fr = arrived(dve, "pos")
            slot = by(arr["slot"], NE)
            for a, z, rows in ((0, NT - 1, P), (NT - 1, NT, TS)):
                ins = dve.tensor_tensor(slot[0:rows, a:z], by(ps[0:rows, 0:NT * NE], NE)[:, a:z],
                                        starts[0:rows].unsqueeze(1).to_broadcast([rows, z - a, NE]), ALU.add)
                if a == 0:
                    link(ins)
            ins.then_inc(fr, 1)
            released("pos")
            link(dve.tensor_tensor(arr["slot"], arr["slot"], arr["chosen"], ALU.mult))
            link(dve.tensor_reduce(slots[:, 0:NT], slot, AX, ALU.max))
            link(dve.tensor_reduce(slots[:, NT:], slot, AX, ALU.add))
            link(dve.tensor_tensor(slots[:, NT:], slots[:, NT:], slots[:, 0:NT], ALU.subtract))
            per_slot = [P, 2 * NT, MOE_T]
            link(dve.tensor_tensor(hot_col[:], slots[:].unsqueeze(2).to_broadcast(per_slot),
                                   tile_starts[:].unsqueeze(1).to_broadcast(per_slot), ALU.is_gt))
            link(dve.tensor_reduce(slot_tiles[:], hot_col[:], AX, ALU.add))
            link(dve.tensor_tensor(hot_col[:], slot_tiles[:].unsqueeze(2).to_broadcast(per_slot),
                                   tile_numbers[:].unsqueeze(1).to_broadcast(per_slot), ALU.is_equal))
            link(dve.tensor_tensor(hot_col[:], hot_col[:], tokens[:].unsqueeze(2).to_broadcast(per_slot), ALU.mult))
            link(dve.scalar_tensor_tensor(slot_tiles[:], slot_tiles[:], -float(P), slots[:], ALU.mult, ALU.add))
            dve.tensor_tensor(hot_row[:], slot_tiles[:].unsqueeze(2).to_broadcast([P, 2 * NT, P]),
                              places[:].unsqueeze(1).to_broadcast([P, 2 * NT, P]), ALU.is_equal).then_inc(hot_ready, 1)
            ps, fr = arrived(dve, "tab")
            dve.tensor_copy(table[:, 0:MOE_T], ps[:, 0:MOE_T]).then_inc(fr, 1)
            link(dve.tensor_tensor(arr["weight"], arr["score"], arr["chosen"], ALU.mult))
            link(dve.tensor_reduce(col["den"][:, 0:NT], by(arr["weight"], NE), AX, ALU.add))
            link(dve.tensor_scalar(col["den"][:, 0:NT], col["den"][:, 0:NT], 1e-37, None, ALU.max))
            link(dve.reciprocal(col["den"][:, 0:NT], col["den"][:, 0:NT]))
            link(dve.tensor_tensor(by(arr["combine"], NE), by(arr["weight"], NE),
                                   col["den"][:, 0:NT].unsqueeze(2).to_broadcast([P, NT, NE]), ALU.mult))
            link(dve.tensor_tensor(by(arr["equal"], NE), slot, slots[:, 0:NT].unsqueeze(2).to_broadcast([P, NT, NE]), ALU.is_equal))
            link(dve.tensor_tensor(arr["scratch"], arr["equal"], arr["combine"], ALU.mult))
            link(dve.tensor_reduce(col["wa"][:, 0:NT], by(arr["scratch"], NE), AX, ALU.add))
            link(dve.tensor_tensor(arr["scratch"], arr["combine"], arr["scratch"], ALU.subtract))
            link(dve.tensor_reduce(col["wb"][:, 0:NT], by(arr["scratch"], NE), AX, ALU.add))
            link(dve.tensor_scalar(slots[:], slots[:], -1.0, None, ALU.add))
            dve.tensor_copy(ints[:, 0, 0:NT], slots[:, 0:NT])
            dve.tensor_copy(ints[:, 1, 0:NT], slots[:, NT:]).then_inc(rt_slots, 1)

            dve.wait_ge(x2_stored, 16 * NT)
            for t in range(NT):
                link(dve.tensor_scalar(tile_of(t), tile_of(t), ALPHA, None, ALU.mult))

            dve.wait_ge(full[3], moe_base[3] + 1)
            dve.tensor_copy(xgT[:, 0, 4:8, :], bank[3][:, :].rearrange("p (a b) -> p a b", a=4)).then_inc(free[3], 1)
            used = tiles_used(dve)
            with dve.Fori(0, MOE_T // 2) as i:
                for u in range(2):
                    with dve.If(i * 2 + u < used):
                        loop_wait(dve, full[1], i * 2 + (moe_base[1] + u + 1))
                        loop_wait(dve, free[0], i * 2 + (moe_base[0] + u + 1))
                        dve.tensor_tensor(hs[:, u, :], hs[:, u, :], bank[1][:, :], ALU.mult).then_inc(free[1], 1)
                        loop_wait(dve, full[3], i * 2 + (moe_base[3] + u + 2))
                        dve.tensor_copy(xgT[:, 1 - u, 4:8, :], bank[3][:, :].rearrange("p (a b) -> p a b", a=4)).then_inc(free[3], 1)
                        loop_wait(dve, full[6], i * 2 + (moe_base[6] + u + 1))
                        loop_wait(dve, ys_stored[u], i * 16 + 16)
                        dve.tensor_copy(y_out[:, u, 512:1024], bank[6][:, :]).then_inc(free[6], 1)
            dve.wait_ge(ld_rows, 176)

            def combine(t):
                rows = TILES[t]
                x = tile_of(t)
                dve.wait_ge(yab_landed[t % 2], 32 * (t // 2 + 1))
                for y, w in ((ya, "wa"), (yb, "wb")):
                    ins = dve.scalar_tensor_tensor(x, y[0:rows, t % 2, :], col[w][0:rows, t:t + 1], x, ALU.mult, ALU.add)
                    if y is ya:
                        link(ins)
                ins.then_inc(combined, 1)
                dve.wait_ge(combined, t + 1)

            norm_tiles(tile_of, lng, lnb, ln_out, combine)

        @block.gpsimd
        def _(pool):
            def rows_of(ap):
                return ap.unsqueeze(0).broadcast_to([P, ap.shape[0]])

            def load_rows(dst, src, s=None):
                pool.dma_start(dst, rows_of(src)).then_inc(s or ld_rows, 16)

            for t in range(4):
                pool.dma_start(x_tok[:, t, :], x_p[0, P * t:P * t + P, :]).then_inc(ld_x, 16)
            pool.dma_start(x_tok[0:TS, 4, :], x_s.rearrange("b t d -> (b t) d")).then_inc(ld_x, 16)
            load_rows(lng[:], ln_in_g)
            load_rows(lnb[:], ln_in_b)
            pool.memset(raw_sb[0:TS], 0.0).then_inc(zeroed, 1)
            pool.memset(small[:, 32:33], RMS_EPS).then_inc(zeroed, 1)
            pool.memset(small[:, 33:34], 1.0).then_inc(zeroed, 1)
            pool.memset(xpad[:, :, 0:3], 0.0).then_inc(zeroed, 1)
            at = 0
            for src in (b_in_rows, conv_w[0].rearrange("k (c p) -> (k c) p", p=P),
                        *(v.rearrange("a (c p) -> (a c) p", p=P) for v in (conv_b, lru_br, lru_bi, lru_lam, pool_b, pool_s)),
                        norm_g):
                pool.dma_start(par[at:at + src.shape[0], :], src).then_inc(ld_par, 16)
                at += src.shape[0]
            assert at == PAR_N
            pool.dma_start(raw_pool[0:120, :], st_pool[0].rearrange("b t c -> (b t) c")).then_inc(ld_raw, 16)
            pool.dma_start(raw_conv[0:24, :], st_conv[0].rearrange("b t c -> (b t) c")).then_inc(ld_raw, 16)
            pool.dma_start(raw_h[0:8, :], st_h[0]).then_inc(ld_raw, 16)
            pool.dma_start(raw_sw[:], sgu_w[0].rearrange("g t s -> t g s")).then_inc(ld_raw, 16)
            pool.wait_ge(zeroed, 3)
            for b in range(NSEQ):
                pool.dma_start(raw_sb[LSEQ * b:LSEQ * b + LSEQ, :, LSEQ * b:LSEQ * b + LSEQ],
                               sgu_w[0, :, 0:LSEQ, 0:LSEQ].rearrange("g t s -> t g s")).then_inc(ld_raw, 16)
            pool.dma_start(wr[:], lru_wr[0].rearrange("h c d -> c h d")).then_inc(ld_small, 16)
            pool.dma_start(wi[:], lru_wi[0].rearrange("h c d -> c h d")).then_inc(ld_small, 16)
            pool.dma_start(wp[:], pool_w[0].rearrange("h c d -> c h d")).then_inc(ld_small, 16)
            load_rows(bias_i[:], b_in[0, GI * W:GI * W + W], ld_bias)
            load_rows(bias_v[:], b_in[0, GV * W:GV * W + W], ld_bias)
            for t in range(NT):
                pool.wait_ge(ln_out, t + 1)
                pool.dma_start(x0_d[P * t:P * t + TILES[t], :], x_tok[0:TILES[t], t, :]).then_inc(x0_stored, 16)
            for (st, out, k) in ((k_stage, o_mk, 3), (v_stage, o_mv, 7)):
                for c in range(k - 3, k + 1):
                    b, n = uses[f"kv{c}"]
                    pool.wait_ge(free[b], n + 1)
                pool.dma_start(out[0, 0].rearrange("(m p) h d -> p m (h d)", p=P), st[:]).then_inc(kv_stored, 16)

            def released(name):
                b, n = uses[name]
                pool.wait_ge(free[b], n + 1)

            def add_bias(buf, rows, name):
                pool.wait_ge(ld_bias, 32)
                for t in range(NT):
                    released(f"{name}{t}_0")
                    v = buf[0:TILES[t], t, :]
                    pool.tensor_tensor(v, v, rows[0:TILES[t]], ALU.add).then_inc(biased, 1)

            add_bias(i_tok, bias_i, "i")
            for h in range(KW):
                if h:
                    b, n = uses[f"OS{h - 1}"]
                    pool.wait_ge(full[b], n + 1)
                else:
                    pool.wait_ge(ln_out, NT)
                pool.dma_start(s_old[:], st_hg[0, :, h].rearrange("b k v -> k b v")).then_inc(s0_landed, 16)
                released(f"U{h}")
                pool.dma_start(o_hg_p[0, 0, h], s_pr[:, 3, :]).then_inc(hg_stored, 16)
                released(f"US{h}a")
                released(f"US{h}b")
                pool.dma_start(o_hg_s[0, :, h].rearrange("b k v -> k b v"), s_new[:]).then_inc(hg_stored, 16)
            pool.wait_ge(hg_done, KW)
            LP, LS = POOL_BUF + TP, POOL_BUF + LSEQ
            for j in range(KW):
                if j < 2:
                    pool.memset(cpad[:, j, 0:POOL_BUF], 0.0)
                else:
                    pool.wait_ge(pl_d, j - 1)
                for half in range(2):
                    released(f"c{j}_{half}")
                released("pst")
                c = cpad[:, j % 2]
                cs = c[:, LP:].rearrange("p (b t) -> p b t", b=NSEQ)
                pool.tensor_copy(c[:, POOL_BUF:LP], ob[:, 2, j, 0:TP])
                pool.tensor_copy(cs[:, :, 0:POOL_BUF], pst[:, j, :].rearrange("p (b t) -> p b t", b=NSEQ))
                pool.tensor_copy(cs[:, :, POOL_BUF:], ob[:, 2, j, TP:T].rearrange("p (b t) -> p b t", b=NSEQ)).then_inc(pl_pad, 1)
            add_bias(v_tok, bias_v, "v")
            pool.wait_ge(hg_stored, 32 * KW)
            pool.wait_ge(biased, 2 * NT)
            load_rows(sg_g[:], sgu_g[0])
            load_rows(sg_b[:], sgu_b_ln[0])
            load_rows(sgu_rows[:], sgu_b[0].rearrange("g t -> (g t)"))
            pool.wait_ge(v_normed, NT)
            pool.dma_start(o_sgu[0].rearrange("b t c -> (b t) c"), v_tok[0:TS, 4, :]).then_inc(out_stored, 16)
            for name in ("oc", "op", "oq"):
                released(name)
            outs = ((o_conv_p[0, 0], st_out[0:3, 0, :]), (o_conv_s[0].rearrange("b t c -> (b t) c"), st_out[3:27, 0, :]),
                    (o_h_p[0], st_out[27:28, 0, :]), (o_h_s[0], st_out[28:36, 0, :]),
                    (o_pool_s[0].rearrange("b t c -> (b t) c"), st_out[0:120, 1, :]), (o_pool_p[0, 0], st_out[0:15, 2, :]))
            for dst, src in outs:
                pool.dma_start(dst, src).then_inc(out_stored, 16)
            pool.wait_ge(sgu_done, KW)
            pool.wait_ge(v_normed, NT + 2)
            for t in range(NT):
                pool.dma_start(x_tok[0:TILES[t], t, :], x0_d[P * t:P * t + TILES[t], :]).then_inc(ld_x, 16)
            load_rows(lng[:], ln_g[0, 0])
            load_rows(lnb[:], ln_b[0, 0])
            pool.wait_ge(ld_x, 32 * NT)
            spare = MOE_T - MOE_MIN
            pool.dma_start(ys_d[MOE_MIN * P:].rearrange("(t p) n -> p t n", p=P),
                           x_tok[:, 0:1, :].to_broadcast([P, spare, D])).then_inc(rows_filled, 16)
            pool.dma_start(rw[:], rt_w.rearrange("(k p) e -> p k e", p=P)).then_inc(rt_landed, 16)
            pool.wait_ge(kv_stored, 32)
            pool.wait_ge(mer_add, 3 * 16)
            pool.wait_ge(out_stored, 16 * 7)
            loads = [0] + list(range(4, ITEMS))

            def load_memory(n, values):
                item = loads[n]
                kset = attention_item(item)[2]
                if n >= 2:
                    before = loads[n - 2] if n > 2 else 3
                    b, use = uses[f"O{before}b" if values else f"KT{loads[n - 2]}_3"]
                    pool.wait_ge(full[b], use + 1)
                prompt, samples = ((o_mk, ck), (o_mv, cv))[values]
                src = prompt[0, 0] if item == 0 else samples[0, item - 4]
                dst, landed_kv = ((kv_k, k_landed), (kv_v, v_landed))[values]
                pool.dma_start(dst[kset][:], src.rearrange("(m p) h d -> p m (h d)", p=P)).then_inc(landed_kv[kset], 16)

            load_memory(0, 0)
            for n in range(len(loads)):
                if n + 1 < len(loads):
                    load_memory(n + 1, 0)
                load_memory(n, 1)
                if n == 1:
                    pool.wait_ge(ln_out, 2 * NT)
                    load_rows(lng[:], ln_g[0, 1])
                    load_rows(lnb[:], ln_b[0, 1])
            pool.wait_ge(rows_filled, 16)
            pool.wait_ge(rt_logit, 1)
            pool.dma_start(c2[:], cst2_in).then_inc(rt_landed, 16)
            pool.dma_start(rbias[:], rows_of(rt_b)).then_inc(rt_landed, 16)
            pool.memset(table[:, MOE_T:], 0).then_inc(table_rest, 1)
            for t in range(NT):
                pool.wait_ge(ln_out, 2 * NT + t + 1)
                pool.dma_start(x2_d[P * t:P * t + TILES[t], :], x_tok[0:TILES[t], t, :]).then_inc(x2_stored, 16)
            pool.wait_ge(ln_out, 3 * NT)
            load_rows(lng[:], ln_g[0, 2])
            load_rows(lnb[:], ln_b[0, 2])
            released("tab")
            pool.wait_ge(table_rest, 1)
            pool.wait_ge(x2_stored, 16 * NT)

            def gather(index, u):
                return pool.indirect_dma_start(xg[:, u, :], None, x2_d, bass.IndirectOffsetOnAxis(ap=index, axis=0))

            gather(table[:, 0:1], 0).then_inc(xg_landed[0], 16)
            used = tiles_used(pool)
            with pool.Fori(0, MOE_T // 2) as i:
                for u in range(2):
                    with pool.If(i * 2 + u < used):
                        loop_wait(pool, full[3], i * 2 + (moe_base[3] + u))
                        pool.tensor_copy(ints[:, 3 + u, 0:1], table[:, bass.ds(i * 2 + (u + 1), 1)]).then_inc(xg_idx, 1)
                        loop_wait(pool, xg_idx, i * 2 + (u + 1))
                        gather(ints[:, 3 + u, 0:1], 1 - u).then_inc(xg_landed[1 - u], 16)
            for u in range(2):
                pool.wait_ge(ys_stored[u], 16 + 16 * (MOE_T // 2))
            pool.wait_ge(rt_slots, 1)
            for t in range(NT):
                rows = TILES[t]
                if t >= 2:
                    pool.wait_ge(combined, t - 1)
                for k, y in enumerate((ya, yb)):
                    pool.indirect_dma_start(y[0:rows, t % 2, :], None, ys_d,
                                            bass.IndirectOffsetOnAxis(ap=ints[0:rows, k, t:t + 1], axis=0)).then_inc(yab_landed[t % 2], 16)
            for t in range(NT):
                pool.wait_ge(ln_out, 3 * NT + t + 1)
                dst = y_p[0, P * t:P * t + P, :] if t < NT - 1 else y_s.rearrange("b t d -> (b t) d")
                pool.dma_start(dst, x_tok[0:TILES[t], t, :]).then_inc(out_stored, 16)
            pool.wait_ge(out_stored, 16 * (7 + NT))
            pool.wait_ge(hg_stored, 32 * KW)


_INS = ["x_prompt", "x_sample", "mem_prompt", "cache_mem_k", "cache_mem_v", "state_conv", "state_rglru", "state_pool",
        "state_hgrn", "ln_in_g", "ln_in_b", "w_in", "b_in", "sgu_ln_g", "sgu_ln_b", "sgu_w", "sgu_b", "conv_w", "conv_b",
        "lru_wr", "lru_br", "lru_wi", "lru_bi", "lru_lambda", "pool_w", "pool_b", "pool_scale", "hgrn_norm_g",
        "w_branch", "w_out", "x_wq", "x_wk", "x_wv", "x_wo", "ln_g", "ln_b", "router_w", "router_b",
        "e_wg", "e_wu", "e_wd"]
_OUTS = [(1, TP, D), (NSEQ, LSEQ, D), (1, 1, NMEM, XH, XD), (1, 1, NMEM, XH, XD), (1, 1, CONV_W - 1, W), (1, 1, W),
         (1, 1, POOL_BUF, W), (1, 1, KW, P, P), (1, NSEQ, CONV_W - 1, W), (1, NSEQ, W), (1, NSEQ, POOL_BUF, W),
         (1, NSEQ, KW, P, P), (1, NSEQ, LSEQ, W)]


def kernel(**inputs):
    import numpy as _np
    import concourse.bacc as _bacc
    from concourse import mybir as _mybir
    from concourse.bass_utils import run_bass_kernel_spmd as _run

    nc = _bacc.Bacc("TRN2", target_bir_lowering=False, num_devices=1)
    arrays, args = {}, []
    named = [(name, _np.ascontiguousarray(inputs[name])) for name in _INS]
    named += list(zip(("shape_constants_a", "shape_constants_b"), shape_constants()))
    for name, a in named:
        arrays[f"in_{name}_dram"] = a
        args.append(nc.dram_tensor(f"in_{name}_dram", a.shape, _mybir.dt.from_np(a.dtype), kind="ExternalInput").ap())
    for i, shape in enumerate(_OUTS):
        args.append(nc.dram_tensor(f"out_{i}_dram", shape, _mybir.dt.float32, kind="ExternalOutput").ap())
    trunk(nc, *args)
    r = _run(nc, [arrays], core_ids=[0])
    return tuple(r.results[0][f"out_{i}_dram"] for i in range(len(_OUTS)))
```

```python
from contextlib import ExitStack

import numpy as np

import concourse.bass as bass
from concourse import mybir

F32 = mybir.dt.float32
F32R = mybir.dt.float32r
I32 = mybir.dt.int32
ALU = mybir.AluOpType
ACT = mybir.ActivationFunctionType
AX = mybir.AxisListType.X

D = 1024
W = 512
TP = 512
NSEQ, LSEQ = 8, 8
TS = NSEQ * LSEQ
T = TP + TS
P = 128
KD = D // P
KW = W // P
TILES = [P] * (TP // P) + [TS]
NT = len(TILES)
HALF = T // 2
PP = HALF * 2 - TP
PH = HALF - PP
NMEM, XH, XD = 256, 4, 256
NE, NG, EPG, DE = 16, 4, 4, 512
ALPHA = 2.0 ** 0.25
LN_EPS, RMS_EPS = 1e-5, 1e-6
CONV_W, POOL_BUF = 4, 15
WINDOWS = (2, 4, 8, 16)
LRU_C = 8.0
LEVELS = (64, 32, 16, 8, 4, 2, 1)
SLOT = 2048
ITEMS = TP // P + NSEQ
PEEL = 2
MOE_MIN = 2 * T // 128
MOE_T = 24
GU, GV, GY, GX, GC, GQ, GF, GI, GO, GZ = range(10)

PAR_BIN = 0
PAR_CW = 68
PAR_CB = PAR_CW + CONV_W * KW
PAR_BR, PAR_BI, PAR_LAM, PAR_PB, PAR_PS = (PAR_CB + 4 * k for k in range(1, 6))
PAR_NG = PAR_PS + 4
PAR_N = PAR_NG + 1

C_ID, C_ONE, C_TRI, C_STRI, C_MASK = 0, 128, 256, 384, 512
C_RH = C_MASK + 7 * 128
C_RL = C_RH + T
C_BLK = C_RL + T
C_RC = C_BLK + NSEQ
C_N = C_RC + 4 * 16
C2_TILE, C2_TOK = 0, MOE_T * NE
C2_N = C2_TOK + NT


def shape_constants():
    c = np.zeros((P, C_N), np.float32)
    i = np.arange(P)
    s, t = i[:, None], i[None, :]
    c[:, C_ID:C_ID + P] = s == t
    c[:, C_ONE:C_ONE + P] = 1.0
    c[:, C_TRI:C_TRI + P] = s <= t
    c[:, C_STRI:C_STRI + P] = s < t
    for n, h in enumerate(LEVELS):
        c[:, C_MASK + n * P:C_MASK + (n + 1) * P] = (s // (2 * h) == t // (2 * h)) & (s // h % 2 == 0) & (t // h % 2 == 1)
    tok = np.arange(T)
    starts = (tok >= TP) & ((tok - TP) % LSEQ == 0)
    c[:, C_RH:C_RH + T] = ~(starts | ((tok < TP) & (tok % P == 0)))
    c[:, C_RL:C_RL + T] = ~(starts | (tok == 0))
    c[:, C_BLK:C_BLK + NSEQ] = (s // LSEQ == np.arange(NSEQ)[None, :])
    for g, w in enumerate(WINDOWS):
        c[:, C_RC + 16 * g:C_RC + 16 * g + 16] = 1.0 / np.minimum(w, np.arange(16) + 1)
    c2 = np.zeros((P, C2_N), np.float32)
    c2[:, C2_TILE:C2_TILE + MOE_T * NE] = np.repeat(np.arange(MOE_T), NE)[None, :]
    c2[:, C2_TOK:C2_TOK + NT] = s + P * np.arange(NT)[None, :]
    return c, c2


def psum_schedule():
    uses, count = {}, [0] * 8

    def add(name, bank):
        uses[name] = (bank, count[bank])
        count[bank] += 1

    turn = {"low": 0, "high": 0}

    def low(name):
        add(name, turn["low"] % 4)
        turn["low"] += 1

    def high(name):
        add(name, 4 + turn["high"] % 4)
        turn["high"] += 1

    for t in range(NT):
        high(f"xT{t}a")
        high(f"xT{t}b")
    for name in [f"memT{k}" for k in range(4)] + ["par", "pst", "cst", "sgw", "wbd"]:
        high(name)
    merge_base = None
    for step in mixer_steps():
        if step[0] == "merge":
            merge_base = merge_base or list(count)
            add(f"mg{step[1]}_{step[2]}", step[2] % 2)
            add(f"mp{step[1]}_{step[2]}", 2 + step[2] % 2)
        for name in step_units(step):
            (low if step[0] in ("z", "kv") else high)(name)
    for b in range(4):
        count[b] += (4 - PEEL) * 8
    turn["low"] = 0
    for t in range(NT):
        low(f"mix{t}a")
        low(f"mix{t}b")
        high(f"yT{t}a")
        high(f"yT{t}b")
    for c in range(4):
        for n in range(4):
            low(f"q{c}{n}")
    for n in range(4):
        high(f"KT0_{n}")
    for item in range(ITEMS + 1):
        if item < ITEMS:
            low(f"S{item}a")
            low(f"S{item}b")
            if 3 <= item < ITEMS - 1:
                for n in range(4):
                    high(f"KT{item + 1}_{n}")
        if item:
            high(f"PT{item - 1}a")
            high(f"PT{item - 1}b")
            low(f"O{item - 1}a")
            low(f"O{item - 1}b")
    high("OTa")
    high("OTb")
    for t in range(NT):
        low(f"att{t}a")
        low(f"att{t}b")
        high(f"zT{t}a")
        high(f"zT{t}b")
    for t in range(NT):
        high(f"rt{t}")
    high("pos")
    high("cnt")
    high("tab")
    moe_base = list(count)
    return uses, merge_base, moe_base


def z_units():
    out = [("go", h) for h in range(KW)] + [(g, j) for j in range(KW) for g in ("xb", "c")]
    out += [(g, j) for j in range(KW) for g in ("yg", "u")] + [("v", t) for t in range(NT)]
    return out


def mixer_steps():
    steps = [("z", "i", t, 0) for t in range(NT)]
    steps += [("z", g, 0, n) for g in ("q", "f") for n in range(2)]
    rest = [("z", g, j, n) for g, j in z_units() for n in range(1 if g == "v" else 2)]
    for c in range(8):
        rest.insert(4 * c + 2, ("kv", c))
    for h in range(1, KW):
        at = 15 * h - 13
        rest[at:at] = [("z", g, h, n) for g in ("q", "f") for n in range(2)]
    own = [("hgrn", what, h) for h in range(KW) for what in ["prep", "keys", "state", "diag"]
           + [f"lev{n}" for n in range(len(LEVELS) + 2)] + ["out", "norm"]]
    weight = {"prep": 5, "keys": 2, "out": 2, "norm": 3}
    total = sum(weight.get(step[1], 1) for step in own) - weight["norm"]
    count, done = len(rest), 0
    for step in own:
        steps.append(step)
        done += weight.get(step[1], 1)
        while rest and (count - len(rest)) * total < count * done:
            steps.append(rest.pop(0))
    units = [("merge", i, u) for i in range(PEEL) for u in range(16)]

    def merge(count):
        for _ in range(count):
            if units:
                steps.append(units.pop(0))

    for j in range(KW):
        steps.append(("pool", "window", j))
        merge(1)
        steps.append(("pool", "product", j))
        merge(1)
        steps.append(("pool", "out", j))
    steps.append(("lru", "conv", 0))
    merge(1)
    steps += [("lru", "product", 0), ("lru", "sigmoids", 0)]
    for j in range(KW):
        merge(1)
        steps.append(("lru", "gate", j))
        merge(2)
        if j:
            steps.append(("sgu", "norm", 2 * j - 1))
        if j < KW - 1:
            steps.append(("lru", "conv", j + 1))
            merge(1)
            steps.append(("lru", "product", j + 1))
        steps.append(("lru", "scan", j))
        if j < KW - 1:
            steps.append(("sgu", "norm", 2 * j))
        if j < KW - 1:
            steps.append(("lru", "sigmoids", j + 1))
        merge(1)
    merge(1)
    for j in range(KW):
        steps.append(("sgu", "product", j))
        merge(1)
        steps.append(("sgu", "out", j))
    merge(len(units))
    steps.append(("states",))
    return steps


def step_chunks(step):
    if step[0] == "kv":
        return [f"w{'kv'[step[1] // 4]}{step[1] % 4}"]
    g, j = step[1:3]
    pair = {"q": "qf", "f": "qf", "xb": "xc", "c": "xc", "yg": "yu", "u": "yu"}
    return [f"{g}0", f"{g}1"] if g in ("i", "v") else [f"go{j // 2}" if g == "go" else f"{pair[g]}{j}"]


def step_units(step):
    if step[0] == "kv":
        return [f"kv{step[1]}"]
    if step[0] == "z":
        return [f"{step[1]}{step[2]}_{step[3]}"]
    if step[0] == "hgrn":
        what, h = step[1], step[2]
        if what == "keys":
            return [f"kdT{h}", f"kdS{h}"]
        if what == "state":
            return [f"U{h}", f"US{h}a", f"US{h}b"]
        if what == "diag":
            return [f"L{h}d", f"M{h}d"]
        if what.startswith("lev"):
            n = int(what[3:]) - 1
            if 0 <= n < len(LEVELS):
                return [f"L{h}{n}"] + ([f"M{h}{n}"] if LEVELS[n] <= 4 else [])
            return []
        if what == "out":
            return [f"OP{h}", f"OS{h}"]
        if what == "norm":
            return [f"SP{h}", f"SS{h}"]
        return []
    if step[0] == "states":
        return ["oc", "op", "oq"]
    if step[1] != "product":
        return []
    return [f"{name}{step[2]}" for name in {"pool": ("pp", "ps"), "lru": ("rp", "ip", "rs"), "sgu": ("gp", "gs")}[step[0]]]


def weight_plan():
    first, last = [], {}
    for step in mixer_steps():
        if step[0] in ("z", "kv"):
            for name in step_chunks(step):
                if name not in last:
                    first.append(name)
                last[name] = step_units(step)[0]
    plan = [(name, 2 if name[:2] in ("qf", "xc", "yu") else 1, last[name]) for name in first]
    before = len(plan)
    plan += [(f"wo{c}", 1, f"mix{NT - 1}{'ab'[c // 2]}") for c in range(4)]
    plan += [(f"wq{c}", 1, f"q{c}3") for c in range(4)]
    plan += [(f"wx{c}", 1, f"att{NT - 1}{'ab'[c // 2]}") for c in range(4)]
    landed, out = [0] * RING, []
    for n, (name, dmas, last) in enumerate(plan):
        landed[n % RING] += 16 * dmas
        out.append((name, n % RING, landed[n % RING], last))
    return out, before, landed


RING = 6


def trunk(nc, x_p, x_s, mem, ck, cv, st_conv, st_h, st_pool, st_hg, ln_in_g, ln_in_b, w_in, b_in, sgu_g, sgu_b_ln,
          sgu_w, sgu_b, conv_w, conv_b, lru_wr, lru_br, lru_wi, lru_bi, lru_lam, pool_w, pool_b, pool_s, norm_g,
          w_branch, w_out, x_wq, x_wk, x_wv, x_wo, ln_g, ln_b, rt_w, rt_b, e_wg, e_wu, e_wd, cst_in, cst2_in,
          y_p, y_s, o_mk, o_mv, o_conv_p, o_h_p, o_pool_p, o_hg_p, o_conv_s, o_h_s, o_pool_s, o_hg_s, o_sgu):
    uses, merge_base, moe_base = psum_schedule()
    steps = mixer_steps()
    chunks, first_merge, landed_all = weight_plan()
    moe_landed = landed_all + [0] * RING
    chunk = {name: (slot, value) for name, slot, value, _ in chunks}

    x0_d = nc.dram_tensor("x0_scratch", (T, D), F32, kind="Internal").ap()
    x2_d = nc.dram_tensor("x2_scratch", (T, D), F32, kind="Internal").ap()
    ys_d = nc.dram_tensor("expert_rows", (MOE_T * P, D), F32, kind="Internal").ap()

    with ExitStack() as ctx:
        base = 16512

        def place(name, at, shape, dtype=F32):
            size = int(np.prod(shape[1:]))
            assert base + 4 * (at + size) <= 229344, name
            return nc.alloc_sbuf_tensor_at(name, shape, dtype, offset=base + 4 * at, align_bytes=4)

        def sem(name):
            return ctx.enter_context(nc.semaphore(name))

        ring = place("ring", 0, [P, RING, SLOT])
        xT = place("xT", 12288, [P, KD, T])
        x_hi = place("x_hi", 7680, [P, KD, T], F32R)
        x_lo = place("x_lo", 12288, [P, KD, T], F32R)
        g_raw = [place(f"gate_weights{b}", 2048 * b, [P, KD, P]) for b in range(2)]
        g_lo = [place(f"gate_weights_lo{b}", 2048 * b, [P, KD, P], F32R) for b in range(2)]
        g_hi = [place(f"gate_weights_hi{b}", 2048 * b + 1024, [P, KD, P], F32R) for b in range(2)]
        p_raw = [place(f"branch_weights{b}", 6144 + 512 * b, [P, KW, P]) for b in range(2)]
        ob = place("ob", 16896, [P, 4, KW, T])
        mer = place("mer", 26112, [P, KD, T])
        q_all = place("q_all", 26112, [P, KW, T])
        f_all = place("f_all", 28416, [P, KW, T])
        v_tok = place("v_tok", 30720, [P, NT, W])
        i_tok = place("i_tok", 33280, [P, NT, W])
        lng = place("lng", 35840, [P, D])
        lnb = place("lnb", 36864, [P, D])
        s_old = place("s_old", 35840, [P, NSEQ, P])
        s_new = place("s_new", 36864, [P, NSEQ, P])
        cst = place("cst", 37888, [P, C_N])
        pc = place("pc", 40520, [P, 120])
        wr = place("wr", 40640, [P, KW, P])
        wi = place("wi", 41152, [P, KW, P])
        wp = place("wp", 41664, [P, KW, P])
        swT = place("swT", 42176, [P, KW, P])
        sbT = place("sbT", 42688, [P, KW, TS])
        x_tok = place("x_tok", 42944, [P, NT, D])
        tmp = place("tmp", 42944, [P, 6, T])
        att = place("att", 46400, [P, T])
        att_m = place("att_m", 46976, [P, T])
        kdT = place("kdT", 47552, [P, 5, P])
        conv_out = [tmp[:, 0], place("conv_odd", 47552, [P, T])[:]]
        s_pr = place("s_pr", 48192, [P, 4, P])
        xpad = place("xpad", 48704, [P, KW, 3 + TP + NSEQ * (3 + LSEQ)])
        bias_i = place("bias_i", 51116, [P, W])
        bias_v = place("bias_v", 51628, [P, W])
        vm = place("vm", 52140, [P, 4, P])
        pst = place("pst", 52652, [P, KW, NSEQ * POOL_BUF])
        h0 = place("h0", 53132, [P, KW, NSEQ])
        mem_tok = place("mem_tok", 16896, [P, 2, D])
        memT = place("memT", 18944, [P, KD, NMEM])
        par = place("par", 20992, [P, P])
        raw_pool = place("raw_pool", 21120, [P, W])
        raw_conv = place("raw_conv", 21632, [P, W])
        raw_h = place("raw_h", 22144, [P, W])
        raw_sw = place("raw_sw", 22656, [P, KW, P])
        raw_sb = place("raw_sb", 23168, [P, KW, TS])
        kv_stage = place("kv_stage", 16896, [P, 4, 2, NMEM])
        small = place("small", 53164, [P, 44])
        st_out = place("st_out", 30720, [P, 3, W])
        cpad = place("cpad", 42944, [P, 2, POOL_BUF + TP + NSEQ * (POOL_BUF + LSEQ)])
        csum = place("csum", 42944 + 1422, [P, 2, POOL_BUF + TP + NSEQ * (POOL_BUF + LSEQ)])
        sgu_rows = place("sgu_rows", 51116, [P, W])
        sg_g = place("sg_g", 35840, [P, W])
        sg_b = place("sg_b", 36352, [P, W])
        gate = place("gate", 33280, [P, 2, HALF])
        prod = place("prod", 33856, [P, 2, HALF])
        qT = place("qT", 26112, [P, KD, T])
        oT = place("oT", 48064, [P, KD, T])
        kv_k = [place("kv_k0", 16896, [P, 2, D]), place("kv_k1", 23040, [P, 2, D])]
        kv_t = [place("kv_t0", 18944, [P, KD, NMEM]), place("kv_t1", 30720, [P, KD, NMEM])]
        kv_v = [place("kv_v0", 20992, [P, 2, D]), place("kv_v1", 32768, [P, 2, D])]
        prob = [place("prob0", 40640, [P, XH, NMEM]), place("prob1", 41664, [P, XH, NMEM])]
        o_rows = place("o_rows", 12288, [P, 2, D])
        o_all = place("o_all", 14336, [P, D])
        pT = [place("pT0", 34816, [P, KD, P]), place("pT1", 25088, [P, KD, P])]
        smx = place("smx", 42688, [P, 2, 12])
        rw = place("rw", 52672, [P, KD, NE])
        NRING = 12
        mring = place("mring", 0, [P, NRING, SLOT])
        xg = place("xg", 24576, [P, 2, D])
        xgT = place("xgT", 26624, [P, 2, KD, P])
        hs = place("hs", 28672, [P, 2, DE])
        hT = place("hT", 29696, [P, 2, 4, P])
        y_out = place("y_out", 30720, [P, 2, D])
        ya = place("ya", 0, [P, NT, D])
        yb = place("yb", 5120, [P, NT, D])
        rsc = place("rsc", 40640, [P, 17, NT * NE])
        c2 = place("c2", 42000, [P, C2_N])
        rbias = place("rbias", 42400, [P, NE])
        cols = place("cols", 42424, [P, 12, 20])
        ints = place("ints", 42664, [P, 5, 8], I32)
        eid = place("eid", 42704, [P, MOE_T], I32)
        eidf = place("eidf", 42728, [P, MOE_T])
        used_tiles = place("used_tiles", 42816, [P, 1], I32)
        table = place("table", 42752, [P, MOE_T + 2], I32)
        hot_row = place("hot_row", 30720, [P, 2 * NT, P])
        hot_col = place("hot_col", 32000, [P, 2 * NT, MOE_T])
        places = place("places", 32240, [P, P])
        tile_starts = place("tile_starts", 32368, [P, MOE_T])
        tile_numbers = place("tile_numbers", 32392, [P, MOE_T])
        slots = place("slots", 32416, [P, 2 * NT])
        slot_tiles = place("slot_tiles", 32432, [P, 2 * NT])
        tokens = place("tokens", 32448, [P, 2 * NT])

        bank = [ctx.enter_context(nc.psum_tensor(f"bank{b}", [P, 512], F32)) for b in range(8)]
        full = [sem(f"bank{b}_full") for b in range(8)]
        free = [sem(f"bank{b}_free") for b in range(8)]
        passed = sem("loop_wait_passed")
        landed = [sem(f"ring{k}_landed") for k in range(RING)]

        def acquire(eng, name):
            b, n = uses[name]
            if n:
                eng.wait_ge(free[b], n)
            return bank[b], full[b]

        def loop_wait(eng, semaphore, value):
            eng.wait_ge(semaphore, value)
            eng.sem_inc(passed, 1)

        def split_before(i, u):
            if u == 0 and not (isinstance(i, int) and 0 < i < PEEL):
                return i, 0
            if u % 2 and u < 15:
                return i, u // 2 + 1
            if u == 15 and isinstance(i, int) and i + 1 < PEEL:
                return i + 1, 0
            return None

        def plain_wait(eng, semaphore, value):
            eng.wait_ge(semaphore, value)

        def tiles_used(eng):
            eng.wait_ge(rt_eid, 1)
            return eng.value_load(used_tiles[0:1, 0:1], min_val=0, max_val=MOE_T)

        def attention_item(item):
            if item < TP // P:
                return P, P * item, 0, item == 0
            b = item - TP // P
            return LSEQ, TP + LSEQ * b, (1 + b) % 2, True

        def arrived(eng, name):
            b, n = uses[name]
            eng.wait_ge(full[b], n + 1)
            return bank[b], free[b]

        ld_x, ld_rows, ld_cst, ld_par, ld_raw, ld_small, ld_bias = (
            sem("x_landed"), sem("norm_rows_landed"), sem("constants_landed"), sem("params_landed"),
            sem("raw_states_landed"), sem("mixer_weights_landed"), sem("bias_rows_landed"))
        ld_masks = sem("masks_landed")
        x_in = [sem(f"x{t}_landed") for t in range(NT)]
        zeroed, mem_landed, s0_landed = sem("zeroed"), sem("memory_landed"), sem("hgrn_state_landed")
        dve_step, act_step, pool_step = sem("vector_step"), sem("scalar_step"), sem("gpsimd_step")
        ln_var, ln_std, ln_out = sem("norm_variance"), sem("norm_deviation"), sem("norm_written")
        x0_stored, out_stored = sem("x0_stored"), sem("outputs_stored")
        kv_stored = [sem(f"memory_stage{k}_stored") for k in range(4)]
        biased = sem("token_major_biased")
        hg_ln, hg_b, hg_e, hg_d, hg_k, hg_kd = (sem("hgrn_log"), sem("hgrn_cumulated"), sem("hgrn_decay"),
                                                sem("hgrn_tail_log"), sem("hgrn_tail"), sem("hgrn_keys"))
        hg_vm, hg_sub, hg_exp, hg_x, hg_att, hg_rs, hg_done = (
            sem("hgrn_values_masked"), sem("hgrn_level_log"), sem("hgrn_level_decay"), sem("hgrn_level_scaled"),
            sem("hgrn_scores"), sem("hgrn_rms"), sem("hgrn_head_done"))
        hg_snew, hg_stored = sem("hgrn_states_new"), sem("hgrn_states_stored")
        pl_pad, pl_d = sem("pool_padded"), sem("pool_differences")
        lr_c0, lr_y, lr_u, lr_l = sem("lru_abs"), sem("lru_exp"), sem("lru_one_plus"), sem("lru_ln")
        lr_xc, lr_a, lr_m, lr_s, lr_done = (sem("lru_conv"), sem("lru_decay"), sem("lru_square"), sem("lru_root"),
                                            sem("lru_head_done"))
        v_normed, st_cols, sgu_done = sem("spatial_values_normed"), sem("state_columns"), sem("sgu_done")
        mer_add = sem("merge_added")
        g_landed, p_landed = ([sem(f"{x}_weights{b}_landed") for b in range(2)] for x in ("gate", "branch"))
        x_hi_done, x_lo_done, g_hi_done, g_lo_done = (sem("x_hi"), sem("x_lo"), sem("gate_weights_hi"), sem("gate_weights_lo"))

        b_in_rows = b_in.rearrange("a (c p) -> (a c) p", p=P)
        win = w_in.rearrange("a (k p) n -> p (a k) n", p=P)

        def w1024(w, c):
            return w[0].rearrange("(k p) n -> p k n", p=P)[:, :, 256 * c:256 * c + 256]

        def slot_k8(k):
            return ring[:, k, :].rearrange("p (k n) -> p k n", k=KD)

        def xp_prompt(t, j, at):
            return t[:, j, at:at + TP]

        table_rest = sem("table_past_tiles_zeroed")
        k_landed, v_landed = ([sem(f"memory_{x}{n}_landed") for n in range(2)] for x in ("keys", "values"))
        att_max, att_prob = sem("scores_max"), sem("probabilities")
        x2_stored, rt_landed, rt_logit, rt_chosen, rt_slots, rt_eid = (
            sem("x2_stored"), sem("router_inputs_landed"), sem("router_scores"), sem("experts_chosen"),
            sem("slots_written"), sem("tile_experts"))
        hot_ready, xg_idx, xg_landed = sem("slot_table_one_hots"), sem("gather_index"), [sem("rows0_gathered"), sem("rows1_gathered")]
        ys_stored, yab_landed = [sem("expert_rows0_stored"), sem("expert_rows1_stored")], [sem(f"pair{t}_gathered") for t in range(NT)]
        landed_hi = [sem(f"ring{k}_landed") for k in range(RING, 2 * RING)]
        mlanded = landed + landed_hi
        last_mean, last_normed, last_gain = sem("last_norm_offset"), sem("last_norm_applied"), sem("last_norm_gain")
        last_written, y_stored = [sem("last_norm_by_pool"), sem("last_norm_by_vector")], sem("y_stored")
        o_moved = [sem(f"sample_rows{k}_moved") for k in range(2)]
        rows_filled = sem("unused_tiles_filled")

        PAR_LOADS, RAW_LOADS, SMALL_LOADS = 9, 4 + NSEQ, 3
        block = ctx.enter_context(nc.Block())

        @block.sync
        def _(sp):
            for t in range(NT):
                src = x_p[0, P * t:P * t + P, :] if t < NT - 1 else x_s.rearrange("b t d -> (b t) d")
                sp.dma_start(x_tok[0:TILES[t], t, :], src).then_inc(x_in[t], 16)

            def slot_free(n):
                if n >= RING:
                    last = chunks[n - RING][3]
                    b, use = uses[last]
                    sp.wait_ge(full[b], use + 1)

            def load(n, parts):
                slot_free(n)
                for dst, src in parts:
                    sp.dma_start(dst, src).then_inc(landed[chunks[n][1]], 16)

            def columns(g, at, size):
                return win[:, :, g * W + at:g * W + at + size]

            pairs = {"qf": (GQ, GF), "xc": (GX, GC), "yu": (GY, GU)}
            for n in range(first_merge):
                name, slot = chunks[n][0], slot_k8(chunks[n][1])
                kind, c = name[:-1], int(name[-1])
                if kind in pairs:
                    ga, gb = pairs[kind]
                    load(n, [(slot[:, :, 0:P], columns(ga, c * P, P)), (slot[:, :, P:2 * P], columns(gb, c * P, P))])
                elif kind in ("wk", "wv"):
                    load(n, [(slot, w1024(x_wk if kind == "wk" else x_wv, c))])
                else:
                    load(n, [(slot, columns({"i": GI, "go": GO, "v": GV}[kind], 256 * c, 256))])
                if n == 2:
                    sp.dma_start(cst[:, C_ID + P:], cst_in[:, C_ID + P:]).then_inc(ld_masks, 16)
                    sp.dma_start(mem_tok[:], mem[0].rearrange("(m p) n -> p m n", p=P)).then_inc(mem_landed, 16)
            def merge_load(wait, i, d):
                if isinstance(i, int) and 8 * i + d < 2:
                    b, use = uses[f"v{NT - 1}_0"]
                    wait(sp, full[b], use + 1)
                else:
                    wait(sp, full[1], i * 8 + (merge_base[1] + d - 1))
                sp.dma_start(g_raw[d % 2][:], win[:, :, bass.ds((3 - i) * D + (GZ * W + P * d), P)]).then_inc(g_landed[d % 2], 16)
                if not (isinstance(i, int) and 8 * i + d < 2):
                    wait(sp, full[3], i * 8 + (merge_base[3] + d - 1))
                src = w_branch[0, bass.ds(3 - i, 1), :, P * d:P * d + P].rearrange("a (k p) n -> p (a k) n", p=P)
                sp.dma_start(p_raw[d % 2][:], src).then_inc(p_landed[d % 2], 16)

            load(first_merge, [(slot_k8(chunks[first_merge][1]), w1024(w_out, 0))])
            for i in range(PEEL):
                for d in range(KD):
                    merge_load(plain_wait, i, d)
            with sp.Fori(PEEL, 4) as i:
                for d in range(KD):
                    merge_load(loop_wait, i, d)
            sp.wait_ge(full[3], merge_base[3] + 4 * KD)
            n = first_merge + 1
            for w in (w_out, x_wq, x_wo):
                for c in range(1 if w is w_out else 0, 4):
                    load(n, [(slot_k8(chunks[n][1]), w1024(w, c))])
                    n += 1
            assert n == len(chunks)

            for item in range(TP // P, ITEMS):
                for s in "ab":
                    b, use = uses[f"O{item}{s}"]
                    sp.wait_ge(free[b], use + 1)
                at = LSEQ * (item - TP // P)
                sp.dma_start(o_all[at:at + LSEQ, :], o_rows[0:LSEQ, item % 2, :]).then_inc(o_moved[item % 2], 16)

            def expert_parts(e, u, k):
                s = mring[:, 6 * u + k, :]
                if k < 4:
                    w = (e_wg, e_wu)[k // 2][0, bass.ds(e, 1), :, 256 * (k % 2):256 * (k % 2) + 256]
                    return s.rearrange("p (k n) -> p k n", k=KD), w.rearrange("a (k p) n -> p (a k) n", p=P)
                w = e_wd[0, bass.ds(e, 1), :, 512 * (k - 4):512 * (k - 4) + 512]
                return s.rearrange("p (k n) -> p k n", k=KW), w.rearrange("a (k p) n -> p (a k) n", p=P)

            chunk_bank = (0, 0, 1, 1, 5, 6)
            sp.wait_ge(rt_eid, 1)
            for u in range(2):
                e = sp.value_load(eid[0:1, u:u + 1], min_val=0, max_val=NE - 1)
                if u:
                    sp.wait_ge(xg_landed[0], 16)
                for k in range(6):
                    if u == 0:
                        b, use = uses[chunks[len(chunks) - RING + (k - len(chunks)) % RING][3]]
                        sp.wait_ge(full[b], use + 1)
                    dst, src = expert_parts(e, u, k)
                    sp.dma_start(dst, src).then_inc(mlanded[6 * u + k], 16)
            used = tiles_used(sp)
            with sp.Fori(1, MOE_T // 2) as i:
                for u in range(2):
                    with sp.If(i * 2 + u < used):
                        e = sp.value_load(eid[0:1, bass.ds(i * 2 + u, 1)], min_val=0, max_val=NE - 1)
                        for k in range(6):
                            b = chunk_bank[k]
                            loop_wait(sp, full[b], i * 2 + (moe_base[b] + u - 1))
                            dst, src = expert_parts(e, u, k)
                            sp.dma_start(dst, src).then_inc(mlanded[6 * u + k], 16)

            for t in range(NT):
                if t < NT - 1:
                    sp.wait_ge(last_written[0], t + 1)
                else:
                    sp.wait_ge(last_written[1], 1)
                dst = y_p[0, P * t:P * t + P, :] if t < NT - 1 else y_s.rearrange("b t d -> (b t) d")
                sp.dma_start(dst, x_tok[0:TILES[t], t, :]).then_inc(y_stored, 16)
            sp.wait_ge(y_stored, 16 * NT)

        @block.scalar
        def _(act):
            seen = [0]

            def link(ins):
                seen[0] += 1
                ins.then_inc(act_step, 1)
                act.wait_ge(act_step, seen[0])

            def copy_out(name, dst, cols, rows=P):
                ps, fr = arrived(act, name)
                act.activation(dst, ps[0:rows, cols[0]:cols[1]] if len(dst.shape) == 2 else
                               ps[0:rows, cols[0]:cols[1]].rearrange("p (a b) -> p a b", a=dst.shape[1]),
                               ACT.Copy).then_inc(fr, 1)

            act.dma_start(cst[:, C_ID:C_ID + P], cst_in[:, C_ID:C_ID + P]).then_inc(ld_cst, 16)
            def deviation(n, rows):
                act.wait_ge(ln_var, n + 1)
                o = 16 * (n % 2)
                act.activation(small[0:rows, o + 15:o + 16], small[0:rows, o + 14:o + 15], ACT.Sqrt).then_inc(ln_std, 1)

            n_ln = NT
            def z_out(step):
                _, g, j, half = step
                name = step_units(step)[0]
                ps, fr = arrived(act, name)
                if g in ("i", "v"):
                    rows = TILES[j]
                    act.activation((i_tok if g == "i" else v_tok)[0:rows, j, :], ps[0:rows, :], ACT.Copy).then_inc(fr, 1)
                    return
                col = {"u": GU, "yg": GY, "xb": GX, "c": GC, "q": GQ, "f": GF, "go": GO}[g] * KW + j
                b = pc[:, col:col + 1]
                fn = {"yg": ACT.Gelu_apprx_tanh, "q": ACT.Silu, "go": ACT.Silu}.get(g, ACT.Identity)
                at = half * HALF
                if g == "xb":
                    if half == 0:
                        act.activation(xpad[:, j, 3:3 + HALF], ps[:, 0:HALF], fn, bias=b).then_inc(fr, 1)
                    else:
                        act.activation(xpad[:, j, 3 + HALF:3 + TP], ps[:, 0:PH], fn, bias=b)
                        dst = xpad[:, j, 3 + TP:].rearrange("p (b t) -> p b t", b=NSEQ)[:, :, 3:]
                        act.activation(dst, ps[:, PH:HALF].rearrange("p (b t) -> p b t", b=NSEQ), fn, bias=b).then_inc(fr, 1)
                    return
                if (g, j, half) == ("u", 0, 0):
                    for k in range(4):
                        act.wait_ge(kv_stored[k], 32)
                dst = {"u": ob[:, 0, j], "yg": ob[:, 1, j], "c": ob[:, 2, j], "go": ob[:, 3, j],
                       "q": q_all[:, j], "f": f_all[:, j]}[g]
                act.activation(dst[:, at:at + HALF], ps[:, 0:HALF], fn, bias=b).then_inc(fr, 1)

            def released(eng, name):
                b, n = uses[name]
                eng.wait_ge(free[b], n + 1)

            def kv_out(c):
                if c >= 4:
                    act.wait_ge(kv_stored[c % 4], 16)
                copy_out(f"kv{c}", kv_stage[:, c % 4], (0, 512))
                released(act, f"kv{c}")
                out = (o_mk, o_mv)[c // 4][0, 0].rearrange("(m p) h d -> p m (h d)", p=P)
                act.dma_start(out[:, :, 256 * (c % 4):256 * (c % 4) + 256], kv_stage[:, c % 4]).then_inc(kv_stored[c % 4], 16)

            for t in range(NT + 2):
                if t < NT:
                    deviation(t, TILES[t])
                if 1 <= t <= NT:
                    for s in range(2):
                        copy_out(f"xT{t - 1}{'ab'[s]}", xT[:, 4 * s:4 * s + 4, (t - 1) * P:(t - 1) * P + TILES[t - 1]],
                                 (0, 4 * TILES[t - 1]))
                if t >= 2:
                    z_out(("z", "i", t - 2, 0))
            for k in range(4):
                copy_out(f"memT{k}", memT[:, 2 * k:2 * k + 2, :], (0, 512))
            copy_out("par", pc[:, 0:PAR_N], (0, PAR_N))
            copy_out("pst", pst[:], (0, 480))
            ps, fr = arrived(act, "cst")
            for j in range(KW):
                dst = xpad[:, j, 3 + TP:].rearrange("p (b t) -> p b t", b=NSEQ)[:, :, 0:3]
                act.activation(dst, ps[:, 24 * j:24 * j + 24].rearrange("p (b t) -> p b t", b=NSEQ), ACT.Copy)
            act.activation(h0[:], ps[:, 96:128].rearrange("p (a b) -> p a b", a=KW), ACT.Copy).then_inc(fr, 1)
            copy_out("sgw", swT[:], (0, 512))
            copy_out("wbd", sbT[0:TS], (0, 256), TS)

            def hgrn(what, h):
                if what == "prep":
                    if h:
                        act.wait_ge(hg_done, h)
                    else:
                        act.wait_ge(x0_stored, 16 * NT)
                    f = f_all[:, h]
                    for half in range(2):
                        released(act, f"f{h}_{half}")
                    act.activation(tmp[:, 3], f, ACT.Sigmoid, scale=-1.0)
                    link(act.activation(tmp[:, 1], f, ACT.Abs))
                    link(act.activation(tmp[:, 1], tmp[:, 1], ACT.Exp, scale=-1.0))
                    act.activation(tmp[:, 4], tmp[:, 1], ACT.Ln, bias=small[:, 33:34]).then_inc(hg_ln, 1)
                elif what == "keys":
                    act.wait_ge(hg_b, h + 1)
                    act.activation(tmp[:, 1], tmp[:, 0], ACT.Exp).then_inc(hg_e, 1)
                    act.wait_ge(hg_d, h + 1)
                    act.activation(tmp[:, 4], tmp[:, 4], ACT.Exp).then_inc(hg_k, 1)
                    copy_out(f"kdT{h}", kdT[:, 0:4, :], (0, 512))
                    copy_out(f"kdS{h}", kdT[0:TS, 4, :], (0, P), TS)
                elif what.startswith("lev") and int(what[3:]) < len(LEVELS):
                    n = len(LEVELS) * h + int(what[3:])
                    act.wait_ge(hg_sub, n + 1)
                    size = T if LEVELS[int(what[3:])] <= 4 else TP
                    e = tmp[:, 1 if int(what[3:]) % 2 == 0 else 4, 0:size]
                    act.activation(e, e, ACT.Exp).then_inc(hg_exp, 1)
                elif what == "out":
                    for name, a, b in ((f"OP{h}", 0, TP), (f"OS{h}", TP, T)):
                        ps, fr = arrived(act, name)
                        act.activation(tmp[:, 1, a:b], ps[:, 0:b - a], ACT.Copy)
                        act.activation(tmp[:, 4, a:b], ps[:, 0:b - a], ACT.Square).then_inc(fr, 1)
                elif what == "norm":
                    for name, a, b in ((f"SP{h}", 0, TP), (f"SS{h}", TP, T)):
                        ps, fr = arrived(act, name)
                        act.activation(tmp[:, 4, a:b], ps[:, 0:b - a], ACT.Ln, bias=small[:, 32:33],
                                       scale=1.0 / P).then_inc(fr, 1)
                    released(act, f"SP{h}")
                    released(act, f"SS{h}")
                    act.activation(tmp[:, 4], tmp[:, 4], ACT.Exp, scale=-0.5).then_inc(hg_rs, 1)

            def lru(what, j):
                if what == "scan":
                    act.wait_ge(lr_m, j + 1)
                    act.activation(tmp[:, 1], tmp[:, 1], ACT.Sqrt).then_inc(lr_s, 1)
                if what != "sigmoids":
                    return
                if j:
                    act.wait_ge(st_cols, KW + j)
                if j == 0:
                    act.wait_ge(lr_c0, 1)
                    act.activation(small[:, 4:8], small[:, 0:4], ACT.Exp, scale=-1.0).then_inc(lr_y, 1)
                    act.wait_ge(lr_u, 1)
                    act.activation(small[:, 20:24], small[:, 8:12], ACT.Ln).then_inc(lr_l, 1)
                for name, row, dst in ((f"rp{j}", PAR_BR, 1), (f"ip{j}", PAR_BI, 2)):
                    ps, fr = arrived(act, name)
                    act.activation(tmp[:, dst, 0:TP], ps[:, :], ACT.Sigmoid, bias=pc[:, row + j:row + j + 1]).then_inc(fr, 1)
                ps, fr = arrived(act, f"rs{j}")
                act.activation(tmp[:, 1, TP:T], ps[:, 0:TS], ACT.Sigmoid, bias=pc[:, PAR_BR + j:PAR_BR + j + 1])
                act.activation(tmp[:, 2, TP:T], ps[:, TS:2 * TS], ACT.Sigmoid,
                               bias=pc[:, PAR_BI + j:PAR_BI + j + 1]).then_inc(fr, 1)
                for name in (f"rp{j}", f"ip{j}", f"rs{j}"):
                    released(act, name)
                act.wait_ge(lr_c0, 2)
                link(act.activation(tmp[:, 3], tmp[:, 1], ACT.Exp, scale=pc[:, 109 + j:110 + j]))
                act.activation(tmp[:, 1], tmp[:, 1], ACT.Tanh, scale=pc[:, 113 + j:114 + j]).then_inc(lr_a, 1)

            def merge_unit(wait, i, u):
                d, b = u // 2, u % 2
                wait(act, full[b], i * 8 + (merge_base[b] + u // 2 + 1))
                wait(act, free[2 + b], i * 8 + (merge_base[2 + b] + u // 2))
                col = i * (-8) + (PAR_BIN + GZ * KW + 8 * 3 + d)
                act.activation(gate[:, b, :], bank[b][:, 0:HALF], ACT.Sigmoid,
                               bias=pc[:, bass.ds(col, 1)]).then_inc(free[b], 1)

            for step in steps[NT:]:
                if step[0] == "z":
                    z_out(step)
                    if step == ("z", "v", NT - 1, 0):
                        for k in range(KD):
                            act.activation(x_hi[:, k, :], xT[:, k, :], ACT.Copy).then_inc(x_hi_done, 1)
                elif step[0] == "kv":
                    kv_out(step[1])
                elif step[0] == "hgrn":
                    hgrn(step[1], step[2])
                elif step[0] == "lru":
                    lru(step[1], step[2])
                elif step[0] == "merge":
                    if step == ("merge", 0, 0):
                        act.wait_ge(hg_done, KW)
                        act.wait_ge(rows_filled, 16)
                    merge_unit(plain_wait, step[1], step[2])
                elif step[:2] == ("sgu", "norm") and step[2] < NT:
                    deviation(n_ln, TILES[step[2]])
                    n_ln += 1
                elif step[0] == "states":
                    for k, (name, rows) in enumerate((("oc", 36), ("op", 120), ("oq", 15))):
                        copy_out(name, st_out[0:rows, k, :], (0, 512), rows)
                    act.dma_start(o_sgu[0].rearrange("b t c -> (b t) c"), v_tok[0:TS, 4, :]).then_inc(out_stored, 16)
                    for name in ("oc", "op", "oq"):
                        released(act, name)
                    outs = ((o_conv_p[0, 0], st_out[0:3, 0, :]), (o_conv_s[0].rearrange("b t c -> (b t) c"), st_out[3:27, 0, :]),
                            (o_h_p[0], st_out[27:28, 0, :]), (o_h_s[0], st_out[28:36, 0, :]),
                            (o_pool_s[0].rearrange("b t c -> (b t) c"), st_out[0:120, 1, :]), (o_pool_p[0, 0], st_out[0:15, 2, :]))
                    for dst, src in outs:
                        act.dma_start(dst, src).then_inc(out_stored, 16)
                    act.wait_ge(sgu_done, KW)
                    for t in range(NT):
                        act.dma_start(x_tok[0:TILES[t], t, :], x0_d[P * t:P * t + TILES[t], :]).then_inc(ld_x, 16)
            with act.Fori(PEEL, 4) as i:
                for u in range(16):
                    merge_unit(loop_wait, i, u)

            def layer_out(n_ln, names, dst):
                for t in range(NT):
                    deviation(n_ln + t, TILES[t])
                for t in range(NT):
                    for s in range(2):
                        copy_out(f"{names}{t}{'ab'[s]}", dst[:, 4 * s:4 * s + 4, t * P:t * P + TILES[t]], (0, 4 * TILES[t]))

            layer_out(n_ln, "yT", xT)
            for c in range(4):
                for n in range(4):
                    copy_out(f"q{c}{n}", qT[:, 2 * c + n // 2, (n % 2) * HALF:(n % 2) * HALF + HALF], (0, HALF))

            def keys_turned(item):
                if item < ITEMS and attention_item(item)[3]:
                    for n in range(4):
                        copy_out(f"KT{item}_{n}", kv_t[attention_item(item)[2]][:, 2 * n:2 * n + 2, :], (0, 512))

            keys_turned(0)
            for item in range(ITEMS + 1):
                keys_turned(item + 1)
                if item:
                    rows = attention_item(item - 1)[0]
                    for s in range(2):
                        copy_out(f"PT{item - 1}{'ab'[s]}", pT[(item - 1) % 2][:, 4 * s:4 * s + 4, 0:rows], (0, 4 * rows))
                if item < ITEMS:
                    rows, _, kset, _ = attention_item(item)
                    p, m = prob[item % 2], smx[:, item % 2, :]
                    act.wait_ge(att_max, item + 1)
                    for s in range(2):
                        ps, fr = arrived(act, f"S{item}{'ab'[s]}")
                        for e in range(2):
                            h = 2 * s + e
                            ins = act.activation(p[0:rows, h, :], ps[0:rows, 256 * e:256 * e + 256], ACT.Exp,
                                                 bias=m[0:rows, h:h + 1], scale=XD ** -0.5, accum_out=m[0:rows, 4 + h:5 + h])
                        ins.then_inc(fr, 1)
            for s in range(2):
                copy_out(f"OT{'ab'[s]}", oT[:, 4 * s:4 * s + 4, TP:T], (0, 4 * TS))
            layer_out(n_ln + NT, "zT", xT)
            for t in range(NT):
                ps, fr = arrived(act, f"rt{t}")
                if t == 0:
                    act.wait_ge(rt_logit, 1)
                act.activation(rsc[0:TILES[t], 0, NE * t:NE * t + NE], ps[0:TILES[t], 0:NE], ACT.Sigmoid).then_inc(fr, 1)

            def turn_rows(n_expr, u):
                loop_wait(act, full[2], n_expr + (moe_base[2] + 1))
                act.activation(xgT[:, u, 0:4, :], bank[2][:, :].rearrange("p (a b) -> p a b", a=4), ACT.Copy).then_inc(free[2], 1)

            act.wait_ge(full[2], moe_base[2] + 1)
            act.activation(xgT[:, 0, 0:4, :], bank[2][:, :].rearrange("p (a b) -> p a b", a=4), ACT.Copy).then_inc(free[2], 1)
            act.sem_inc(ys_stored[0], 16)
            act.sem_inc(ys_stored[1], 16)
            used = tiles_used(act)
            with act.Fori(0, MOE_T // 2) as i:
                for u in range(2):
                    with act.If(i * 2 + u < used):
                        n = i * 2 + u
                        loop_wait(act, full[0], i * 2 + (moe_base[0] + u + 1))
                        act.activation(hs[:, u, :], bank[0][:, :], ACT.Silu).then_inc(free[0], 1)
                        turn_rows(i * 2 + (u + 1), 1 - u)
                        loop_wait(act, full[4], i * 2 + (moe_base[4] + u + 1))
                        act.activation(hT[:, u], bank[4][:, :].rearrange("p (a b) -> p a b", a=4), ACT.Copy).then_inc(free[4], 1)
                        loop_wait(act, full[5], i * 2 + (moe_base[5] + u + 1))
                        loop_wait(act, ys_stored[u], i * 16 + 16)
                        act.activation(y_out[:, u, 0:512], bank[5][:, :], ACT.Copy).then_inc(free[5], 1)
                        loop_wait(act, free[5], i * 2 + (moe_base[5] + u + 1))
                        loop_wait(act, free[6], i * 2 + (moe_base[6] + u + 1))
                        act.dma_start(ys_d[bass.ds(i * (2 * P) + u * P, P), :], y_out[:, u, :]).then_inc(ys_stored[u], 16)
                    with act.If(i * 2 + u >= used):
                        act.sem_inc(ys_stored[u], 16)
            for t in range(NT):
                n, rows = n_ln + 2 * NT + t, TILES[t]
                o = 16 * (n % 2)
                deviation(n, rows)
                x = x_tok[0:rows, t, :]
                act.wait_ge(last_mean, t + 1)
                act.activation(x, x, ACT.Identity, bias=small[0:rows, o + 11:o + 12],
                               scale=small[0:rows, o + 14:o + 15]).then_inc(last_normed, 1)

        @block.tensor
        def _(pe):
            ident = cst[:, C_ID:C_ID + P]

            def mm(out, lhsT, rhs, start, stop):
                return pe.matmul(out, lhsT, rhs, start=start, stop=stop)

            def released(name):
                b, n = uses[name]
                pe.wait_ge(free[b], n + 1)

            def arrived_chunk(name):
                slot, value = chunk[name]
                pe.wait_ge(landed[slot], value)
                return slot

            pe.wait_ge(ld_cst, 16)
            def turn_tokens(name, source, t, ready, value):
                pe.wait_ge(ready, value)
                rows = TILES[t]
                for s in range(2):
                    ps, fu = acquire(pe, f"{name}{t}{'ab'[s]}")
                    for e in range(4):
                        c = 4 * s + e
                        m = pe.transpose(ps[:, rows * e:rows * e + rows], source[0:rows, t, P * c:P * c + P],
                                         ident[0:rows, 0:rows])
                    m.then_inc(fu, 1)

            def z_mm(step):
                _, g, j, half = step
                ps, fu = acquire(pe, step_units(step)[0])
                if g in ("i", "v"):
                    rows = TILES[j]
                    for c in range(2):
                        slot = arrived_chunk(f"{g}{c}")
                        for k in range(KD):
                            m = mm(ps[0:rows, 256 * c:256 * c + 256], xT[:, k, P * j:P * j + rows],
                                   slot_k8(slot)[:, k, :], k == 0, k == KD - 1)
                    m.then_inc(fu, 1)
                    return
                slot = arrived_chunk(step_chunks(step)[0])
                at = P * (j % 2) if g == "go" else {"q": 0, "f": P, "xb": 0, "c": P, "yg": 0, "u": P}[g]
                for k in range(KD):
                    m = mm(ps[:, 0:HALF], slot_k8(slot)[:, k, at:at + P], xT[:, k, half * HALF:half * HALF + HALF],
                           k == 0, k == KD - 1)
                m.then_inc(fu, 1)

            def kv_mm(c):
                slot = arrived_chunk(step_chunks(("kv", c))[0])
                ps, fu = acquire(pe, f"kv{c}")
                for m2 in range(2):
                    for k in range(KD):
                        m = mm(ps[:, 256 * m2:256 * m2 + 256], memT[:, k, P * m2:P * m2 + P], slot_k8(slot)[:, k, :],
                               k == 0, k == KD - 1)
                m.then_inc(fu, 1)

            for t in range(NT + 1):
                if t < NT:
                    turn_tokens("xT", x_tok, t, ln_out, t + 1)
                if t:
                    released(f"xT{t - 1}a")
                    released(f"xT{t - 1}b")
                    z_mm(("z", "i", t - 1, 0))
            pe.wait_ge(mem_landed, 16)
            for k in range(4):
                ps, fu = acquire(pe, f"memT{k}")
                for e in range(2):
                    for m2 in range(2):
                        c = 2 * k + e
                        m = pe.transpose(ps[:, 256 * e + P * m2:256 * e + P * m2 + P], mem_tok[:, m2, P * c:P * c + P], ident)
                m.then_inc(fu, 1)
            for k in range(4):
                released(f"memT{k}")
            pe.wait_ge(zeroed, 3)
            pe.wait_ge(ld_par, PAR_LOADS * 16)
            ps, fu = acquire(pe, "par")
            pe.transpose(ps[:, 0:PAR_N], par[0:PAR_N, :], ident[0:PAR_N, 0:PAR_N]).then_inc(fu, 1)
            pe.wait_ge(ld_raw, 16 * RAW_LOADS)
            ps, fu = acquire(pe, "pst")
            for j in range(KW):
                m = pe.transpose(ps[:, 120 * j:120 * j + 120], raw_pool[0:120, P * j:P * j + P], ident[0:120, 0:120])
            m.then_inc(fu, 1)
            ps, fu = acquire(pe, "cst")
            for j in range(KW):
                pe.transpose(ps[:, 24 * j:24 * j + 24], raw_conv[0:24, P * j:P * j + P], ident[0:24, 0:24])
            for j in range(KW):
                m = pe.transpose(ps[:, 96 + 8 * j:104 + 8 * j], raw_h[0:8, P * j:P * j + P], ident[0:8, 0:8])
            m.then_inc(fu, 1)
            ps, fu = acquire(pe, "sgw")
            for j in range(KW):
                m = pe.transpose(ps[:, P * j:P * j + P], raw_sw[:, j, :], ident)
            m.then_inc(fu, 1)
            ps, fu = acquire(pe, "wbd")
            for j in range(KW):
                m = pe.transpose(ps[0:TS, TS * j:TS * j + TS], raw_sb[0:TS, j, :], ident[0:TS, 0:TS])
            m.then_inc(fu, 1)

            def hgrn(what, h):
                hc = slice(P * h, P * h + P)
                if what == "keys":
                    pe.wait_ge(hg_kd, h + 1)
                    ps, fu = acquire(pe, f"kdT{h}")
                    for c in range(4):
                        m = pe.transpose(ps[:, P * c:P * c + P], tmp[:, 4, P * c:P * c + P], ident)
                    m.then_inc(fu, 1)
                    ps, fu = acquire(pe, f"kdS{h}")
                    pe.transpose(ps[0:TS, 0:P], tmp[:, 4, TP:T], ident).then_inc(fu, 1)
                elif what == "state":
                    released(f"kdT{h}")
                    released(f"kdS{h}")
                    if h == 0:
                        pe.wait_ge(biased, NT)
                    ps, fu = acquire(pe, f"U{h}")
                    for c in range(4):
                        m = mm(ps[:, P * c:P * c + P], kdT[:, c, :], i_tok[:, c, hc], True, True)
                    m.then_inc(fu, 1)
                    for s in range(2):
                        pe.wait_ge(hg_vm, 2 * h + s + 1)
                        ps, fu = acquire(pe, f"US{h}{'ab'[s]}")
                        rhs = vm[0:TS].rearrange("p a b -> p (a b)") if s == 0 else att_m[0:TS, 0:512]
                        mm(ps[:, :], kdT[0:TS, 4, :], rhs, True, True).then_inc(fu, 1)
                elif what == "diag":
                    pe.wait_ge(hg_ln, h + 1)
                    for half in range(2):
                        released(f"q{h}_{half}")
                    level(f"L{h}d", f"M{h}d", tmp[:, 3], q_all[:, h])
                elif what.startswith("lev"):
                    n = int(what[3:]) - 1
                    if 0 <= n < len(LEVELS):
                        pe.wait_ge(hg_x, len(LEVELS) * h + n + 1)
                        x = tmp[:, 2 if n % 2 == 0 else 5]
                        level(f"L{h}{n}", f"M{h}{n}" if LEVELS[n] <= 4 else None, x, x)
                elif what == "out":
                    pe.wait_ge(hg_att, h + 1)
                    released(f"U{h}")
                    qe = f_all[:, h]
                    ps, fu = acquire(pe, f"OP{h}")
                    for c in range(4):
                        o = ps[:, P * c:P * c + P]
                        m = mm(o, i_tok[:, c, hc], att[:, P * c:P * c + P], True, c == 0)
                        if c:
                            m = mm(o, s_pr[:, c - 1, :], qe[:, P * c:P * c + P], False, True)
                    m.then_inc(fu, 1)
                    pe.wait_ge(s0_landed, 16 * (h + 1))
                    ps, fu = acquire(pe, f"OS{h}")
                    mm(ps[:, 0:TS], i_tok[0:TS, 4, hc], att[0:TS, TP:T], True, False)
                    for b in range(NSEQ):
                        m = mm(ps[:, LSEQ * b:LSEQ * b + LSEQ], s_old[:, b, :], qe[:, TP + LSEQ * b:TP + LSEQ * b + LSEQ],
                               False, b == NSEQ - 1)
                    m.then_inc(fu, 1)
                elif what == "norm":
                    released(f"OP{h}")
                    released(f"OS{h}")
                    ones = cst[:, C_ONE:C_ONE + P]
                    ps, fu = acquire(pe, f"SP{h}")
                    mm(ps[:, :], ones, tmp[:, 4, 0:TP], True, True).then_inc(fu, 1)
                    ps, fu = acquire(pe, f"SS{h}")
                    mm(ps[:, 0:TS], ones, tmp[:, 4, TP:T], True, True).then_inc(fu, 1)

            def level(name, sname, left, right):
                ps, fu = acquire(pe, name)
                for c in range(4):
                    m = mm(ps[:, P * c:P * c + P], left[:, P * c:P * c + P], right[:, P * c:P * c + P], True, True)
                m.then_inc(fu, 1)
                if sname:
                    ps, fu = acquire(pe, sname)
                    mm(ps[0:TS, 0:TS], left[:, TP:T], right[:, TP:T], True, True).then_inc(fu, 1)

            def both(weights, x, names):
                ps, fu = acquire(pe, names[0])
                mm(ps[:, :], weights, x[:, 0:TP], True, True).then_inc(fu, 1)
                ps, fu = acquire(pe, names[1])
                mm(ps[:, 0:TS], weights, x[:, TP:T], True, True).then_inc(fu, 1)

            def merge_unit(wait, i, u):
                d, half = u // 2, u % 2
                wait(pe, g_lo_done, i * 8 + (d + 1))
                wait(pe, free[half], i * 8 + (merge_base[half] + u // 2))
                cols = slice(half * HALF, half * HALF + HALF)
                for k in range(KD):
                    pairs = ((g_hi, x_hi), (g_hi, x_lo), (g_lo, x_hi))
                    for n, (w, x) in enumerate(pairs):
                        m = mm(bank[half][:, 0:HALF], w[d % 2][:, k, :], x[:, k, cols], k == 0 and n == 0, k == KD - 1 and n == 2)
                m.then_inc(full[half], 1)
                wait(pe, p_landed[d % 2], i * 64 + 16 * (d // 2 + 1))
                wait(pe, free[2 + half], i * 8 + (merge_base[2 + half] + u // 2))
                for k in range(KW):
                    rhs = ob[:, bass.ds(3 - i, 1), k, half * HALF:half * HALF + HALF].rearrange("p a n -> p (a n)")
                    m = mm(bank[2 + half][:, 0:HALF], p_raw[d % 2][:, k, :], rhs, k == 0, k == KW - 1)
                m.then_inc(full[2 + half], 1)

            pe.wait_ge(ld_masks, 16)
            for step in steps[NT:]:
                if step[0] == "z":
                    z_mm(step)
                elif step[0] == "kv":
                    kv_mm(step[1])
                elif step[0] == "hgrn":
                    hgrn(step[1], step[2])
                elif step[0] == "merge":
                    if step[2] == 0:
                        if step[1] == 0:
                            pe.wait_ge(hg_done, KW)
                            pe.wait_ge(x_lo_done, KD)
                        else:
                            for j in range(KW):
                                released(f"pp{j}")
                                released(f"ps{j}")
                    merge_unit(plain_wait, step[1], step[2])
                elif step[0] != "states" and step[1] != "product":
                    pass
                elif step[0] == "pool":
                    j = step[2]
                    pe.wait_ge(ld_small, 16 * SMALL_LOADS)
                    pe.wait_ge(pl_d, j + 1)
                    both(wp[:, j, :], ob[:, 2, j], (f"pp{j}", f"ps{j}"))
                elif step[0] == "lru":
                    j = step[2]
                    pe.wait_ge(lr_xc, j + 1)
                    x = conv_out[j % 2]
                    ps, fu = acquire(pe, f"rp{j}")
                    mm(ps[:, :], wr[:, j, :], x[:, 0:TP], True, True).then_inc(fu, 1)
                    ps, fu = acquire(pe, f"ip{j}")
                    mm(ps[:, :], wi[:, j, :], x[:, 0:TP], True, True).then_inc(fu, 1)
                    ps, fu = acquire(pe, f"rs{j}")
                    mm(ps[:, 0:TS], wr[:, j, :], x[:, TP:T], True, True)
                    mm(ps[:, TS:2 * TS], wi[:, j, :], x[:, TP:T], True, True).then_inc(fu, 1)
                elif step[0] == "sgu":
                    j = step[2]
                    pe.wait_ge(v_normed, NT + 2)
                    ps, fu = acquire(pe, f"gp{j}")
                    for c in range(4):
                        m = mm(ps[:, P * c:P * c + P], v_tok[:, c, P * j:P * j + P], swT[:, j, :], True, True)
                    m.then_inc(fu, 1)
                    ps, fu = acquire(pe, f"gs{j}")
                    mm(ps[:, 0:TS], v_tok[0:TS, 4, P * j:P * j + P], sbT[0:TS, j, :], True, True).then_inc(fu, 1)
                elif step[0] == "states":
                    pe.wait_ge(st_cols, KW * 2)
                    for name, src, rows in (("oc", lambda j: att_m[:, 36 * j:36 * j + 36], 36),
                                            ("op", lambda j: att[:, 135 * j + 15:135 * j + 135], 120),
                                            ("oq", lambda j: att[:, 135 * j:135 * j + 15], 15)):
                        ps, fu = acquire(pe, name)
                        for j in range(KW):
                            m = pe.transpose(ps[0:rows, P * j:P * j + P], src(j), ident)
                        m.then_inc(fu, 1)
            pe.wait_ge(sgu_done, KW)
            with pe.Fori(PEEL, 4) as i:
                for u in range(16):
                    merge_unit(loop_wait, i, u)

            def token_major(name, x, w, t):
                rows = TILES[t]
                for s in range(2):
                    ps, fu = acquire(pe, f"{name}{t}{'ab'[s]}")
                    for c in range(2):
                        slot = arrived_chunk(f"{w}{2 * s + c}")
                        for k in range(KD):
                            m = mm(ps[0:rows, 256 * c:256 * c + 256], x[:, k, P * t:P * t + rows], slot_k8(slot)[:, k, :],
                                   k == 0, k == KD - 1)
                    m.then_inc(fu, 1)

            pe.wait_ge(mer_add, 3 * 16)
            for t in range(NT):
                token_major("mix", mer, "wo", t)
            for t in range(NT):
                turn_tokens("yT", x_tok, t, ln_out, NT + t + 1)
            for t in range(NT):
                released(f"yT{t}a")
                released(f"yT{t}b")
            for c in range(4):
                slot = arrived_chunk(f"wq{c}")
                for n in range(4):
                    ps, fu = acquire(pe, f"q{c}{n}")
                    for k in range(KD):
                        m = mm(ps[:, 0:HALF], slot_k8(slot)[:, k, P * (n // 2):P * (n // 2) + P],
                               xT[:, k, (n % 2) * HALF:(n % 2) * HALF + HALF], k == 0, k == KD - 1)
                    m.then_inc(fu, 1)
            k_use, v_use = [0, 0], [0, 0]

            def turn_keys(item):
                if item == ITEMS or not attention_item(item)[3]:
                    return
                kset = attention_item(item)[2]
                k_use[kset] += 1
                pe.wait_ge(k_landed[kset], 16 * k_use[kset])
                for n in range(4):
                    ps, fu = acquire(pe, f"KT{item}_{n}")
                    for e in range(2):
                        for m2 in range(2):
                            c = 2 * n + e
                            m = pe.transpose(ps[:, 256 * e + P * m2:256 * e + P * m2 + P],
                                             kv_k[kset][:, m2, P * c:P * c + P], ident)
                    m.then_inc(fu, 1)

            turn_keys(0)
            for item in range(ITEMS + 1):
                if item < ITEMS:
                    rows, at, kset, fresh = attention_item(item)
                    if fresh:
                        for n in range(4):
                            released(f"KT{item}_{n}")
                    if item == 0:
                        for c in range(4):
                            for n in range(4):
                                released(f"q{c}{n}")
                    for s in range(2):
                        ps, fu = acquire(pe, f"S{item}{'ab'[s]}")
                        for e in range(2):
                            for k in range(2):
                                c = 2 * (2 * s + e) + k
                                m = mm(ps[0:rows, 256 * e:256 * e + 256], qT[:, c, at:at + rows], kv_t[kset][:, c, :],
                                       k == 0, k == 1)
                        m.then_inc(fu, 1)
                    turn_keys(item + 1)
                if item:
                    it = item - 1
                    rows, at, kset, fresh = attention_item(it)
                    if fresh:
                        v_use[kset] += 1
                        pe.wait_ge(v_landed[kset], 16 * v_use[kset])
                    pe.wait_ge(att_prob, it + 1)
                    for s in range(2):
                        ps, fu = acquire(pe, f"PT{it}{'ab'[s]}")
                        for e in range(4):
                            h, m2 = 2 * s + e // 2, e % 2
                            m = pe.transpose(ps[:, rows * e:rows * e + rows], prob[it % 2][0:rows, h, P * m2:P * m2 + P],
                                             ident[0:rows, 0:rows])
                        m.then_inc(fu, 1)
                    released(f"PT{it}a")
                    released(f"PT{it}b")
                    for s in range(2):
                        ps, fu = acquire(pe, f"O{it}{'ab'[s]}")
                        if it >= TP // P:
                            for e in range(2):
                                h = 2 * s + e
                                for m2 in range(2):
                                    m = mm(ps[0:rows, XD * e:XD * e + XD], pT[it % 2][:, 2 * h + m2, 0:rows],
                                           kv_v[kset][:, m2, XD * h:XD * h + XD], m2 == 0, m2 == 1)
                            m.then_inc(fu, 1)
                            continue
                        for e in range(4):
                            c = 4 * s + e
                            for m2 in range(2):
                                m = mm(ps[:, rows * e:rows * e + rows], kv_v[kset][:, m2, P * c:P * c + P],
                                       pT[it % 2][:, 2 * (c // 2) + m2, 0:rows], m2 == 0, m2 == 1)
                        m.then_inc(fu, 1)
            for item in range(ITEMS):
                released(f"O{item}a")
                released(f"O{item}b")
            def turn_sample_outputs():
                for k in range(2):
                    pe.wait_ge(o_moved[k], 16 * NSEQ // 2)
                for s in range(2):
                    ps, fu = acquire(pe, f"OT{'ab'[s]}")
                    for e in range(4):
                        c = 4 * s + e
                        m = pe.transpose(ps[:, TS * e:TS * e + TS], o_all[0:TS, P * c:P * c + P], ident[0:TS, 0:TS])
                    m.then_inc(fu, 1)

            for t in range(NT):
                if t == NT - 1:
                    released("OTa")
                    released("OTb")
                token_major("att", oT, "wx", t)
                if t == 0:
                    turn_sample_outputs()
            for t in range(NT):
                turn_tokens("zT", x_tok, t, ln_out, 2 * NT + t + 1)
            pe.wait_ge(rt_landed, 16 * 3)
            for t in range(NT):
                released(f"zT{t}a")
                released(f"zT{t}b")
                ps, fu = acquire(pe, f"rt{t}")
                for k in range(KD):
                    m = mm(ps[0:TILES[t], 0:NE], xT[:, k, P * t:P * t + TILES[t]], rw[:, k, :], k == 0, k == KD - 1)
                m.then_inc(fu, 1)
            pe.wait_ge(rt_chosen, 1)
            chosen = rsc[:, 5, :]
            ps, fu = acquire(pe, "pos")
            for t in range(NT):
                for j in range(t + 1):
                    rows = TILES[j]
                    lhs = cst[0:rows, (C_STRI if j == t else C_ONE):(C_STRI if j == t else C_ONE) + TILES[t]]
                    m = mm(ps[0:TILES[t], NE * t:NE * t + NE], lhs, chosen[0:rows, NE * j:NE * j + NE], j == 0, j == t)
            m.then_inc(fu, 1)
            ps, fu = acquire(pe, "cnt")
            for j in range(NT):
                m = mm(ps[:, 0:NE], cst[0:TILES[j], C_ONE:C_ONE + P], chosen[0:TILES[j], NE * j:NE * j + NE],
                       j == 0, j == NT - 1)
            m.then_inc(fu, 1)
            pe.wait_ge(hot_ready, 1)
            ps, fu = acquire(pe, "tab")
            for j in range(2 * NT):
                rows = TILES[j % NT]
                m = mm(ps[:, 0:MOE_T], hot_row[0:rows, j, :], hot_col[0:rows, j, :], j == 0, j == 2 * NT - 1)
            m.then_inc(fu, 1)

            def turn_gathered(u):
                for s in range(2):
                    for e in range(4):
                        c = 4 * s + e
                        m = pe.transpose(bank[2 + s][:, P * e:P * e + P], xg[:, u, P * c:P * c + P], ident)
                    m.then_inc(full[2 + s], 1)

            pe.wait_ge(xg_landed[0], 16)
            pe.wait_ge(free[2], moe_base[2])
            pe.wait_ge(free[3], moe_base[3])
            turn_gathered(0)
            used = tiles_used(pe)
            with pe.Fori(0, MOE_T // 2) as i:
                for u in range(2):
                    with pe.If(i * 2 + u < used):
                        loop_wait(pe, free[2], i * 2 + (moe_base[2] + u + 1))
                        loop_wait(pe, free[3], i * 2 + (moe_base[3] + u + 1))
                        for g in range(2):
                            loop_wait(pe, free[g], i * 2 + (moe_base[g] + u))
                            for c in range(2):
                                k6 = 6 * u + 2 * g + c
                                loop_wait(pe, mlanded[k6], i * 16 + (moe_landed[k6] + 16))
                                w = mring[:, k6, :].rearrange("p (k n) -> p k n", k=KD)
                                for k in range(KD):
                                    m = mm(bank[g][:, 256 * c:256 * c + 256], xgT[:, u, k, :], w[:, k, :], k == 0, k == KD - 1)
                            m.then_inc(full[g], 1)
                        loop_wait(pe, xg_landed[1 - u], i * 16 + (16 + 16 * u))
                        turn_gathered(1 - u)
                        loop_wait(pe, free[1], i * 2 + (moe_base[1] + u + 1))
                        loop_wait(pe, free[4], i * 2 + (moe_base[4] + u))
                        for e in range(4):
                            m = pe.transpose(bank[4][:, P * e:P * e + P], hs[:, u, P * e:P * e + P], ident)
                        m.then_inc(full[4], 1)
                        loop_wait(pe, free[4], i * 2 + (moe_base[4] + u + 1))
                        for s in range(2):
                            k6 = 6 * u + 4 + s
                            loop_wait(pe, free[5 + s], i * 2 + (moe_base[5 + s] + u))
                            loop_wait(pe, mlanded[k6], i * 16 + (moe_landed[k6] + 16))
                            w = mring[:, k6, :].rearrange("p (k n) -> p k n", k=KW)
                            for k in range(KW):
                                m = mm(bank[5 + s][:, :], hT[:, u, k, :], w[:, k, :], k == 0, k == KW - 1)
                            m.then_inc(full[5 + s], 1)

        @block.vector
        def _(dve):
            seen = [0]

            def link(ins):
                seen[0] += 1
                ins.then_inc(dve_step, 1)
                dve.wait_ge(dve_step, seen[0])

            def released(name):
                b, n = uses[name]
                dve.wait_ge(free[b], n + 1)

            n_ln = [0]

            def norm_stats(x, rows):
                o = 16 * (n_ln[0] % 2)
                size = x.shape[-1]
                pieces = size // 512
                for k in range(pieces):
                    ins = dve.bn_stats(small[0:rows, o + 6 * k:o + 6 * k + 6], x[:, 512 * k:512 * k + 512])
                    link(ins)
                link(dve.bn_aggr(small[0:rows, o + 12:o + 14], small[0:rows, o:o + 6 * pieces]))
                dve.tensor_scalar(small[0:rows, o + 14:o + 15], small[0:rows, o + 13:o + 14], LN_EPS, None,
                                  ALU.add).then_inc(ln_var, 1)
                n_ln[0] += 1

            def norm_apply(n, x, g, b, rows, done):
                o = 16 * (n % 2)
                dve.wait_ge(ln_std, n + 1)
                link(dve.reciprocal(small[0:rows, o + 14:o + 15], small[0:rows, o + 15:o + 16]))
                link(dve.tensor_scalar(x, x, small[0:rows, o + 12:o + 13], small[0:rows, o + 14:o + 15],
                                       ALU.subtract, ALU.mult))
                link(dve.tensor_tensor(x, x, g[0:rows], ALU.mult))
                dve.tensor_tensor(x, x, b[0:rows], ALU.add).then_inc(done, 1)

            def norm_tiles(get, g, b, done, before=None, rows_ready=None):
                first = n_ln[0]
                for t in range(NT + 1):
                    if t < NT:
                        if before:
                            before(t)
                        norm_stats(get(t), TILES[t])
                    if t == 1 and rows_ready:
                        rows_ready()
                    if t:
                        norm_apply(first + t - 1, get(t - 1), g, b, TILES[t - 1], done)

            norm_tiles(lambda t: x_tok[0:TILES[t], t, :], lng, lnb, ln_out, lambda t: dve.wait_ge(x_in[t], 16),
                       lambda: dve.wait_ge(ld_rows, 32))
            dve.wait_ge(ld_masks, 16)

            def cview(col, rows, shape):
                return cst[0:rows, col:col + shape[1]].unsqueeze(1).to_broadcast([rows, shape[0], shape[1]])

            def hgrn(what, h):
                b, e1, x2, kk, e4, x5 = (tmp[:, n] for n in range(6))
                q, qe, f = q_all[:, h], f_all[:, h], f_all[:, h]
                bs = b[:, TP:T].rearrange("p (a c) -> p a c", c=LSEQ)
                bp = b[:, 0:TP].rearrange("p (a c) -> p a c", c=P)
                if what == "prep":
                    dve.wait_ge(hg_ln, h + 1)
                    link(dve.scalar_tensor_tensor(x2, f, 0.0, e4, ALU.min, ALU.subtract))
                    dve.tensor_tensor_scan(b, cst[:, C_RH:C_RH + T], x2, 0.0, ALU.mult, ALU.add).then_inc(hg_b, 1)
                    dve.wait_ge(hg_b, h + 1)
                elif what == "keys":
                    dve.tensor_tensor(e4[:, 0:TP].rearrange("p (a c) -> p a c", c=P),
                                      bp[:, :, P - 1:P].to_broadcast([P, 4, P]), bp, ALU.subtract)
                    dve.tensor_tensor(e4[:, TP:T].rearrange("p (a c) -> p a c", c=LSEQ),
                                      bs[:, :, LSEQ - 1:LSEQ].to_broadcast([P, NSEQ, LSEQ]), bs,
                                      ALU.subtract).then_inc(hg_d, 1)
                    dve.wait_ge(hg_e, h + 1)
                    for half in range(2):
                        released(f"q{h}_{half}")
                    dve.tensor_tensor(qe, q, e1, ALU.mult)
                    dve.tensor_copy(small[:, 16:20], e1[:, P - 1:TP:P])
                    link(dve.tensor_copy(small[:, 20:28], e1[:, TP + LSEQ - 1:T:LSEQ]))
                    dve.wait_ge(hg_k, h + 1)
                    dve.tensor_tensor(e4, kk, e4, ALU.mult).then_inc(hg_kd, 1)
                elif what == "state":
                    if h == 0:
                        dve.wait_ge(biased, NT)
                    vals = i_tok[0:TS, 4, P * h:P * h + P].unsqueeze(1).to_broadcast([TS, 4, P])
                    for s in range(2):
                        out = vm[0:TS] if s == 0 else att_m[0:TS, 0:512].rearrange("p (a c) -> p a c", c=P)
                        if s == 0 and h:
                            b0, n0 = uses[f"US{h - 1}b"]
                            dve.wait_ge(full[b0], n0 + 1)
                        mask = cst[0:TS, C_BLK + 4 * s:C_BLK + 4 * s + 4].unsqueeze(2).to_broadcast([TS, 4, P])
                        dve.tensor_tensor(out, vals, mask, ALU.mult).then_inc(hg_vm, 1)
                    ps, fr = arrived(dve, f"U{h}")
                    if h:
                        dve.wait_ge(hg_stored, 32 * h)
                    link(dve.tensor_copy(s_pr[:, 0, :], ps[:, 0:P]))
                    for c in range(1, 4):
                        ins = dve.scalar_tensor_tensor(s_pr[:, c, :], s_pr[:, c - 1, :], small[:, 16 + c:17 + c],
                                                       ps[:, P * c:P * c + P], ALU.mult, ALU.add)
                        if c < 3:
                            link(ins)
                    ins.then_inc(fr, 1)
                    dve.wait_ge(s0_landed, 16 * (h + 1))
                    link(dve.tensor_tensor(s_new[:], s_old[:], small[:, 20:28].unsqueeze(2).to_broadcast([P, NSEQ, P]),
                                           ALU.mult))
                    for s in range(2):
                        ps, fr = arrived(dve, f"US{h}{'ab'[s]}")
                        v = s_new[:, 4 * s:4 * s + 4, :]
                        dve.tensor_tensor(v, v, ps[:, :].rearrange("p (a c) -> p a c", c=P), ALU.add).then_inc(fr, 1)
                elif what == "diag":
                    for name, out, shape, rows in ((f"L{h}d", att[:, 0:TP], (4, P), P), (f"M{h}d", att[0:TS, TP:T], (1, TS), TS)):
                        ps, fr = arrived(dve, name)
                        o = out.rearrange("p (a c) -> p a c", c=shape[1])
                        dve.tensor_tensor(o, ps[0:rows, 0:shape[0] * shape[1]].rearrange("p (a c) -> p a c", c=shape[1]),
                                          cview(C_ID, rows, shape), ALU.mult).then_inc(fr, 1)
                        released(name)
                elif what.startswith("lev"):
                    n = int(what[3:])
                    if n < len(LEVELS):
                        step, size = LEVELS[n], (T if LEVELS[n] <= 4 else TP)
                        src = b[:, 0:size].rearrange("p (a u c) -> p a u c", u=2, c=step)
                        dst = (e1 if n % 2 == 0 else e4)[:, 0:size].rearrange("p (a u c) -> p a u c", u=2, c=step)
                        ref = src[:, :, 0, step - 1:step].to_broadcast([P, size // step // 2, step])
                        if n == 1:
                            for k in ("kdT", "kdS"):
                                b1, n1 = uses[f"{k}{h}"]
                                dve.wait_ge(full[b1], n1 + 1)
                        if n >= 2:
                            dve.wait_ge(hg_x, len(LEVELS) * h + n - 1)
                        dve.tensor_tensor(dst[:, :, 1, :], src[:, :, 1, :], ref, ALU.subtract)
                        dve.tensor_tensor(dst[:, :, 0, :], ref, src[:, :, 0, :], ALU.subtract).then_inc(hg_sub, 1)
                    if 1 <= n <= len(LEVELS):
                        l = n - 1
                        step, size = LEVELS[l], (T if LEVELS[l] <= 4 else TP)
                        dve.wait_ge(hg_exp, len(LEVELS) * h + l + 1)
                        if l >= 2:
                            b1, n1 = uses[f"M{h}{l - 2}" if LEVELS[l - 2] <= 4 else f"L{h}{l - 2}"]
                            dve.wait_ge(full[b1], n1 + 1)

                        def cut(t, side):
                            return t[:, 0:size].rearrange("p (a u c) -> p a u c", u=2, c=step)[:, :, side, :]

                        e, x = (e1, e4)[l % 2], (x2, x5)[l % 2]
                        dve.tensor_tensor(cut(x, 1), cut(q, 1), cut(e, 1), ALU.mult)
                        dve.tensor_tensor(cut(x, 0), cut(kk, 0), cut(e, 0), ALU.mult).then_inc(hg_x, 1)
                    if n >= 2:
                        l = n - 2
                        parts = [(f"L{h}{l}", 0, TP, (4, P), P)]
                        if LEVELS[l] <= 4:
                            parts.append((f"M{h}{l}", TP, T, (1, TS), TS))
                        for name, a, z, shape, rows in parts:
                            ps, fr = arrived(dve, name)
                            o = att_m[0:rows, a:z]
                            dve.tensor_tensor(o.rearrange("p (a c) -> p a c", c=shape[1]),
                                              ps[0:rows, 0:z - a].rearrange("p (a c) -> p a c", c=shape[1]),
                                              cview(C_MASK + P * l, rows, shape), ALU.mult).then_inc(fr, 1)
                            released(name)
                            s = att[0:rows, a:z]
                            ins = dve.tensor_tensor(s, s, o, ALU.add)
                            if l == len(LEVELS) - 1 and a:
                                ins.then_inc(hg_att, 1)
                            else:
                                link(ins)
                elif what == "norm":
                    dve.wait_ge(hg_rs, h + 1)
                    for half in range(2):
                        released(f"go{h}_{half}")
                    link(dve.scalar_tensor_tensor(e1, e1, pc[:, PAR_NG:PAR_NG + 1], e4, ALU.mult, ALU.mult))
                    o = ob[:, 3, h, :]
                    dve.tensor_tensor(o, o, e1, ALU.mult).then_inc(hg_done, 1)

            LP, LS = POOL_BUF + TP, POOL_BUF + LSEQ

            def pool(what, j):
                c = cpad[:, j % 2, :]
                o = ob[:, 2, j]
                if what == "out":
                    for name, a, z in ((f"pp{j}", 0, TP), (f"ps{j}", TP, T)):
                        ps, fr = arrived(dve, name)
                        dve.tensor_scalar(o[:, a:z], ps[:, 0:z - a], pc[:, PAR_PB + j:PAR_PB + j + 1],
                                          pc[:, PAR_PS + j:PAR_PS + j + 1], ALU.add, ALU.mult).then_inc(fr, 1)
                if what != "window":
                    return
                dve.wait_ge(pl_pad, j + 1)
                src = c
                for n in range(j + 1):
                    h = 1 << n
                    lo = 2 * h - 1
                    dst = csum[:, n % 2, :]
                    link(dve.tensor_tensor(dst[:, lo:], src[:, lo:], src[:, lo - h:LP + NSEQ * LS - h], ALU.add))
                    src = dst

                def prompt(t):
                    return t[:, POOL_BUF:LP]

                def samples(t):
                    return t[:, LP:].rearrange("p (b t) -> p b t", b=NSEQ)[:, :, POOL_BUF:]

                w = 1.0 / WINDOWS[j]
                link(dve.scalar_tensor_tensor(o[:, 0:TP], prompt(src), w, prompt(c), ALU.mult, ALU.subtract))
                dve.scalar_tensor_tensor(o[:, TP:T].rearrange("p (b t) -> p b t", b=NSEQ), samples(src), w, samples(c),
                                         ALU.mult, ALU.subtract)
                link(dve.tensor_tensor(small[:, 0:16], src[:, POOL_BUF:POOL_BUF + 16],
                                       cst[:, C_RC + 16 * j:C_RC + 16 * j + 16], ALU.mult))
                link(dve.tensor_tensor(o[:, 0:16], small[:, 0:16], c[:, POOL_BUF:POOL_BUF + 16], ALU.subtract))
                dve.tensor_copy(att[:, 135 * j:135 * j + 15], c[:, LP - 15:LP]).then_inc(st_cols, 1)
                dve.tensor_copy(att[:, 135 * j + 15:135 * j + 135].rearrange("p (b t) -> p b t", b=NSEQ),
                                c[:, LP:].rearrange("p (b t) -> p b t", b=NSEQ)[:, :, LSEQ:]).then_inc(pl_d, 1)

            def lru_conv(j):
                x = conv_out[j % 2]
                if j == 0:
                    lam = pc[:, PAR_LAM:PAR_LAM + 4]
                    link(dve.tensor_scalar(small[:, 28:32], lam, -1.0, None, ALU.mult))
                    dve.tensor_tensor(small[:, 0:4], small[:, 28:32], lam, ALU.max).then_inc(lr_c0, 1)
                    dve.wait_ge(lr_y, 1)
                    dve.tensor_scalar(small[:, 8:12], small[:, 4:8], 1.0, None, ALU.add).then_inc(lr_u, 1)
                    dve.wait_ge(lr_u, 1)
                    link(dve.tensor_scalar(small[:, 12:16], small[:, 8:12], -1.0, None, ALU.add))
                    link(dve.tensor_scalar(small[:, 16:20], small[:, 12:16], 0.0, None, ALU.is_equal))
                    link(dve.tensor_tensor(small[:, 12:16], small[:, 12:16], small[:, 16:20], ALU.add))
                    link(dve.reciprocal(small[:, 12:16], small[:, 12:16]))
                    dve.wait_ge(lr_l, 1)
                    link(dve.tensor_tensor(small[:, 20:24], small[:, 20:24], small[:, 16:20], ALU.add))
                    link(dve.tensor_tensor(small[:, 20:24], small[:, 20:24], small[:, 4:8], ALU.mult))
                    link(dve.tensor_tensor(small[:, 20:24], small[:, 20:24], small[:, 12:16], ALU.mult))
                    link(dve.scalar_tensor_tensor(small[:, 20:24], small[:, 28:32], 0.0, small[:, 20:24], ALU.max, ALU.add))
                    dve.tensor_scalar(pc[:, 109:113], small[:, 20:24], -LRU_C, None, ALU.mult)
                    dve.tensor_scalar(pc[:, 113:117], small[:, 20:24], LRU_C, None, ALU.mult).then_inc(lr_c0, 1)
                xs = xpad[:, j, 3 + TP:].rearrange("p (b t) -> p b t", b=NSEQ)
                for half in range(2):
                    released(f"xb{j}_{half}")
                released("cst")
                dve.wait_ge(zeroed, 4)
                dve.wait_ge(pl_d, KW)
                xo = x[:, TP:T].rearrange("p (b t) -> p b t", b=NSEQ)

                def cw(k):
                    return pc[:, PAR_CW + KW * k + j:PAR_CW + KW * k + j + 1]

                cb = pc[:, PAR_CB + j:PAR_CB + j + 1]
                dve.tensor_scalar(x[:, 0:TP], xpad[:, j, 0:TP], cw(0), cb, ALU.mult, ALU.add)
                link(dve.tensor_scalar(xo, xs[:, :, 0:LSEQ], cw(0), cb, ALU.mult, ALU.add))
                for k in range(1, CONV_W):
                    dve.scalar_tensor_tensor(x[:, 0:TP], xpad[:, j, k:k + TP], cw(k), x[:, 0:TP], ALU.mult, ALU.add)
                    ins = dve.scalar_tensor_tensor(xo, xs[:, :, k:k + LSEQ], cw(k), xo, ALU.mult, ALU.add)
                    if k < CONV_W - 1:
                        link(ins)
                ins.then_inc(lr_xc, 1)
                dve.tensor_copy(att_m[:, 36 * j:36 * j + 3], xpad[:, j, TP:TP + 3])
                dve.tensor_copy(att_m[:, 36 * j + 3:36 * j + 27].rearrange("p (b t) -> p b t", b=NSEQ),
                                xs[:, :, LSEQ:LSEQ + 3])

            def lru_gate(j):
                r, g, a, u, hh = (tmp[:, n] for n in range(1, 6))
                dve.wait_ge(lr_xc, j + 1)
                dve.wait_ge(lr_a, j + 1)
                link(dve.tensor_tensor(g, g, conv_out[j % 2], ALU.mult))
                link(dve.tensor_scalar(u, r, 1.0, None, ALU.add))
                link(dve.reciprocal(u, u))
                dve.scalar_tensor_tensor(r, r, 2.0, u, ALU.mult, ALU.mult).then_inc(lr_m, 1)

            def lru_scan(j):
                r, g, a, u, hh = (tmp[:, n] for n in range(1, 6))
                dve.wait_ge(lr_s, j + 1)
                link(dve.tensor_tensor(g, g, r, ALU.mult))
                link(dve.tensor_tensor(small[:, 0:8], a[:, TP:T:LSEQ], h0[:, j, :], ALU.mult))
                dve.tensor_tensor(g[:, TP:T:LSEQ], g[:, TP:T:LSEQ], small[:, 0:8], ALU.add)
                link(dve.tensor_tensor(a, a, cst[:, C_RL:C_RL + T], ALU.mult))
                link(dve.tensor_tensor_scan(hh, a, g, 0.0, ALU.mult, ALU.add))
                dve.tensor_copy(att_m[:, 36 * j + 27:36 * j + 28], hh[:, TP - 1:TP])
                dve.tensor_copy(att_m[:, 36 * j + 28:36 * j + 36], hh[:, TP + LSEQ - 1:T:LSEQ]).then_inc(st_cols, 1)
                for half in range(2):
                    released(f"yg{j}_{half}")
                o = ob[:, 1, j]
                link(dve.tensor_tensor(o, o, hh, ALU.mult))

            v_first = [0]

            def sgu(what, j):
                if what == "norm":
                    if j == 0:
                        dve.wait_ge(biased, 2 * NT)
                        dve.wait_ge(ld_rows, 32 + 48)
                        v_first[0] = n_ln[0]
                    if j < NT:
                        norm_stats(v_tok[0:TILES[j], j, :], TILES[j])
                    if j:
                        norm_apply(v_first[0] + j - 1, v_tok[0:TILES[j - 1], j - 1, :], sg_g, sg_b, TILES[j - 1], v_normed)
                    if j == NT:
                        released("sgw")
                        released("wbd")
                        dve.tensor_tensor(swT[:], swT[:], cview(C_TRI, P, (KW, P)), ALU.mult).then_inc(v_normed, 1)
                        dve.tensor_tensor(sbT[0:TS], sbT[0:TS], cview(C_TRI, TS, (KW, TS)), ALU.mult).then_inc(v_normed, 1)
                if what != "out":
                    return
                t0 = tmp[:, 0]
                row = sgu_rows[:, P * j:P * j + P]
                ps, fr = arrived(dve, f"gp{j}")
                dve.tensor_tensor(t0[:, 0:TP].rearrange("p (a c) -> p a c", c=P),
                                  ps[:, :].rearrange("p (a c) -> p a c", c=P),
                                  row.unsqueeze(1).to_broadcast([P, 4, P]), ALU.add).then_inc(fr, 1)
                ps, fr = arrived(dve, f"gs{j}")
                dve.tensor_tensor(t0[:, TP:T].rearrange("p (a c) -> p a c", c=LSEQ),
                                  ps[:, 0:TS].rearrange("p (a c) -> p a c", c=LSEQ),
                                  row[:, 0:LSEQ].unsqueeze(1).to_broadcast([P, NSEQ, LSEQ]), ALU.add).then_inc(fr, 1)
                released(f"gp{j}")
                released(f"gs{j}")
                for half in range(2):
                    released(f"u{j}_{half}")
                dve.tensor_tensor(ob[:, 0, j], ob[:, 0, j], t0, ALU.mult).then_inc(sgu_done, 1)
                dve.wait_ge(sgu_done, j + 1)

            def merge_unit(wait, i, u, first=False, second=False):
                d, half = u // 2, u % 2
                nb = 2 + half
                wait(dve, full[nb], i * 8 + (merge_base[nb] + u // 2 + 1))
                wait(dve, free[half], i * 8 + (merge_base[half] + u // 2 + 1))
                o = mer[:, d, half * HALF:half * HALF + HALF]
                if first:
                    dve.tensor_tensor(o, gate[:, half, :], bank[nb][:, 0:HALF], ALU.mult).then_inc(free[nb], 1)
                    wait(dve, free[nb], i * 8 + (merge_base[nb] + u // 2 + 1))
                    return
                if not (second and u == 0):
                    wait(dve, mer_add, (i - 1) * 16 + u)
                dve.tensor_tensor(prod[:, half, :], gate[:, half, :], bank[nb][:, 0:HALF], ALU.mult).then_inc(free[nb], 1)
                wait(dve, free[nb], i * 8 + (merge_base[nb] + u // 2 + 1))
                dve.tensor_tensor(o, o, prod[:, half, :], ALU.add).then_inc(mer_add, 1)

            for step in steps:
                if step[0] == "hgrn":
                    hgrn(step[1], step[2])
                elif step == ("z", "v", NT - 1, 0):
                    for k in range(3, KD):
                        dve.wait_ge(x_hi_done, k + 1)
                        dve.tensor_tensor(x_lo[:, k, :], xT[:, k, :], x_hi[:, k, :].bitcast(F32), ALU.subtract).then_inc(x_lo_done, 1)
                elif step[0] == "pool":
                    pool(step[1], step[2])
                elif step[0] == "merge":
                    if step == ("merge", 0, 0):
                        dve.wait_ge(hg_done, KW)
                    merge_unit(plain_wait, step[1], step[2], step[1] == 0, step[1] == 1)
                elif step[0] == "lru" and step[1] in ("conv", "gate", "scan"):
                    {"conv": lru_conv, "gate": lru_gate, "scan": lru_scan}[step[1]](step[2])
                elif step[0] == "sgu":
                    sgu(step[1], step[2])
            with dve.Fori(PEEL, 4) as i:
                for u in range(16):
                    merge_unit(loop_wait, i, u)

            def freed(name, ins):
                b, n = uses[name]
                ins.then_inc(free[b], 1)
                dve.wait_ge(free[b], n + 1)

            def residual(name, t):
                rows = TILES[t]
                for s in range(2):
                    ps, _ = arrived(dve, f"{name}{t}{'ab'[s]}")
                    x = x_tok[0:rows, t, 512 * s:512 * s + 512]
                    freed(f"{name}{t}{'ab'[s]}", dve.scalar_tensor_tensor(x, x, ALPHA, ps[0:rows, :], ALU.mult, ALU.add))

            def tile_of(t):
                return x_tok[0:TILES[t], t, :]

            dve.wait_ge(ld_x, 16 * NT)
            dve.wait_ge(ld_rows, 112)
            norm_tiles(tile_of, lng, lnb, ln_out, lambda t: residual("mix", t))
            for item in range(ITEMS + 1):
                if item < ITEMS:
                    rows = attention_item(item)[0]
                    m, p = smx[0:rows, item % 2, :], prob[item % 2][0:rows]
                    for s in range(2):
                        ps, _ = arrived(dve, f"S{item}{'ab'[s]}")
                        link(dve.tensor_reduce(m[:, 2 * s:2 * s + 2], ps[0:rows, :].rearrange("p (a c) -> p a c", a=2), AX, ALU.max))
                    dve.tensor_scalar(m[:, 0:4], m[:, 0:4], -XD ** -0.5, None, ALU.mult).then_inc(att_max, 1)
                if item:
                    r, at, _, _ = attention_item(item - 1)
                    for s in range(2):
                        name = f"O{item - 1}{'ab'[s]}"
                        ps, fr = arrived(dve, name)
                        if r == LSEQ:
                            if item - 1 >= TP // P + 2:
                                dve.wait_ge(o_moved[(item - 1) % 2], 16 * ((item - 1 - TP // P) // 2))
                            dve.tensor_copy(o_rows[0:r, (item - 1) % 2, 512 * s:512 * s + 512], ps[0:r, :]).then_inc(fr, 1)
                            continue
                        dve.tensor_copy(oT[:, 4 * s:4 * s + 4, at:at + r],
                                        ps[:, 0:4 * r].rearrange("p (a c) -> p a c", a=4)).then_inc(fr, 1)
                if item < ITEMS:
                    released(f"S{item}a")
                    released(f"S{item}b")
                    link(dve.reciprocal(m[:, 8:12], m[:, 4:8]))
                    dve.tensor_tensor(p, p, m[:, 8:12].unsqueeze(2).to_broadcast([rows, XH, NMEM]), ALU.mult).then_inc(att_prob, 1)
            released(f"PT{ITEMS - 1}a")
            released(f"PT{ITEMS - 1}b")
            dve.wait_ge(att_prob, ITEMS)
            dve.memset(rsc[:], 0.0).then_inc(rt_logit, 1)
            dve.wait_ge(ld_rows, 144)
            norm_tiles(tile_of, lng, lnb, ln_out, lambda t: residual("att", t))

            dve.wait_ge(rt_landed, 16 * 3)
            link(dve.tensor_tensor_scan(places[:], cst[:, C_ONE:C_ONE + P], cst[:, C_ONE:C_ONE + P], -float(P), ALU.mult, ALU.add))
            tile_row = c2[:, C2_TILE:C2_TILE + MOE_T * NE:NE]
            dve.tensor_scalar(tile_starts[:], tile_row, float(P), None, ALU.mult)
            dve.tensor_scalar(tile_numbers[:], tile_row, 1.0, None, ALU.add)
            dve.tensor_copy(tokens[:, 0:NT], c2[:, C2_TOK:C2_TOK + NT])
            link(dve.tensor_copy(tokens[:, NT:], c2[:, C2_TOK:C2_TOK + NT]))
            for t in range(NT):
                released(f"rt{t}")
            names = ("score", "select", "first", "second", "scratch", "chosen", "weight", "combine", "slot", "equal")
            arr = {n: rsc[:, k, :] for k, n in enumerate(names)}
            col = {n: cols[:, k, :] for k, n in enumerate(("m1", "m2", "group", "rest", "gmax", "gbest", "den", "wa", "wb"))}

            def by(a, size):
                return a.rearrange("p (a c) -> p a c", c=size)

            def first_max(v, mx, out, rest, n):
                link(dve.tensor_tensor(arr["equal"][:, 0:4 * n].rearrange("p (a c) -> p a c", c=4), v,
                                       mx.unsqueeze(2).to_broadcast([P, n, 4]), ALU.is_equal))
                eq = arr["equal"][:, 0:4 * n].rearrange("p (a c) -> p a c", c=4)
                dve.tensor_copy(out[:, :, 0], eq[:, :, 0])
                link(dve.tensor_scalar(rest, eq[:, :, 0], -1.0, 1.0, ALU.mult, ALU.add))
                for k in range(1, 4):
                    link(dve.tensor_tensor(out[:, :, k], eq[:, :, k], rest, ALU.mult))
                    if k < 3:
                        link(dve.tensor_tensor(rest, rest, out[:, :, k], ALU.subtract))

            sel, fst, snd = by(arr["select"], 4), by(arr["first"], 4), by(arr["second"], 4)
            link(dve.tensor_tensor(by(arr["select"], NE), by(arr["score"], NE), rbias[:].unsqueeze(1).to_broadcast([P, NT, NE]), ALU.add))
            link(dve.tensor_reduce(col["m1"], sel, AX, ALU.max))
            first_max(sel, col["m1"], fst, col["rest"], NT * NG)
            link(dve.scalar_tensor_tensor(arr["scratch"], arr["first"], -1e30, arr["select"], ALU.mult, ALU.add))
            link(dve.tensor_reduce(col["m2"], by(arr["scratch"], 4), AX, ALU.max))
            first_max(by(arr["scratch"], 4), col["m2"], snd, col["rest"], NT * NG)
            link(dve.tensor_tensor(col["group"], col["m1"], col["m2"], ALU.add))
            link(dve.tensor_reduce(col["gmax"][:, 0:NT], by(col["group"], NG), AX, ALU.max))
            first_max(by(col["group"], NG), col["gmax"][:, 0:NT], by(col["gbest"], NG), col["rest"][:, 0:NT], NT)
            link(dve.tensor_tensor(arr["chosen"], arr["first"], arr["second"], ALU.add))
            dve.tensor_tensor(by(arr["chosen"], EPG), by(arr["chosen"], EPG),
                              col["gbest"].unsqueeze(2).to_broadcast([P, NT * NG, EPG]), ALU.mult).then_inc(rt_chosen, 1)
            dve.wait_ge(rt_chosen, 1)
            ps, fr = arrived(dve, "cnt")
            cnt, tiles, ends, starts = (rsc[:, 10, NE * k:NE * k + NE] for k in range(4))
            link(dve.tensor_scalar(tiles, ps[:, 0:NE], 0.0, None, ALU.is_gt))
            for k in range(1, NT):
                ins = dve.scalar_tensor_tensor(tiles, ps[:, 0:NE], float(P * k), tiles, ALU.is_gt, ALU.add)
                if k < NT - 1:
                    link(ins)
            ins.then_inc(fr, 1)
            released("cnt")
            ones = cst[:, C_ONE:C_ONE + NE]
            link(dve.tensor_tensor_scan(ends, ones, tiles, 0.0, ALU.mult, ALU.add))
            link(dve.tensor_tensor(starts, ends, tiles, ALU.subtract))
            link(dve.tensor_scalar(starts, starts, float(P), 1.0, ALU.mult, ALU.add))
            grid = rsc[0:1, 11:17, :].rearrange("p a b -> p (a b)")[:, 0:MOE_T * NE].rearrange("p (a c) -> p a c", c=NE)
            link(dve.tensor_tensor(grid, c2[0:1, C2_TILE:C2_TILE + MOE_T * NE].rearrange("p (a c) -> p a c", c=NE),
                                   ends[0:1].unsqueeze(1).to_broadcast([1, MOE_T, NE]), ALU.is_ge))
            link(dve.tensor_reduce(eidf[0:1, :], grid, AX, ALU.add))
            link(dve.tensor_scalar(eidf[0:1, :], eidf[0:1, :], float(NE - 1), None, ALU.min))
            dve.tensor_copy(used_tiles[0:1, :], ends[0:1, NE - 1:NE])
            dve.tensor_copy(eid[0:1, :], eidf[0:1, :]).then_inc(rt_eid, 1)
            ps, fr = arrived(dve, "pos")
            slot = by(arr["slot"], NE)
            for a, z, rows in ((0, NT - 1, P), (NT - 1, NT, TS)):
                ins = dve.tensor_tensor(slot[0:rows, a:z], by(ps[0:rows, 0:NT * NE], NE)[:, a:z],
                                        starts[0:rows].unsqueeze(1).to_broadcast([rows, z - a, NE]), ALU.add)
                if a == 0:
                    link(ins)
            ins.then_inc(fr, 1)
            released("pos")
            link(dve.tensor_tensor(arr["slot"], arr["slot"], arr["chosen"], ALU.mult))
            link(dve.tensor_reduce(slots[:, 0:NT], slot, AX, ALU.max))
            link(dve.tensor_reduce(slots[:, NT:], slot, AX, ALU.add))
            link(dve.tensor_tensor(slots[:, NT:], slots[:, NT:], slots[:, 0:NT], ALU.subtract))
            per_slot = [P, 2 * NT, MOE_T]
            link(dve.tensor_tensor(hot_col[:], slots[:].unsqueeze(2).to_broadcast(per_slot),
                                   tile_starts[:].unsqueeze(1).to_broadcast(per_slot), ALU.is_gt))
            link(dve.tensor_reduce(slot_tiles[:], hot_col[:], AX, ALU.add))
            link(dve.tensor_tensor(hot_col[:], slot_tiles[:].unsqueeze(2).to_broadcast(per_slot),
                                   tile_numbers[:].unsqueeze(1).to_broadcast(per_slot), ALU.is_equal))
            link(dve.tensor_tensor(hot_col[:], hot_col[:], tokens[:].unsqueeze(2).to_broadcast(per_slot), ALU.mult))
            link(dve.scalar_tensor_tensor(slot_tiles[:], slot_tiles[:], -float(P), slots[:], ALU.mult, ALU.add))
            dve.tensor_tensor(hot_row[:], slot_tiles[:].unsqueeze(2).to_broadcast([P, 2 * NT, P]),
                              places[:].unsqueeze(1).to_broadcast([P, 2 * NT, P]), ALU.is_equal).then_inc(hot_ready, 1)
            ps, fr = arrived(dve, "tab")
            dve.tensor_copy(table[:, 0:MOE_T], ps[:, 0:MOE_T]).then_inc(fr, 1)
            link(dve.tensor_tensor(arr["weight"], arr["score"], arr["chosen"], ALU.mult))
            link(dve.tensor_reduce(col["den"][:, 0:NT], by(arr["weight"], NE), AX, ALU.add))
            link(dve.tensor_scalar(col["den"][:, 0:NT], col["den"][:, 0:NT], 1e-37, None, ALU.max))
            link(dve.reciprocal(col["den"][:, 0:NT], col["den"][:, 0:NT]))
            link(dve.tensor_tensor(by(arr["combine"], NE), by(arr["weight"], NE),
                                   col["den"][:, 0:NT].unsqueeze(2).to_broadcast([P, NT, NE]), ALU.mult))
            link(dve.tensor_tensor(by(arr["equal"], NE), slot, slots[:, 0:NT].unsqueeze(2).to_broadcast([P, NT, NE]), ALU.is_equal))
            link(dve.tensor_tensor(arr["scratch"], arr["equal"], arr["combine"], ALU.mult))
            link(dve.tensor_reduce(col["wa"][:, 0:NT], by(arr["scratch"], NE), AX, ALU.add))
            link(dve.tensor_tensor(arr["scratch"], arr["combine"], arr["scratch"], ALU.subtract))
            link(dve.tensor_reduce(col["wb"][:, 0:NT], by(arr["scratch"], NE), AX, ALU.add))
            link(dve.tensor_scalar(slots[:], slots[:], -1.0, None, ALU.add))
            dve.tensor_copy(ints[:, 0, 0:NT], slots[:, 0:NT])
            dve.tensor_copy(ints[:, 1, 0:NT], slots[:, NT:]).then_inc(rt_slots, 1)

            dve.wait_ge(x2_stored, 16 * NT)
            for t in range(NT):
                link(dve.tensor_scalar(tile_of(t), tile_of(t), ALPHA, None, ALU.mult))

            dve.wait_ge(full[3], moe_base[3] + 1)
            dve.tensor_copy(xgT[:, 0, 4:8, :], bank[3][:, :].rearrange("p (a b) -> p a b", a=4)).then_inc(free[3], 1)
            used = tiles_used(dve)
            with dve.Fori(0, MOE_T // 2) as i:
                for u in range(2):
                    with dve.If(i * 2 + u < used):
                        loop_wait(dve, full[1], i * 2 + (moe_base[1] + u + 1))
                        loop_wait(dve, free[0], i * 2 + (moe_base[0] + u + 1))
                        dve.tensor_tensor(hs[:, u, :], hs[:, u, :], bank[1][:, :], ALU.mult).then_inc(free[1], 1)
                        loop_wait(dve, full[3], i * 2 + (moe_base[3] + u + 2))
                        dve.tensor_copy(xgT[:, 1 - u, 4:8, :], bank[3][:, :].rearrange("p (a b) -> p a b", a=4)).then_inc(free[3], 1)
                        loop_wait(dve, full[6], i * 2 + (moe_base[6] + u + 1))
                        loop_wait(dve, ys_stored[u], i * 16 + 16)
                        dve.tensor_copy(y_out[:, u, 512:1024], bank[6][:, :]).then_inc(free[6], 1)
            dve.wait_ge(ld_rows, 176)
            first = n_ln[0]
            for t in range(NT + 2):
                if t >= 2:
                    dve.wait_ge(last_normed, t - 1)
                    x = tile_of(t - 2)
                    dve.tensor_tensor(x, x, lng[0:TILES[t - 2]], ALU.mult).then_inc(last_gain, 1)
                if t < NT:
                    rows, x = TILES[t], tile_of(t)
                    dve.wait_ge(yab_landed[t], 32)
                    for y, w in ((ya, "wa"), (yb, "wb")):
                        link(dve.scalar_tensor_tensor(x, y[0:rows, t, :], col[w][0:rows, t:t + 1], x, ALU.mult, ALU.add))
                    norm_stats(x, rows)
                if 1 <= t <= NT:
                    n, rows = first + t - 1, TILES[t - 1]
                    o = 16 * (n % 2)
                    dve.wait_ge(ln_std, n + 1)
                    link(dve.reciprocal(small[0:rows, o + 14:o + 15], small[0:rows, o + 15:o + 16]))
                    dve.scalar_tensor_tensor(small[0:rows, o + 11:o + 12], small[0:rows, o + 12:o + 13], -1.0,
                                             small[0:rows, o + 14:o + 15], ALU.mult, ALU.mult).then_inc(last_mean, 1)
            dve.wait_ge(last_gain, NT)
            x = tile_of(NT - 1)
            dve.tensor_tensor(x, x, lnb[0:TS], ALU.add).then_inc(last_written[1], 1)

        @block.gpsimd
        def _(pool):
            def rows_of(ap):
                return ap.unsqueeze(0).broadcast_to([P, ap.shape[0]])

            def load_rows(dst, src, s=None):
                pool.dma_start(dst, rows_of(src)).then_inc(s or ld_rows, 16)

            load_rows(lng[:], ln_in_g)
            load_rows(lnb[:], ln_in_b)
            pool.memset(raw_sb[0:TS], 0.0).then_inc(zeroed, 1)
            pool.memset(small[:, 32:33], RMS_EPS).then_inc(zeroed, 1)
            pool.memset(small[:, 33:34], 1.0).then_inc(zeroed, 1)
            pool.memset(xpad[:, :, 0:3], 0.0).then_inc(zeroed, 1)
            at = 0
            for src in (b_in_rows, conv_w[0].rearrange("k (c p) -> (k c) p", p=P),
                        *(v.rearrange("a (c p) -> (a c) p", p=P) for v in (conv_b, lru_br, lru_bi, lru_lam, pool_b, pool_s)),
                        norm_g):
                pool.dma_start(par[at:at + src.shape[0], :], src).then_inc(ld_par, 16)
                at += src.shape[0]
            assert at == PAR_N
            pool.dma_start(raw_pool[0:120, :], st_pool[0].rearrange("b t c -> (b t) c")).then_inc(ld_raw, 16)
            pool.dma_start(raw_conv[0:24, :], st_conv[0].rearrange("b t c -> (b t) c")).then_inc(ld_raw, 16)
            pool.dma_start(raw_h[0:8, :], st_h[0]).then_inc(ld_raw, 16)
            pool.dma_start(raw_sw[:], sgu_w[0].rearrange("g t s -> t g s")).then_inc(ld_raw, 16)
            pool.wait_ge(zeroed, 3)
            for b in range(NSEQ):
                pool.dma_start(raw_sb[LSEQ * b:LSEQ * b + LSEQ, :, LSEQ * b:LSEQ * b + LSEQ],
                               sgu_w[0, :, 0:LSEQ, 0:LSEQ].rearrange("g t s -> t g s")).then_inc(ld_raw, 16)
            pool.dma_start(wr[:], lru_wr[0].rearrange("h c d -> c h d")).then_inc(ld_small, 16)
            pool.dma_start(wi[:], lru_wi[0].rearrange("h c d -> c h d")).then_inc(ld_small, 16)
            pool.dma_start(wp[:], pool_w[0].rearrange("h c d -> c h d")).then_inc(ld_small, 16)
            load_rows(bias_i[:], b_in[0, GI * W:GI * W + W], ld_bias)
            load_rows(bias_v[:], b_in[0, GV * W:GV * W + W], ld_bias)
            for t in range(NT):
                pool.wait_ge(ln_out, t + 1)
                pool.dma_start(x0_d[P * t:P * t + TILES[t], :], x_tok[0:TILES[t], t, :]).then_inc(x0_stored, 16)
            def released(name):
                b, n = uses[name]
                pool.wait_ge(free[b], n + 1)

            def add_bias(buf, rows, name):
                pool.wait_ge(ld_bias, 32)
                for t in range(NT):
                    released(f"{name}{t}_0")
                    v = buf[0:TILES[t], t, :]
                    pool.tensor_tensor(v, v, rows[0:TILES[t]], ALU.add).then_inc(biased, 1)

            add_bias(i_tok, bias_i, "i")
            pool.wait_ge(biased, 2)
            spare = MOE_T - MOE_MIN
            pool.dma_start(ys_d[MOE_MIN * P:].rearrange("(t p) n -> p t n", p=P),
                           i_tok[:, 0:2, :].rearrange("p a b -> p (a b)").unsqueeze(1).to_broadcast([P, spare, D])).then_inc(rows_filled, 16)
            for h in range(KW):
                if h:
                    b, n = uses[f"OS{h - 1}"]
                    pool.wait_ge(full[b], n + 1)
                else:
                    pool.wait_ge(ln_out, NT)
                pool.dma_start(s_old[:], st_hg[0, :, h].rearrange("b k v -> k b v")).then_inc(s0_landed, 16)
                released(f"U{h}")
                pool.dma_start(o_hg_p[0, 0, h], s_pr[:, 3, :]).then_inc(hg_stored, 16)
                released(f"US{h}a")
                released(f"US{h}b")
                pool.dma_start(o_hg_s[0, :, h].rearrange("b k v -> k b v"), s_new[:]).then_inc(hg_stored, 16)
            for k in range(3):
                pool.wait_ge(x_hi_done, k + 1)
                pool.tensor_tensor(x_lo[:, k, :], xT[:, k, :], x_hi[:, k, :].bitcast(F32), ALU.subtract).then_inc(x_lo_done, 1)
            LP, LS = POOL_BUF + TP, POOL_BUF + LSEQ
            def pad(j):
                if j < 2:
                    pool.memset(cpad[:, j, 0:POOL_BUF], 0.0)
                else:
                    pool.wait_ge(pl_d, j - 1)
                for half in range(2):
                    released(f"c{j}_{half}")
                released("pst")
                c = cpad[:, j % 2]
                cs = c[:, LP:].rearrange("p (b t) -> p b t", b=NSEQ)
                pool.tensor_copy(c[:, POOL_BUF:LP], ob[:, 2, j, 0:TP])
                pool.tensor_copy(cs[:, :, 0:POOL_BUF], pst[:, j, :].rearrange("p (b t) -> p b t", b=NSEQ))
                pool.tensor_copy(cs[:, :, POOL_BUF:], ob[:, 2, j, TP:T].rearrange("p (b t) -> p b t", b=NSEQ)).then_inc(pl_pad, 1)

            def split_gate_weights(wait, i, u):
                if split_before(i, u):
                    j, d = split_before(i, u)
                    wait(pool, g_landed[d % 2], j * 64 + 16 * (d // 2 + 1))
                    pool.tensor_copy(g_hi[d % 2][:], g_raw[d % 2][:]).then_inc(g_hi_done, 1)
                    wait(pool, g_hi_done, j * 8 + (d + 1))
                    pool.tensor_tensor(g_lo[d % 2][:], g_raw[d % 2][:], g_hi[d % 2][:].bitcast(F32), ALU.subtract).then_inc(g_lo_done, 1)

            split_gate_weights(plain_wait, 0, 0)
            for step in steps:
                if step == ("pool", "window", 0):
                    pool.wait_ge(hg_done, KW)
                    pad(0)
                    pad(1)
                elif step[:2] == ("pool", "window") and step[2] + 1 < KW:
                    pad(step[2] + 1)
                elif step[0] == "merge" and step != ("merge", 0, 0):
                    split_gate_weights(plain_wait, step[1], step[2])
                elif step == ("lru", "conv", 0):
                    add_bias(v_tok, bias_v, "v")
                    pool.wait_ge(hg_stored, 32 * KW)
                    pool.wait_ge(biased, 2 * NT)
                    load_rows(sg_g[:], sgu_g[0])
                    load_rows(sg_b[:], sgu_b_ln[0])
                    load_rows(sgu_rows[:], sgu_b[0].rearrange("g t -> (g t)"))
            with pool.Fori(PEEL, 4) as i:
                for u in range(16):
                    split_gate_weights(loop_wait, i, u)
            pool.wait_ge(v_normed, NT + 2)
            load_rows(lng[:], ln_g[0, 0])
            load_rows(lnb[:], ln_b[0, 0])
            pool.dma_start(rw[:], rt_w.rearrange("(k p) e -> p k e", p=P)).then_inc(rt_landed, 16)
            for k in range(4):
                pool.wait_ge(kv_stored[k], 32)
            pool.wait_ge(mer_add, 3 * 16)
            pool.wait_ge(out_stored, 16 * 7)
            loads = [0] + list(range(4, ITEMS))

            def load_memory(n, values):
                item = loads[n]
                kset = attention_item(item)[2]
                if n >= 2:
                    before = loads[n - 2] if n > 2 else 3
                    b, use = uses[f"O{before}b" if values else f"KT{loads[n - 2]}_3"]
                    pool.wait_ge(full[b], use + 1)
                prompt, samples = ((o_mk, ck), (o_mv, cv))[values]
                src = prompt[0, 0] if item == 0 else samples[0, item - 4]
                dst, landed_kv = ((kv_k, k_landed), (kv_v, v_landed))[values]
                pool.dma_start(dst[kset][:], src.rearrange("(m p) h d -> p m (h d)", p=P)).then_inc(landed_kv[kset], 16)

            load_memory(0, 0)
            for n in range(len(loads)):
                if n + 1 < len(loads):
                    load_memory(n + 1, 0)
                load_memory(n, 1)
                if n == 1:
                    pool.wait_ge(ln_out, 2 * NT)
                    load_rows(lng[:], ln_g[0, 1])
                    load_rows(lnb[:], ln_b[0, 1])
            pool.wait_ge(rows_filled, 16)
            pool.wait_ge(rt_logit, 1)
            pool.dma_start(c2[:], cst2_in).then_inc(rt_landed, 16)
            pool.dma_start(rbias[:], rows_of(rt_b)).then_inc(rt_landed, 16)
            pool.memset(table[:, MOE_T:], 0).then_inc(table_rest, 1)
            for t in range(NT):
                pool.wait_ge(ln_out, 2 * NT + t + 1)
                pool.dma_start(x2_d[P * t:P * t + TILES[t], :], x_tok[0:TILES[t], t, :]).then_inc(x2_stored, 16)
            pool.wait_ge(ln_out, 3 * NT)
            load_rows(lng[:], ln_g[0, 2])
            load_rows(lnb[:], ln_b[0, 2])
            released("tab")
            pool.wait_ge(table_rest, 1)
            pool.wait_ge(x2_stored, 16 * NT)

            def gather(index, u):
                return pool.indirect_dma_start(xg[:, u, :], None, x2_d, bass.IndirectOffsetOnAxis(ap=index, axis=0))

            gather(table[:, 0:1], 0).then_inc(xg_landed[0], 16)
            used = tiles_used(pool)
            with pool.Fori(0, MOE_T // 2) as i:
                for u in range(2):
                    with pool.If(i * 2 + u < used):
                        loop_wait(pool, full[3], i * 2 + (moe_base[3] + u))
                        pool.tensor_copy(ints[:, 3 + u, 0:1], table[:, bass.ds(i * 2 + (u + 1), 1)]).then_inc(xg_idx, 1)
                        loop_wait(pool, xg_idx, i * 2 + (u + 1))
                        gather(ints[:, 3 + u, 0:1], 1 - u).then_inc(xg_landed[1 - u], 16)
            for u in range(2):
                pool.wait_ge(ys_stored[u], 16 + 16 * (MOE_T // 2))
            pool.wait_ge(rt_slots, 1)
            for t in range(NT):
                rows = TILES[t]
                for k, y in enumerate((ya, yb)):
                    pool.indirect_dma_start(y[0:rows, t, :], None, ys_d,
                                            bass.IndirectOffsetOnAxis(ap=ints[0:rows, k, t:t + 1], axis=0)).then_inc(yab_landed[t], 16)
            for t in range(NT - 1):
                x = x_tok[:, t, :]
                pool.wait_ge(last_gain, t + 1)
                pool.tensor_tensor(x, x, lnb[:], ALU.add).then_inc(last_written[0], 1)
            pool.wait_ge(out_stored, 16 * 7)
            pool.wait_ge(hg_stored, 32 * KW)


_INS = ["x_prompt", "x_sample", "mem_prompt", "cache_mem_k", "cache_mem_v", "state_conv", "state_rglru", "state_pool",
        "state_hgrn", "ln_in_g", "ln_in_b", "w_in", "b_in", "sgu_ln_g", "sgu_ln_b", "sgu_w", "sgu_b", "conv_w", "conv_b",
        "lru_wr", "lru_br", "lru_wi", "lru_bi", "lru_lambda", "pool_w", "pool_b", "pool_scale", "hgrn_norm_g",
        "w_branch", "w_out", "x_wq", "x_wk", "x_wv", "x_wo", "ln_g", "ln_b", "router_w", "router_b",
        "e_wg", "e_wu", "e_wd"]
_OUTS = [(1, TP, D), (NSEQ, LSEQ, D), (1, 1, NMEM, XH, XD), (1, 1, NMEM, XH, XD), (1, 1, CONV_W - 1, W), (1, 1, W),
         (1, 1, POOL_BUF, W), (1, 1, KW, P, P), (1, NSEQ, CONV_W - 1, W), (1, NSEQ, W), (1, NSEQ, POOL_BUF, W),
         (1, NSEQ, KW, P, P), (1, NSEQ, LSEQ, W)]


def kernel(**inputs):
    import numpy as _np
    import concourse.bacc as _bacc
    from concourse import mybir as _mybir
    from concourse.bass_utils import run_bass_kernel_spmd as _run

    nc = _bacc.Bacc("TRN2", target_bir_lowering=False, num_devices=1)
    arrays, args = {}, []
    named = [(name, _np.ascontiguousarray(inputs[name])) for name in _INS]
    named += list(zip(("shape_constants_a", "shape_constants_b"), shape_constants()))
    for name, a in named:
        arrays[f"in_{name}_dram"] = a
        args.append(nc.dram_tensor(f"in_{name}_dram", a.shape, _mybir.dt.from_np(a.dtype), kind="ExternalInput").ap())
    for i, shape in enumerate(_OUTS):
        args.append(nc.dram_tensor(f"out_{i}_dram", shape, _mybir.dt.float32, kind="ExternalOutput").ap())
    trunk(nc, *args)
    r = _run(nc, [arrays], core_ids=[0])
    return tuple(r.results[0][f"out_{i}_dram"] for i in range(len(_OUTS)))
```
